# Optimizing a Trainium2 kernel written in Bass

```python
import math
import jax
import jax.numpy as jnp
from jax import lax
import numpy as np

D_MODEL = 1024
BATCH = 1
SEQ = 128
DEPTH = 2
DEC_BATCH = 1
DEC_SEQ = 1024
PAST_LEN = 128

GRID_W = 64
CHUNK = 64
EPS = 1e-6
HEAD_DIM = 64
D_MIX = D_MODEL
HG_W = D_MIX // 4
SSD_W = D_MIX // 2
RET_W = D_MIX - HG_W - SSD_W
HG_HEADS = HG_W // HEAD_DIM
HG_DK = HEAD_DIM
HG_DV = HEAD_DIM
SSD_HEADS = SSD_W // HEAD_DIM
SSD_P = HEAD_DIM
SSD_N = 64
SSD_GROUPS = 2
SSD_CONV = 3
SSD_CONV_CH = SSD_W + 2 * SSD_GROUPS * SSD_N
RET_HEADS = RET_W // HEAD_DIM
RET_DK = HEAD_DIM
RET_DV = HEAD_DIM
RET_BWD_OFFSET = 0.5
ROPE_BASE = 10000.0
HG_COLS = 5 * HG_W
SSD_COLS = SSD_W + SSD_CONV_CH + 2 * SSD_HEADS
RET_COLS = 4 * RET_W
D_IN = HG_COLS + SSD_COLS + RET_COLS
N_EXPERTS = 16
EC_CAPACITY_FACTOR = 2
D_EXPERT = 512

kernel_name = "hybrid_diffusion_ctx_prefix_step"

def rms_norm(x, g):
    xf = x.astype(jnp.float32)
    y = xf * lax.rsqrt(jnp.mean(xf * xf, axis=-1, keepdims=True) + EPS) * g.astype(jnp.float32)
    return y.astype(x.dtype)

def head_norm(o, n_heads, gain, centre):
    B, T, W = o.shape
    oh = o.astype(jnp.float32).reshape(B, T, n_heads, W // n_heads)
    if centre:
        oh = oh - jnp.mean(oh, axis=-1, keepdims=True)
    oh = oh * lax.rsqrt(jnp.mean(oh * oh, axis=-1, keepdims=True) + EPS)
    return oh.reshape(B, T, W) * gain.astype(jnp.float32)

def axial_rope(n_tokens):
    rows = n_tokens // GRID_W
    row = jnp.repeat(jnp.arange(rows, dtype=jnp.float32), GRID_W)
    col = jnp.tile(jnp.arange(GRID_W, dtype=jnp.float32), rows)
    n_freq = RET_DK // 4
    inv_freq = ROPE_BASE ** (-jnp.arange(n_freq, dtype=jnp.float32) / n_freq)
    ang = jnp.concatenate([row[:, None] * inv_freq, col[:, None] * inv_freq], axis=-1)
    return jnp.cos(ang), jnp.sin(ang)

def apply_rope(x, cos, sin):
    half = x.shape[-1] // 2
    x1, x2 = x[..., :half], x[..., half:]
    cos, sin = cos[None, :, None, :], sin[None, :, None, :]
    return jnp.concatenate([x1 * cos - x2 * sin, x1 * sin + x2 * cos], axis=-1)

def centred_depthwise_conv(u, w, b):
    ch = u.shape[-1]
    out = lax.conv_general_dilated(
        u, w[:, None, :].astype(u.dtype), window_strides=(1,),
        padding=[((SSD_CONV - 1) // 2, SSD_CONV // 2)],
        dimension_numbers=("NWC", "WIO", "NWC"), feature_group_count=ch)
    return out + b.astype(u.dtype)

def chunked_linear_recurrence(q, k, v, log_g, s0):
    B, T, H, K = q.shape
    V = v.shape[-1]
    Kd = log_g.shape[-1]
    n = T // CHUNK

    def to_chunks(a):
        a = a.astype(jnp.float32)
        return a.reshape(B, n, CHUNK, H, a.shape[-1]).transpose(1, 0, 3, 2, 4)

    causal = jnp.tril(jnp.ones((CHUNK, CHUNK), dtype=bool))[:, :, None]

    def step(S, blk):
        qb, kb, vb, gb = blk
        b = jnp.cumsum(gb, axis=2)
        diff = jnp.where(causal, b[:, :, :, None, :] - b[:, :, None, :, :], 0.0)
        dec = jnp.where(causal, jnp.exp(diff), 0.0)
        if Kd == 1:
            A = jnp.einsum("bhtk,bhsk->bhts", qb, kb) * dec[..., 0]
        else:
            A = jnp.einsum("bhtk,bhsk,bhtsk->bhts", qb, kb, dec)
        o = jnp.einsum("bhts,bhsv->bhtv", A, vb) + jnp.einsum("bhtk,bhkv->bhtv", qb * jnp.exp(b), S)
        b_end = b[:, :, -1:, :]
        S = jnp.exp(b_end[:, :, 0, :, None]) * S + jnp.einsum("bhsk,bhsv->bhkv", kb * jnp.exp(b_end - b), vb)
        return S, o

    S, o = lax.scan(step, s0.astype(jnp.float32), (to_chunks(q), to_chunks(k), to_chunks(v), to_chunks(log_g)))
    return o.transpose(1, 0, 3, 2, 4).reshape(B, T, H, V), S

def bidirectional_recurrence(fwd, bwd, s0):
    B, T, H, K = fwd[0].shape
    V = fwd[2].shape[-1]
    q, k, v, g = (jnp.concatenate([a, b[:, ::-1]], axis=2) for a, b in zip(fwd, bwd))
    o, s = chunked_linear_recurrence(q, k, v, g, s0.reshape(B, 2 * H, K, V))
    return o[:, :, :H] + o[:, ::-1, H:], s.reshape(B, 2, H, K, V)

def hgrn2_group(u, s0, lb, norm_g):
    B, T, _ = u.shape
    q, i, f_f, f_b, g = jnp.split(u, 5, axis=-1)
    heads = lambda a: a.reshape(B, T, HG_HEADS, -1)
    q = heads(jax.nn.silu(q.astype(jnp.float32))) * HG_DK ** -0.5
    v = heads(i.astype(jnp.float32))

    def direction(f_raw, lb_dir):
        fr = f_raw.astype(jnp.float32)
        f = lb_dir + (1.0 - lb_dir) * jax.nn.sigmoid(fr)
        key = (1.0 - lb_dir) * jax.nn.sigmoid(-fr)
        return (q, heads(key), v, heads(jnp.log(f)))

    o, s = bidirectional_recurrence(direction(f_f, lb[0]), direction(f_b, lb[1]), s0)
    o = head_norm(o.reshape(B, T, HG_W), HG_HEADS, norm_g, centre=False) * jax.nn.silu(g.astype(jnp.float32))
    return o.astype(u.dtype), s

def ssd_group(u, s0, conv_w, conv_b, dt_bias, a_log, d_skip, norm_g):
    B, T, _ = u.shape
    z, xbc, dt_f, dt_b = jnp.split(u, [SSD_W, SSD_W + SSD_CONV_CH, SSD_W + SSD_CONV_CH + SSD_HEADS], axis=-1)
    xbc = jax.nn.silu(centred_depthwise_conv(xbc, conv_w, conv_b)).astype(jnp.float32)
    xs, bm, cm = jnp.split(xbc, [SSD_W, SSD_W + SSD_GROUPS * SSD_N], axis=-1)
    xs = xs.reshape(B, T, SSD_HEADS, SSD_P)
    per_group = SSD_HEADS // SSD_GROUPS
    bm = jnp.repeat(bm.reshape(B, T, SSD_GROUPS, SSD_N), per_group, axis=2)
    cm = jnp.repeat(cm.reshape(B, T, SSD_GROUPS, SSD_N), per_group, axis=2)

    def direction(dt_raw, d):
        dt = jax.nn.softplus(dt_raw.astype(jnp.float32) + dt_bias[d].astype(jnp.float32))
        log_a = (dt * -jnp.exp(a_log[d].astype(jnp.float32)))[..., None]
        return (cm, bm, xs * dt[..., None], log_a)

    y, s = bidirectional_recurrence(direction(dt_f, 0), direction(dt_b, 1), s0)
    y = (y + xs * d_skip.astype(jnp.float32)[:, None]).reshape(B, T, SSD_W)
    y = rms_norm(y * jax.nn.silu(z.astype(jnp.float32)), norm_g)
    return y.astype(u.dtype), s

def retention_log_decay(offset):
    return jnp.log1p(-(2.0 ** (-5.0 - offset - jnp.arange(RET_HEADS, dtype=jnp.float32))))

def retention_group(u, s0, rope, norm_g):
    B, T, _ = u.shape
    q, k, v, g = jnp.split(u, 4, axis=-1)
    heads = lambda a: a.astype(jnp.float32).reshape(B, T, RET_HEADS, -1)
    q, k, v = heads(q), heads(k) * RET_DK ** -0.5, heads(v)
    if rope is not None:
        q, k = apply_rope(q, *rope), apply_rope(k, *rope)

    def log_decay(offset):
        return jnp.broadcast_to(retention_log_decay(offset)[:, None], (B, T, RET_HEADS, 1))

    o, s = bidirectional_recurrence((q, k, v, log_decay(0.0)), (q, k, v, log_decay(RET_BWD_OFFSET)), s0)
    o = head_norm(o.reshape(B, T, RET_W), RET_HEADS, norm_g, centre=True) * jax.nn.silu(g.astype(jnp.float32))
    return o.astype(u.dtype), s

def mixer_block(h, s0, rope, lb, l, p):
    proj = h @ p["w_in"][l]
    u_hg, u_ssd, u_ret = jnp.split(proj, [HG_COLS, HG_COLS + SSD_COLS], axis=-1)
    y_hg, st_hg = hgrn2_group(u_hg, s0[0], lb, p["hg_norm_g"][l])
    y_ssd, st_ssd = ssd_group(u_ssd, s0[1], p["ssd_conv_w"][l], p["ssd_conv_b"][l], p["ssd_dt_bias"][l],
                              p["ssd_a_log"][l], p["ssd_d"][l], p["ssd_norm_g"][l])
    y_ret, st_ret = retention_group(u_ret, s0[2], rope, p["ret_norm_g"][l])
    y = jnp.concatenate([y_hg, y_ssd, y_ret], axis=-1) @ p["w_out"][l]
    return y, (st_hg, st_ssd, st_ret)

def expert_choice_ffn(h, w_router, w_gate, w_up, w_down):
    B, N, D = h.shape
    cap = EC_CAPACITY_FACTOR * N // N_EXPERTS
    aff = jax.nn.softmax((h @ w_router).astype(jnp.float32), axis=-1)
    gate, idx = lax.top_k(jnp.swapaxes(aff, 1, 2), cap)
    xs = jax.vmap(lambda hb, ib: hb[ib])(h, idx)
    hid = jax.nn.silu(jnp.einsum("becd,edf->becf", xs, w_gate)) * jnp.einsum("becd,edf->becf", xs, w_up)
    ys = jnp.einsum("becf,efd->becd", hid, w_down) * gate[..., None].astype(h.dtype)
    return jax.vmap(lambda yb, ib: jnp.zeros((N, D), yb.dtype).at[ib.reshape(-1)].add(yb.reshape(-1, D)))(ys, idx)

def run_trunk(x, cond, s_hg, s_ssd, s_ret, rope, lb_all, p):
    B = x.shape[0]
    new_hg, new_ssd, new_ret = [], [], []
    for l in range(DEPTH):
        if s_hg is None:
            s0 = (jnp.zeros((B, 2, HG_HEADS, HG_DK, HG_DV), jnp.float32),
                  jnp.zeros((B, 2, SSD_HEADS, SSD_N, SSD_P), jnp.float32),
                  jnp.zeros((B, 2, RET_HEADS, RET_DK, RET_DV), jnp.float32))
        else:
            s0 = (s_hg[:, l], s_ssd[:, l], s_ret[:, l])
        mod = jax.nn.silu(cond) @ p["w_ada"][l] + p["b_ada"][l]
        sh1, sc1, g1, sh2, sc2, g2 = jnp.split(mod[:, None, :], 6, axis=-1)
        h = rms_norm(x, p["norm1_g"][l]) * (1 + sc1) + sh1
        y, (st_hg, st_ssd, st_ret) = mixer_block(h, s0, rope, lb_all[l], l, p)
        x = x + g1 * y
        h = rms_norm(x, p["norm2_g"][l]) * (1 + sc2) + sh2
        x = x + g2 * expert_choice_ffn(h, p["w_router"][l], p["w_gate"][l], p["w_up"][l], p["w_down"][l])
        new_hg.append(st_hg)
        new_ssd.append(st_ssd)
        new_ret.append(st_ret)
    return rms_norm(x, p["final_g"]), jnp.stack(new_hg, axis=1), jnp.stack(new_ssd, axis=1), jnp.stack(new_ret, axis=1)

def setup_inputs(seed: int = 0) -> dict:
    key = jax.random.key(seed)
    ks = iter(jax.random.split(key, 32))
    f32 = jnp.float32

    def nrm(shape, scale):
        return jax.random.normal(next(ks), shape, f32) * scale

    L, D = DEPTH, D_MODEL
    dt0 = jnp.exp(jax.random.uniform(next(ks), (L, 2, SSD_HEADS), f32, math.log(1e-3), math.log(1e-1)))
    a0 = jax.random.uniform(next(ks), (L, 2, SSD_HEADS), f32, 1.0, 16.0)
    return {
        "x_prompt": nrm((BATCH, SEQ, D), 1.0),
        "x_sample": nrm((DEC_BATCH, DEC_SEQ, D), 1.0),
        "state_hgrn": nrm((DEC_BATCH, L, 2, HG_HEADS, HG_DK, HG_DV), 0.5),
        "state_ssd": nrm((DEC_BATCH, L, 2, SSD_HEADS, SSD_N, SSD_P), 0.5),
        "state_ret": nrm((DEC_BATCH, L, 2, RET_HEADS, RET_DK, RET_DV), 0.5),
        "c": nrm((DEC_BATCH, D), 1.0),
        "c_ctx": nrm((D,), 1.0),
        "norm1_g": 1.0 + nrm((L, D), 0.02),
        "norm2_g": 1.0 + nrm((L, D), 0.02),
        "final_g": 1.0 + nrm((D,), 0.02),
        "w_ada": nrm((L, D, 6 * D), D ** -0.5),
        "b_ada": nrm((L, 6 * D), 0.02),
        "w_in": nrm((L, D, D_IN), D ** -0.5),
        "w_out": nrm((L, D_MIX, D), D_MIX ** -0.5),
        "hg_lb": nrm((L, 2, HG_W), 1.0),
        "hg_norm_g": 1.0 + nrm((L, HG_W), 0.02),
        "ssd_conv_w": nrm((L, SSD_CONV, SSD_CONV_CH), SSD_CONV ** -0.5),
        "ssd_conv_b": nrm((L, SSD_CONV_CH), 0.02),
        "ssd_dt_bias": dt0 + jnp.log(-jnp.expm1(-dt0)),
        "ssd_a_log": jnp.log(a0),
        "ssd_d": 1.0 + nrm((L, SSD_HEADS), 0.1),
        "ssd_norm_g": 1.0 + nrm((L, SSD_W), 0.02),
        "ret_norm_g": 1.0 + nrm((L, RET_W), 0.02),
        "w_router": nrm((L, D, N_EXPERTS), D ** -0.5),
        "w_gate": nrm((L, N_EXPERTS, D, D_EXPERT), D ** -0.5),
        "w_up": nrm((L, N_EXPERTS, D, D_EXPERT), D ** -0.5),
        "w_down": nrm((L, N_EXPERTS, D_EXPERT, D), D_EXPERT ** -0.5),
    }

def reference(x_prompt, x_sample, state_hgrn, state_ssd, state_ret, c, c_ctx, norm1_g, norm2_g, final_g,
              w_ada, b_ada, w_in, w_out, hg_lb, hg_norm_g, ssd_conv_w, ssd_conv_b, ssd_dt_bias, ssd_a_log,
              ssd_d, ssd_norm_g, ret_norm_g, w_router, w_gate, w_up, w_down):
    p = {
        "norm1_g": norm1_g, "norm2_g": norm2_g, "final_g": final_g, "w_ada": w_ada, "b_ada": b_ada,
        "w_in": w_in, "w_out": w_out, "hg_norm_g": hg_norm_g, "ssd_conv_w": ssd_conv_w,
        "ssd_conv_b": ssd_conv_b, "ssd_dt_bias": ssd_dt_bias, "ssd_a_log": ssd_a_log, "ssd_d": ssd_d,
        "ssd_norm_g": ssd_norm_g, "ret_norm_g": ret_norm_g, "w_router": w_router, "w_gate": w_gate,
        "w_up": w_up, "w_down": w_down,
    }
    lb_p = jax.nn.softmax(hg_lb.astype(jnp.float32), axis=0)
    lb_all = jnp.cumsum(lb_p, axis=0) - lb_p[0]
    y_prompt, new_state_hgrn, new_state_ssd, new_state_ret = run_trunk(
        x_prompt, c_ctx[None, :], None, None, None, None, lb_all, p)
    rope = axial_rope(x_sample.shape[1])
    y_sample, _, _, _ = run_trunk(x_sample, c, state_hgrn, state_ssd, state_ret, rope, lb_all, p)
    return (y_prompt, y_sample, new_state_hgrn, new_state_ssd, new_state_ret)


_drawn_inputs = setup_inputs


def setup_inputs(seed=0):
    import zlib

    import numpy as np

    out = dict(_drawn_inputs(seed))
    spreads = {}
    factors = {'state_hgrn': 8.0,
     'state_ret': 2.705,
     'final_g': 7.878,
     'hg_norm_g': 13.807,
     'ssd_norm_g': 8.226,
     'ret_norm_g': 14.285,
     'norm2_g': 2.903}
    for name, (base, spread) in spreads.items():
        noise = np.random.default_rng([zlib.crc32(name.encode()), seed]).standard_normal(out[name].shape)
        drawn = base * np.exp(spread * noise) if base else spread * noise
        out[name] = jnp.asarray(drawn.astype(out[name].dtype))
    for name, factor in factors.items():
        out[name] = (out[name] * factor).astype(out[name].dtype)
    return out
```

```python
import math
from contextlib import ExitStack

import numpy as np

import concourse.bass as bass
from concourse import mybir

F32 = mybir.dt.float32
U8 = mybir.dt.uint8
U32 = mybir.dt.uint32
ALU = mybir.AluOpType
ACT = mybir.ActivationFunctionType
AX = mybir.AxisListType.X

P = 128
D = 1024
DC = D // P
DEPTH = 2
SEQ = 128
DEC = 1024
T = SEQ + DEC
NT = T // P
HD = 64
GRID_W = 64
EPS = 1e-6
HGW, SSDW, RETW = 256, 512, 256
D_IN = 3600
NE = 16
DE = 512
FC = DE // P
CAP_S = 2 * DEC // NE
CAP_P = 2 * SEQ // NE
NL = 7

W_Q, W_I, W_F, W_G, W_Z, W_X, W_DT, W_RQ, W_RV, W_RG = 0, 256, 512, 1024, 1280, 1792, 2560, 2576, 3088, 3344
J_Q, J_V, J_F, J_K, J_Z, J_G, J_RQ, J_RV, J_N = 0, 256, 512, 1024, 1536, 2048, 2560, 3072, 3328
UC = 6

C_ID, C_ONE = 0, 128
C_TRI = 256
C_LEV = C_TRI + 4 * P
C_RM = C_LEV + 2 * 8 * P
C_RQ = C_RM + 4 * P
C_RK = C_RQ + 4 * P
C_RT = C_RK + 8
C_COS = C_RT + 4
C_SIN = C_COS + NT * 64
C_HALO = C_SIN + NT * 64
C_N = C_HALO + NT * 2


def shape_constants():
    c = np.zeros((P, C_N), np.float64)
    i = np.arange(P)
    r, t = i[:, None], i[None, :]
    c[:, C_ID:C_ID + P] = np.eye(P)
    c[:, C_ONE:C_ONE + P] = 1
    for j, m in enumerate((r <= t, r >= t, r > t, r < t)):
        c[:, C_TRI + j * P:C_TRI + (j + 1) * P] = m
    masks = np.zeros((P, NL, P), np.float32)
    for lev in range(NL):
        half = P >> (lev + 1)
        mid = t // (2 * half) * 2 * half + half
        f = np.where(t >= mid, (r >= mid) & (r <= t), (r > t) & (r < mid))
        b = np.where(t < mid, (r >= t) & (r < mid), (r >= mid) & (r < t))
        for d, m in enumerate((f, b)):
            o = C_LEV + (d * 8 + lev) * P
            c[:, o:o + P] = m
        masks[:, lev] = (r // (2 * half) == t // (2 * half)) & (r // half != t // half)
    c[:, C_LEV + 7 * P:C_LEV + 8 * P] = r <= t
    c[:, C_LEV + 15 * P:C_LEV + 16 * P] = r >= t
    for d in range(2):
        for h in range(4):
            lg = math.log1p(-(2.0 ** (-5.0 - 0.5 * d - h)))
            c[:, C_RM + h * P:C_RM + (h + 1) * P] += np.exp(lg * np.abs(t - r)) * ((r <= t) if d == 0 else (r >= t))
            rows = slice(64 * (h % 2), 64 * (h % 2) + 64)
            o = C_RQ + (d * 2 + h // 2) * P
            c[rows, o:o + P] = np.exp(lg * (t + 1 if d == 0 else P - t))
            c[:, C_RK + d * 4 + h] = np.exp(lg * (127 - i if d == 0 else i))
            c[rows, C_RT + d * 2 + h // 2] = np.exp(lg * P)
    nf = HD // 4
    inv = 10000.0 ** (-np.arange(nf) / nf)
    for tile in range(NT):
        tok = np.arange(P) + (tile - 1) * P
        ang = np.concatenate([(tok // GRID_W)[:, None] * inv, (tok % GRID_W)[:, None] * inv], 1)
        co, si = (np.cos(ang), np.sin(ang)) if tile else (np.ones_like(ang), np.zeros_like(ang))
        for j, sc in enumerate((1.0, HD ** -0.5)):
            c[:, C_COS + tile * 64 + j * 32:][:, :32] = co * sc
            c[:, C_SIN + tile * 64 + j * 32:][:, :32] = si * sc
        c[:, C_HALO + tile * 2] = tile > 1
        c[:, C_HALO + tile * 2 + 1] = 0 < tile < NT - 1
    return c.astype(np.float32), masks.reshape(P, NL * P)


class Signal:

    def __init__(self, k, start=1):
        self.k, self.start = k, start

    def by(self, n, i=None):
        return n * self.k + ((i - self.k if i is not None else 0) + self.start)

    def before(self, n):
        return n * self.k + (1 - self.k)


def trunk(nc, x_prompt, x_sample, state_hgrn, state_ssd, state_ret, c, c_ctx, norm1_g, norm2_g, final_g,
          w_ada, b_ada, w_in, w_out, hg_lb, hg_norm_g, ssd_conv_w, ssd_conv_b, ssd_dt_bias, ssd_a_log,
          ssd_d, ssd_norm_g, ret_norm_g, w_router, w_gate, w_up, w_down, const_f, const_m,
          y_prompt, y_sample, new_hg, new_ssd, new_ret):
    ctx = ExitStack()
    with ctx:
        def sb(name, shape, dt=F32):
            return ctx.enter_context(nc.sbuf_tensor(name, shape, dt))

        x_d = nc.dram_tensor("x_d", (T, D), F32).ap()
        xn_d = nc.dram_tensor("xn_d", (T, D), F32).ap()
        proj_d = nc.dram_tensor("proj_d", (T, J_N), F32).ap()
        u_d = nc.dram_tensor("u_d", (UC, P, T + 2), F32).ap()
        o_d = nc.dram_tensor("o_d", (T, D), F32).ap()
        qe_d = nc.dram_tensor("qe_d", (NT, P, 9 * P), F32).ap()

        cst = sb("cst", [P, C_N])
        lev_mask = sb("lev_mask", [P, NL, P], U8)
        ident = cst[:, C_ID:C_ID + P]
        ones = cst[:, C_ONE:C_ONE + P]
        tri = cst[:, C_TRI:C_TRI + 4 * P].rearrange("p (j t) -> p j t", j=4)
        LE, GE, GT, LT = range(4)
        lev = cst[:, C_LEV:C_RM].rearrange("p (d n t) -> p d n t", d=2, n=8)
        minus_half = sb("minus_half", [P, 16])
        lb = sb("lb", [P, DEPTH, 2, 512])
        cond = sb("cond", [P, DC, 2])
        vecs = sb("vecs", [P, 88])
        mod = sb("mod", [P, 48, 2])
        scale1 = sb("scale1", [P, NT, DC])
        shift1 = sb("shift1", [P, NT, DC])
        scale2 = sb("scale2", [P, NT, DC])
        shift2 = sb("shift2", [P, NT, DC])
        gate_row = sb("gate_row", [P, 2, 2, D])
        head_row = sb("head_row", [P, 40])
        w_r = sb("w_r", [P, DC, NE])
        dt_all = sb("dt_all", [P, NT, 16])
        la_all = sb("la_all", [P, NT, 16])
        eb_all = sb("eb_all", [P, NT, 16])
        dtee = sb("dtee", [P, NT, 16])
        etot = sb("etot", [P, NT, 16])
        dec = sb("dec", [P, NT, 2, 8])
        small = sb("small", [P, 64])
        WORK = 39800
        work = sb("work", [P, WORK])

        def carve():
            at = [0]

            def take(*shape):
                n = int(np.prod(shape))
                assert at[0] + n <= WORK, (at[0], n, WORK)
                v = work[:, at[0]:at[0] + n]
                at[0] += n
                if len(shape) > 1:
                    names = "abcd"[:len(shape)]
                    v = v.rearrange(f"p ({' '.join(names)}) -> p {' '.join(names)}", **dict(zip(names, shape)))
                return v
            return take

        bank = ctx.enter_context(nc.psum_tensor("bank", [P, 8, 512], F32))

        signals, sem = {}, {}

        def by(name, n, i=None):
            return signals[name].by(n, i)

        def before(name, n):
            return signals[name].before(n)

        take = carve()
        a_rows = take(P)
        a_slab = take(6, DC, 512)
        a_diag = take(DC, P)
        a_lb = take(DEPTH, 512)
        a_mask = take(NL * P)
        a_lbt = take(4, 512)
        a_m = take(DC, 2)

        take = carve()
        p_w = take(DC, D_IN)
        p_x = take(D)
        p_xn = take(D)
        p_h = take(DC, P)
        p_out = take(J_N)
        p_sig = take(2, 512)
        p_u = take(UC, P)

        take = carve()
        st_f = take(NT + 1, 8, HD)
        st_b = take(NT + 1, 8, HD)
        l_in = take(J_N)
        l_u = take(UC, P + 2)
        l_c = take(UC, P)
        l_ct = take(UC, P)
        l_g = take(512)
        l_q = take(2, P)
        l_k = take(2, 2, P)
        l_kk = take(2, P)
        l_ex = take(2, 2, 8, P)
        l_xl = take(2, 2, NL, P)
        l_ee = take(512)
        l_kb = take(512)
        l_tm = take(5, P)
        l_rot = take(512)
        l_r1 = take(512)
        l_r2 = take(512)
        l_rqk = take(4, P)
        l_rkb = take(512)
        l_ah = take(4, P)
        l_ar = take(4, P)
        l_bc = take(2, 2, P)
        l_pr = take(2, 8, P)
        l_at = take(2, 8, P)
        l_v1 = take(2, 512)
        l_v2 = take(2, 512)
        l_sk = take(512)
        l_o = l_in[:, J_Z:J_RQ]
        l_qe = take(9, P)
        l_s = take(4, NT, 16)
        l_lt = l_s

        take = carve()
        take(NT + 1, 8, HD)
        take(NT + 1, 8, HD)
        aff_t = take(T)[0:NE, :]
        gain_row = take(D)
        r_w = take(DC, D)
        r_st = take(2, 8, HD)
        r_o = take(D)
        r_qe = take(9, P)
        r_g = take(D)
        r_gg = take(D)
        r_x = take(D)
        r_t = take(2, 512)
        r_t1, r_t2 = r_t[:, 0], r_t[:, 1]
        r_sq = take(D)
        r_y = take(D)
        r_yt = take(DC, P)
        r_gy = take(D)
        r_x1 = take(D)
        r_xn = take(D)
        r_ht = take(DC, P)
        r_af = take(P)

        take = carve()
        take(NT + 1, 8, HD)
        take(NT + 1, 8, HD)
        take(T)
        e_wg = take(DC, DE)
        e_wu = take(DC, DE)
        e_wd = take(FC, D)
        e_x = take(D)
        e_xp = take(D)
        e_xt = take(DC, CAP_S + CAP_P)
        e_sg = take(FC, CAP_S + CAP_P)
        e_h = take(FC, CAP_S + CAP_P)
        e_y = take(D)
        e_yp = take(D)
        k_t = take(4, P)
        k_idx = take(2, NE)
        k_val = take(2, NE)
        e_i = take(2)
        e_g = take(2)
        k_m8 = take(8)
        k_i8 = take(8)
        k_j = take(2)

        take = carve()
        f_g = take(D)
        f_x = take(D)
        f_y = take(D)
        f_junk = take(D)

        tick = ctx.enter_context(nc.semaphore("tick"))
        phase_end = ctx.enter_context(nc.semaphore("phase_end"))
        NPH = 6

        def barrier(eng, l, ph):
            eng.drain().then_inc(phase_end, 1)
            eng.wait_ge(phase_end, (l * NPH + ph) * 5)
            eng.sem_inc(tick, 1)

        class Link:

            def __init__(self, eng, name, n):
                self.eng, self.name, self.n, self.i = eng, name, n, 0

            def __call__(self, ins, last=False):
                self.i += 1
                ins.then_inc(sem[self.name], 1)
                if last:
                    assert self.i == signals[self.name].k, (self.name, self.i)
                else:
                    self.eng.wait_ge(sem[self.name], by(self.name, self.n, self.i))
                return ins

            def hold(self, ins):
                self(ins)
                self.eng.sem_inc(tick, 1)

        COUNTS = {
            "a_rows_in": 80, "rows_in": 48, "gain_in": 48, "wr_in": 16, "a_used": 12, "a_vecT": 1, "a_vecs": 1, "a_mod": 1,
            "a_scales": 1, "a_diag": 4, "a_rowmm": 4, "a_rowcp": 4,
            "p_x_in": 16, "p_ss": 1, "p_rv": 1, "p_rstd": 1, "p_xn": 1, "p_xT": 1, "p_hTd": 1, "p_hTa": 1,
            "p_mm": 7,
            "p_eva": 5,
            "p_evF": 1, "p_evV": 1,
            "p_f1": 1, "p_f2": 1, "p_fk": 1, "p_proj_st": 16, "p_u_st": 16,
            "l_dt": 16, "l_de": 2, "l_bmm": 1, "l_bex": 1, "l_dec0": 1,
            "l_in": 32, "l_uin": 16, "l_g": 1, "l_halo": 1, "l_cv": 5, "l_silu": 1, "l_rope": 4, "l_rkb": 1,
            "l_v": 1, "l_sk": 1, "l_prf": 1, "l_T": 4, "l_ev1": 1, "l_ev2": 1,
            "l_ev3": 1, "l_ev3b": 1, "l_ev4": 1, "l_kk": 1, "l_BC": 1, "l_RA": 1, "l_bcm": 1, "l_ar": 1, "l_D": 4,
            "l_ex": 4, "l_E": 1, "l_ee": 1, "l_kb": 1, "l_pm": 2, "l_pe": 2, "l_at": 2, "l_xl": 2, "l_lv": 8,
            "l_lc": 8, "l_oS": 1, "l_oR": 1, "l_oeR": 1, "l_oeS": 1, "l_dS": 4, "l_incA": 2, "l_incD": 2,
            "l_qe": 2, "l_qc": 1, "l_ost": 16, "l_qst": 16,
            "s_in": 128, "s_init": 1, "s_fs": 14, "s_bs": 14, "s_out": 128, "r_w_in": 16, "r_gg0": 2,
            "r_in": 48, "r_x_in": 16, "r_st": 1, "r_gg": 1, "r_i1": 1, "r_i2": 1, "r_o": 10, "r_sq": 1,
            "r_red": 2, "r_var": 1, "r_rs": 1, "r_y": 2, "r_yT": 2, "r_yt": 2, "r_out": 2, "r_gy": 2, "r_x1": 1,
            "r_ss": 1, "r_rv2": 1, "r_rs2": 1, "r_xn": 1, "r_xT": 2, "r_ht": 1, "r_lg": 1, "r_mx": 2, "r_e": 1,
            "r_ri": 1, "r_af": 1, "r_aT": 1, "r_at": 1, "r_xst": 16, "r_nst": 16,
            "k_r": 5, "k_z": 1, "k_done": 1, "k_T": 1, "k_ix": 1,
            "e_wg": 16, "e_wu": 16, "e_wd": 16, "e_ic": 1, "e_jc": 1, "e_gc": 1, "e_xg": 32, "e_xT": 4, "e_xtd": 2,
            "e_xta": 1, "e_gu": 4, "e_sg": 4, "e_h": 4, "e_dn": 4, "e_y": 4, "e_sc": 16, "e_scp": 16,
        }
        W_GROUPS = [[(W_X, 768)], [(W_Q, 512)], [(W_Z, 512), (W_G, 256), (W_RG, 256)], [(W_F, 512)], [(W_RQ, 512), (W_RV, 256), (W_DT, 16)], []]
        for j, group in enumerate(W_GROUPS):
            COUNTS[f"w{j}"] = 32 + 16 * len(group)
        SWDGE = ("e_xg", "e_sc", "e_scp")
        for name, k in COUNTS.items():
            signals[name] = Signal(k, int(name not in SWDGE))
            sem[name] = ctx.enter_context(nc.semaphore(name))
        const_in, lb_in, cond_in, x_init, zero_u, final_g_in = (
            ctx.enter_context(nc.semaphore(x)) for x in ("const_in", "lb_in", "cond_in", "x_init", "zero_u", "final_g_in"))
        dve_once, act_once, pool_once, primed = (
            ctx.enter_context(nc.semaphore(x)) for x in ("dve_once", "act_once", "pool_once", "primed"))

        def row_bc(v, n):
            return v.rearrange("(a n) -> a n", a=1).broadcast_to([P, n])

        def rows(h):
            return slice(64 * (h % 2), 64 * (h % 2) + 64)

        def halves(v, level, second):
            half = P >> (level + 1)
            lead = " ".join("xyz"[:len(v.shape) - 2])
            w = v.rearrange(f"p {lead} (n two i) -> p {lead} n two i", two=2, i=half)
            return w[(slice(None),) * (len(v.shape) - 1) + (slice(None), int(second), slice(None))]

        def tile_rows(t):
            return bass.ds(t * P, P)

        block = ctx.enter_context(nc.Block())

        @block.sync
        def _(sp):
            sp.dma_start(cst[:, :], const_f).then_inc(const_in, 16)
            sp.dma_start(a_mask, const_m).then_inc(const_in, 16)
            sp.dma_start(cond[:, :, 0], c_ctx.rearrange("(p c) -> p c", c=DC), allow_slow_non_contiguous=True).then_inc(cond_in, 16)
            sp.dma_start(cond[:, :, 1], c[0].rearrange("(p c) -> p c", c=DC), allow_slow_non_contiguous=True).then_inc(cond_in, 16)
            for l in range(DEPTH):
                sp.dma_start(a_lb[:, l, :], row_bc(hg_lb[l].rearrange("d w -> (d w)"), 512)).then_inc(lb_in, 16)
            sp.dma_start(x_d[0:SEQ, :], x_prompt[0]).then_inc(x_init, 16)
            sp.dma_start(x_d[SEQ:T, :], x_sample[0]).then_inc(x_init, 16)
            sp.wait_ge(const_in, 32)
            for col in (0, T + 1):
                sp.dma_start(u_d.rearrange("u p t -> p u t")[:, :, col:col + 1], cst[:, C_SIN:C_SIN + UC].unsqueeze(2),
                             allow_slow_non_contiguous=True).then_inc(zero_u, 16)
            sp.wait_ge(zero_u, 32)
            sp.wait_ge(x_init, 32)
            sp.wait_ge(primed, 1)

            def load_x(t, n):
                sp.wait_ge(sem["p_xn"], before("p_xn", n))
                sp.sem_inc(tick, 1)
                sp.dma_start(p_x, x_d[tile_rows(t), :]).then_inc(sem["p_x_in"], 16)

            def store_u(t, n):
                sp.wait_ge(sem["p_eva"], by("p_eva", n, 1))
                sp.sem_inc(tick, 1)
                sp.dma_start(u_d.rearrange("u p t -> p u t")[:, :, bass.ds(t * P + 1, P)], p_u).then_inc(sem["p_u_st"], 16)

            def store_proj(t, n):
                sp.wait_ge(sem["p_fk"], by("p_fk", n))
                sp.sem_inc(tick, 1)
                sp.wait_ge(sem["p_f2"], by("p_f2", n))
                sp.sem_inc(tick, 1)
                sp.wait_ge(sem["p_evV"], by("p_evV", n))
                sp.sem_inc(tick, 1)
                sp.wait_ge(sem["p_eva"], by("p_eva", n, 4))
                sp.sem_inc(tick, 1)
                sp.dma_start(proj_d[tile_rows(t), :], p_out).then_inc(sem["p_proj_st"], 16)

            with sp.Fori(0, DEPTH) as l:
                nl = l + 1
                for r0, r1, src in ((0, 8, norm1_g[l].rearrange("(b p) -> b p", p=P)), (8, 16, norm2_g[l].rearrange("(b p) -> b p", p=P)),
                                    (16, 64, b_ada[l].rearrange("(b p) -> b p", p=P)),
                                    (64, 82, ssd_conv_w[l].rearrange("j (b p) -> (j b) p", p=P)),
                                    (82, 88, ssd_conv_b[l].rearrange("(b p) -> b p", p=P))):
                    sp.dma_start(a_rows[r0:r1, :], src).then_inc(sem["a_rows_in"], 16)
                for dst, src, m in ((head_row[:, 0:16], ssd_dt_bias[l].rearrange("d h -> (d h)"), 16),
                                    (head_row[:, 16:32], ssd_a_log[l].rearrange("d h -> (d h)"), 16),
                                    (head_row[:, 32:40], ssd_d[l], 8)):
                    sp.dma_start(dst, row_bc(src, m)).then_inc(sem["rows_in"], 16)
                sp.dma_start(w_r[:, :, :], w_router[l].rearrange("(c p) e -> p c e", p=P)).then_inc(sem["wr_in"], 16)
                for j in range(12):
                    if j >= 6:
                        sp.wait_ge(sem["a_used"], by("a_used", nl, j - 5))
                        sp.sem_inc(tick, 1)
                    sp.dma_start(a_slab[:, j % 6], w_ada[l].rearrange("(p c) n -> p c n", c=DC)[:, :, j * 512:(j + 1) * 512])\
                        .then_inc(sem[f"w{j % 6}"], 16)
                sp.wait_ge(sem["rows_in"], by("rows_in", nl))
                sp.sem_inc(tick, 1)
                sp.wait_ge(sem["wr_in"], by("wr_in", nl))
                sp.sem_inc(tick, 1)
                barrier(sp, l, 1)
                for j, group in enumerate(W_GROUPS):
                    for c0, w in group:
                        sp.dma_start(p_w[:, :, c0:c0 + w], w_in[l].rearrange("(c p) n -> p c n", p=P)[:, :, c0:c0 + w])\
                            .then_inc(sem[f"w{j}"], 16)
                load_x(0, l * NT + 1)
                with sp.Fori(0, NT - 1) as t:
                    n = l * NT + t + 1
                    store_u(t, n)
                    load_x(t + 1, n + 1)
                    store_proj(t, n)
                store_u(NT - 1, l * NT + NT)
                store_proj(NT - 1, l * NT + NT)
                sp.wait_ge(sem["p_u_st"], by("p_u_st", l * NT + NT))
                sp.sem_inc(tick, 1)
                sp.wait_ge(sem["p_proj_st"], by("p_proj_st", l * NT + NT))
                sp.sem_inc(tick, 1)
                barrier(sp, l, 2)
                with sp.Fori(0, NT) as t:
                    n = l * NT + t + 1
                    sp.wait_ge(sem["l_dS"], before("l_dS", n))
                    sp.sem_inc(tick, 1)
                    sp.dma_start(l_in[:, 0:J_Z], proj_d[tile_rows(t), 0:J_Z]).then_inc(sem["l_in"], 16)
                    sp.dma_start(l_in[:, J_RQ:J_N], proj_d[tile_rows(t), J_RQ:J_N]).then_inc(sem["l_in"], 16)
                    sp.dma_start(l_u, u_d.rearrange("u p t -> p u t")[:, :, bass.ds(t * P, P + 2)]).then_inc(sem["l_uin"], 16)
                    sp.wait_ge(sem["l_qe"], by("l_qe", n))
                    sp.sem_inc(tick, 1)
                    sp.wait_ge(sem["l_qc"], by("l_qc", n))
                    sp.sem_inc(tick, 1)
                    sp.dma_start(qe_d[t], l_qe.rearrange("p a b -> p (a b)")).then_inc(sem["l_qst"], 16)
                    sp.wait_ge(sem["l_oeR"], by("l_oeR", n))
                    sp.sem_inc(tick, 1)
                    sp.wait_ge(sem["l_oeS"], by("l_oeS", n))
                    sp.sem_inc(tick, 1)
                    sp.dma_start(o_d[tile_rows(t), :], l_o).then_inc(sem["l_ost"], 16)
                sp.wait_ge(sem["l_qst"], by("l_qst", l * NT + NT))
                sp.sem_inc(tick, 1)
                sp.wait_ge(sem["l_ost"], by("l_ost", l * NT + NT))
                sp.sem_inc(tick, 1)
                barrier(sp, l, 3)
                for d, slots, slot in ((0, st_f, 1), (1, st_b, 0)):
                    for b0, st in ((0, new_hg), (2, new_ret)):
                        sp.dma_start(st[0, l, d].rearrange("(q h) k v -> (h k) q v", h=2), slots[:, slot, b0:b0 + 2, :]).then_inc(sem["s_out"], 16)
                    for g in range(2):
                        sp.dma_start(new_ssd[0, l, d][4 * g:4 * g + 4].rearrange("a n p -> n a p"), slots[64 * g:64 * g + 64, slot, 4:8, :])\
                            .then_inc(sem["s_out"], 16)
                for dst, src, m in ((gain_row[:, 0:256], hg_norm_g[l], 256), (gain_row[:, 256:768], ssd_norm_g[l], 512),
                                    (gain_row[:, 768:1024], ret_norm_g[l], 256)):
                    sp.dma_start(dst, row_bc(src, m)).then_inc(sem["gain_in"], 16)
                sp.wait_ge(sem["s_out"], by("s_out", nl))
                sp.sem_inc(tick, 1)
                for d, slots, slot in ((0, st_f, 1), (1, st_b, NT)):
                    for b0, st in ((0, state_hgrn), (2, state_ret)):
                        sp.dma_start(slots[:, slot, b0:b0 + 2, :], st[0, l, d].rearrange("(q h) k v -> (h k) q v", h=2)).then_inc(sem["s_in"], 16)
                    for g in range(2):
                        sp.dma_start(slots[64 * g:64 * g + 64, slot, 4:8, :], state_ssd[0, l, d][4 * g:4 * g + 4].rearrange("a n p -> n a p"))\
                            .then_inc(sem["s_in"], 16)
                sp.dma_start(r_w, w_out[l].rearrange("(c p) n -> p c n", p=P)).then_inc(sem["r_w_in"], 16)
                with sp.Fori(0, NT) as t:
                    n = l * NT + t + 1
                    sp.wait_ge(sem["r_i2"], before("r_i2", n))
                    sp.sem_inc(tick, 1)
                    sp.wait_ge(sem["r_gg"], before("r_gg", n))
                    sp.sem_inc(tick, 1)
                    sp.wait_ge(sem["r_y"], before("r_y", n))
                    sp.sem_inc(tick, 1)
                    sp.dma_start(r_o, o_d[tile_rows(t), :]).then_inc(sem["r_in"], 16)
                    sp.dma_start(r_qe.rearrange("p a b -> p (a b)"), qe_d[t]).then_inc(sem["r_in"], 16)
                    sp.dma_start(r_g, proj_d[tile_rows(t), J_Z:J_RQ]).then_inc(sem["r_in"], 16)
                    sp.wait_ge(sem["r_x1"], before("r_x1", n))
                    sp.sem_inc(tick, 1)
                    sp.dma_start(r_x, x_d[tile_rows(t), :]).then_inc(sem["r_x_in"], 16)
                    sp.wait_ge(sem["r_x1"], by("r_x1", n))
                    sp.sem_inc(tick, 1)
                    sp.dma_start(x_d[tile_rows(t), :], r_x1).then_inc(sem["r_xst"], 16)
                    sp.wait_ge(sem["r_xn"], by("r_xn", n))
                    sp.sem_inc(tick, 1)
                    sp.dma_start(xn_d[tile_rows(t), :], r_xn).then_inc(sem["r_nst"], 16)
                sp.wait_ge(sem["r_xst"], by("r_xst", l * NT + NT))
                sp.sem_inc(tick, 1)
                sp.wait_ge(sem["r_nst"], by("r_nst", l * NT + NT))
                sp.sem_inc(tick, 1)
                barrier(sp, l, 4)
                barrier(sp, l, 5)
                with sp.Fori(0, NE) as e:
                    n = l * NE + e + 1
                    sp.wait_ge(sem["e_gu"], before("e_gu", n))
                    sp.sem_inc(tick, 1)
                    sp.dma_start(e_wg, w_gate[l, e].rearrange("(c p) n -> p c n", p=P)).then_inc(sem["e_wg"], 16)
                    sp.dma_start(e_wu, w_up[l, e].rearrange("(c p) n -> p c n", p=P)).then_inc(sem["e_wu"], 16)
                    sp.wait_ge(sem["e_dn"], before("e_dn", n))
                    sp.sem_inc(tick, 1)
                    sp.dma_start(e_wd, w_down[l, e].rearrange("(c p) n -> p c n", p=P)).then_inc(sem["e_wd"], 16)
                barrier(sp, l, 6)
            sp.dma_start(f_g, row_bc(final_g, D)).then_inc(final_g_in, 16)
            for t in range(NT):
                n = DEPTH * NT + t + 1
                sp.wait_ge(sem["p_xn"], before("p_xn", n))
                sp.sem_inc(tick, 1)
                sp.dma_start(f_x, x_d[tile_rows(t), :]).then_inc(sem["p_x_in"], 16)
                sp.wait_ge(sem["p_f1"], by("p_f1", n))
                sp.sem_inc(tick, 1)
                dst = y_prompt[0] if t == 0 else y_sample[0][(t - 1) * P:t * P, :]
                sp.dma_start(dst, f_y).then_inc(sem["p_u_st"], 16)
            sp.wait_ge(sem["p_u_st"], by("p_u_st", DEPTH * NT + NT))
            sp.sem_inc(tick, 1)

        @block.tensor
        def _(pe):
            def turn(out, in_, k=P):
                return pe.transpose(out, in_, cst[0:k, C_ID:C_ID + k])

            pe.wait_ge(const_in, 32)
            pe.wait_ge(act_once, 1)
            pe.wait_ge(primed, 1)
            with pe.Fori(0, DEPTH) as l:
                nl = l + 1
                pe.wait_ge(sem["a_rows_in"], by("a_rows_in", nl))
                turn(bank[:, 0, 0:88], a_rows[0:88, :], 88).then_inc(sem["a_vecT"], 1)
                for j in range(12):
                    pe.wait_ge(sem[f"w{j % 6}"], by(f"w{j % 6}", nl, 16 if j < 6 else 32))
                    for b in range(4):
                        o = (j * 4 + b) * 2
                        for ch in range(DC):
                            mm = pe.matmul(bank[:, 1, o:o + 2], a_slab[:, j % 6, ch, b * P:(b + 1) * P], cond[:, ch, :],
                                           start=(ch == 0), stop=(ch == DC - 1))
                    mm.then_inc(sem["a_used"], 1)
                for i in range(4):
                    pe.wait_ge(sem["a_diag"], by("a_diag", nl, i + 1))
                    if i >= 2:
                        pe.wait_ge(sem["a_rowcp"], by("a_rowcp", nl, i - 1))
                    for half in range(2):
                        mm = pe.matmul(bank[:, 2 + 2 * (i % 2) + half, :], ones, a_diag[:, 4 * half:4 * half + 4, :], start=True, stop=True)
                    mm.then_inc(sem["a_rowmm"], 1)
                barrier(pe, l, 1)

                with pe.Fori(0, NT) as t:
                    n = l * NT + t + 1
                    pe.wait_ge(sem["p_xn"], by("p_xn", n))
                    pe.wait_ge(sem["p_eva"], before("p_eva", n))
                    for ch in range(DC):
                        mm = turn(bank[:, ch // 4, (ch % 4) * P:(ch % 4 + 1) * P], p_xn[:, ch * P:(ch + 1) * P])
                    mm.then_inc(sem["p_xT"], 1)
                    pe.wait_ge(sem["p_hTd"], by("p_hTd", n))
                    pe.wait_ge(sem["p_hTa"], by("p_hTa", n))
                    pe.wait_ge(sem["w0"], by("w0", nl))
                    for b in range(UC):
                        for ch in range(DC):
                            mm = pe.matmul(bank[:, b // 4, (b % 4) * P:(b % 4 + 1) * P], p_w[:, ch, W_X + b * P:W_X + (b + 1) * P],
                                           p_h[:, ch, :], start=(ch == 0), stop=(ch == DC - 1))
                    mm.then_inc(sem["p_mm"], 1)
                    for bk, tag, group, segs in ((2, "A", 1, [(W_Q, 512)]), (4, "C", 2, [(W_Z, 512)]), (5, "G", 2, [(W_G, 256), (W_RG, 256)]),
                                                 (3, "B", 3, [(W_F, 512)]), (6, "F", 4, [(W_RQ, 512)]), (7, "V", 4, [(W_RV, 256), (W_DT, 16)])):
                        taken = "p_ev" + tag if tag in "FV" else "p_eva"
                        pe.wait_ge(sem[taken], before(taken, n))
                        o = 0
                        pe.wait_ge(sem[f"w{group}"], by(f"w{group}", nl))
                        for c0, w in segs:
                            for ch in range(DC):
                                mm = pe.matmul(bank[:, bk, o:o + w], p_h[:, ch, :], p_w[:, ch, c0:c0 + w], start=(ch == 0), stop=(ch == DC - 1))
                            o += w
                        mm.then_inc(sem["p_mm"], 1)
                barrier(pe, l, 2)

                pe.wait_ge(sem["l_dt"], by("l_dt", nl))
                pe.matmul(bank[:, 0, 0:72], tri[:, LE, :], la_all[:, :, 0:8], start=True, stop=True)
                pe.matmul(bank[:, 0, 72:144], tri[:, GE, :], la_all[:, :, 8:16], start=True, stop=True)
                pe.matmul(bank[:, 1, 0:72], tri[:, GT, :], la_all[:, :, 0:8], start=True, stop=True)
                pe.matmul(bank[:, 1, 72:144], tri[:, LT, :], la_all[:, :, 8:16], start=True, stop=True)
                pe.matmul(bank[:, 2, 0:144], ones, la_all[:, :, :], start=True, stop=True).then_inc(sem["l_bmm"], 1)
                pe.wait_ge(sem["l_bex"], by("l_bex", nl))
                pe.sem_inc(tick, 1)
                with pe.Fori(0, NT) as t:
                    n = l * NT + t + 1
                    pe.wait_ge(sem["l_in"], by("l_in", n))
                    pe.wait_ge(sem["l_incA"], before("l_incA", n))
                    for i in range(4):
                        mm = turn(bank[:, 0, i * P:(i + 1) * P], l_in[:, (J_Q if i < 2 else J_K - 256) + i * P:][:, :P])
                    mm.then_inc(sem["l_T"], 1)
                    for i in range(2):
                        mm = turn(bank[:, 1, i * P:(i + 1) * P], l_in[:, J_K + 256 + i * P:][:, :P])
                    mm.then_inc(sem["l_T"], 1)

                    def levels(d, pair, b0):
                        for half in range(2):
                            mm = pe.matmul(bank[:, b0 + half, :], l_g[:, d * 256 + pair * P:][:, :P], lev[:, d, 4 * half:4 * half + 4, :],
                                           start=True, stop=True)
                        mm.then_inc(sem["l_D"], 1)

                    pe.wait_ge(sem["l_g"], by("l_g", n))
                    pe.wait_ge(sem["l_lc"], before("l_lc", n))
                    levels(0, 0, 6)
                    pe.wait_ge(sem["l_ev1"], by("l_ev1", n))
                    pe.wait_ge(sem["l_ev2"], by("l_ev2", n))
                    levels(0, 1, 0)
                    pe.wait_ge(sem["l_rope"], by("l_rope", n))
                    pe.wait_ge(sem["l_oeR"], before("l_oeR", n))
                    for i in range(4):
                        mm = turn(bank[:, 4, i * P:(i + 1) * P], l_rot[:, i * P:(i + 1) * P])
                    mm.then_inc(sem["l_T"], 1)
                    pe.wait_ge(sem["l_silu"], by("l_silu", n))
                    pe.wait_ge(sem["l_incD"], before("l_incD", n))
                    for i in range(5):
                        mm = turn(bank[:, 2 + i // 4, (i % 4) * P:(i % 4 + 1) * P], l_c[:, i, :])
                    mm.then_inc(sem["l_T"], 1)
                    pe.wait_ge(sem["l_oeS"], before("l_oeS", n))
                    pe.wait_ge(sem["l_ev4"], by("l_ev4", n))
                    for g in range(2):
                        mm = pe.matmul(bank[:, 5 - g, 0:P], l_c[rows(g), 4, :], l_c[rows(g), 5, :], start=True, stop=True)
                    mm.then_inc(sem["l_BC"], 1)
                    for h in range(4):
                        mm = pe.matmul(bank[:, 5 - h % 2, (2 + h // 2) * P:(3 + h // 2) * P], l_rqk[rows(h), 2 + h // 2, :], l_rqk[rows(h), h // 2, :],
                                       start=True, stop=True)
                    mm.then_inc(sem["l_RA"], 1)
                    pe.wait_ge(sem["l_ev3"], by("l_ev3", n))
                    pe.wait_ge(sem["l_ev3b"], by("l_ev3b", n))
                    levels(1, 0, 2)
                    pe.wait_ge(sem["l_ex"], by("l_ex", n, 1))
                    levels(1, 1, 6)
                    pe.wait_ge(sem["l_ar"], by("l_ar", n))
                    pe.matmul(bank[:, 5, 0:256], tri[:, GT, :], l_g[:, 0:256], start=True, stop=True)
                    pe.matmul(bank[:, 5, 256:512], tri[:, LT, :], l_g[:, 256:512], start=True, stop=True).then_inc(sem["l_E"], 1)
                    pe.wait_ge(sem["l_prf"], by("l_prf", n))
                    for d in range(2):
                        pe.wait_ge(sem["l_ex"], by("l_ex", n, 2 + d))
                        for g in range(2):
                            mm = pe.matmul(bank[:, 2 * d + g, :], tri[:, GT + d, :], l_pr[:, d, 4 * g:4 * g + 4, :], start=True, stop=True)
                        mm.then_inc(sem["l_pm"], 1)
                    pe.wait_ge(sem["l_ex"], by("l_ex", n, 4))
                    pe.wait_ge(sem["l_kk"], by("l_kk", n))
                    for i in range(8):
                        bk = 6 if i % 2 == 0 else 0
                        if i == 1:
                            pe.wait_ge(sem["l_pe"], by("l_pe", n, 1))
                        if i >= 2:
                            pe.wait_ge(sem["l_lc"], by("l_lc", n, i - 1))
                        if i == 1:
                            pe.wait_ge(sem["l_xl"], by("l_xl", n))
                        for h in range(4):
                            out = bank[:, bk + h % 2, (h // 2) * P:(h // 2 + 1) * P]
                            if i == 0:
                                mm = pe.matmul(out, l_kk[rows(h), h // 2, :], l_q[rows(h), h // 2, :], start=True, stop=True)
                                continue
                            for d in range(2):
                                x = l_xl[rows(h), d, h // 2, i - 1, :]
                                mm = pe.matmul(halves(out, i - 1, d == 0), x, halves(x, i - 1, d == 0), start=True, stop=True)
                        mm.then_inc(sem["l_lv"], 1)
                    pe.wait_ge(sem["l_lc"], by("l_lc", n))
                    for h in range(8):
                        a, v = (l_ah, J_V) if h < 4 else (l_ar, J_RV)
                        mm = pe.matmul(bank[:, 4, h * HD:(h + 1) * HD], a[:, h % 4, :], l_in[:, v + (h % 4) * HD:][:, :HD], start=True, stop=True)
                    mm.then_inc(sem["l_oR"], 1)
                    pe.wait_ge(sem["l_ee"], by("l_ee", n))
                    pe.wait_ge(sem["l_at"], by("l_at", n))
                    pe.wait_ge(sem["l_v"], by("l_v", n))
                    for h in range(8):
                        for d in range(2):
                            mm = pe.matmul(bank[:, 5, h * HD:(h + 1) * HD], l_at[:, d, h, :], l_v1[:, d, h * HD:(h + 1) * HD], start=(d == 0), stop=(d == 1))
                    mm.then_inc(sem["l_oS"], 1)
                    pe.wait_ge(sem["l_kb"], by("l_kb", n))
                    pe.wait_ge(sem["l_rkb"], by("l_rkb", n))
                    for bk, kb, v in ((0, l_kb, J_V), (1, l_rkb, J_RV)):
                        for i in range(4):
                            mm = pe.matmul(bank[:, bk, i * P:(i + 1) * P], kb[:, i * P:(i + 1) * P], l_in[:, v + (i % 2) * P:][:, :P], start=True, stop=True)
                        mm.then_inc(sem["l_dS"], 1)
                    for d in range(2):
                        pe.matmul(bank[:, 2 + d, :], l_tm[:, 4, :], l_v2[:, d, :], start=True, stop=True).then_inc(sem["l_dS"], 1)
                barrier(pe, l, 3)

                pe.wait_ge(sem["r_w_in"], by("r_w_in", nl))
                pe.sem_inc(tick, 1)
                with pe.Fori(0, NT) as t:
                    n = l * NT + t + 1
                    pe.wait_ge(sem["r_in"], by("r_in", n))
                    pe.wait_ge(sem["r_st"], by("r_st", n))
                    pe.wait_ge(sem["r_o"], before("r_o", n))
                    for b in range(4):
                        for h in range(2):
                            for d in range(2):
                                mm = pe.matmul(bank[:, 7 * h, b * HD:(b + 1) * HD], r_qe[rows(h), d * 4 + b, :], r_st[rows(h), d, b, :],
                                               start=(d == 0), stop=(d == 1))
                    mm.then_inc(sem["r_i1"], 1)
                    pe.wait_ge(sem["r_at"], before("r_at", n))
                    for d in range(2):
                        for g in range(2):
                            mm = pe.matmul(bank[:, 1 + g, d * 256:(d + 1) * 256], r_qe[rows(g), 8, :], r_st[rows(g), d, 4:8, :], start=True, stop=True)
                    mm.then_inc(sem["r_i2"], 1)
                    pe.wait_ge(sem["r_y"], by("r_y", n))
                    pe.wait_ge(sem["r_ht"], before("r_ht", n))
                    pe.wait_ge(sem["r_mx"], before("r_mx", n))
                    for half in range(2):
                        for i in range(4):
                            ch = half * 4 + i
                            mm = turn(bank[:, 3 + half, i * P:(i + 1) * P], r_y[:, ch * P:(ch + 1) * P])
                        mm.then_inc(sem["r_yT"], 1)
                    pe.wait_ge(sem["r_yt"], by("r_yt", n))
                    pe.wait_ge(sem["r_gy"], before("r_gy", n))
                    for half in range(2):
                        for ch in range(DC):
                            mm = pe.matmul(bank[:, 5 + half, :], r_yt[:, ch, :], r_w[:, ch, half * 512:(half + 1) * 512], start=(ch == 0), stop=(ch == DC - 1))
                        mm.then_inc(sem["r_out"], 1)
                    pe.wait_ge(sem["r_xn"], by("r_xn", n))
                    for half in range(2):
                        for i in range(4):
                            ch = half * 4 + i
                            mm = turn(bank[:, 7 if half == 0 else 3, i * P:(i + 1) * P], r_xn[:, ch * P:(ch + 1) * P])
                        mm.then_inc(sem["r_xT"], 1)
                    pe.wait_ge(sem["r_ht"], by("r_ht", n))
                    for ch in range(DC):
                        mm = pe.matmul(bank[:, 4, 0:NE], r_ht[:, ch, :], w_r[:, ch, :], start=(ch == 0), stop=(ch == DC - 1))
                    mm.then_inc(sem["r_lg"], 1)
                    pe.wait_ge(sem["r_af"], by("r_af", n))
                    turn(bank[:, 2, 0:P], r_af).then_inc(sem["r_aT"], 1)
                barrier(pe, l, 4)

                pe.wait_ge(sem["k_done"], by("k_done", nl))
                for i in range(4):
                    mm = turn(bank[:, 0, i * P:(i + 1) * P], k_t[:, i, :])
                mm.then_inc(sem["k_T"], 1)
                barrier(pe, l, 5)

                with pe.Fori(0, NE) as e:
                    n = l * NE + e + 1
                    pe.wait_ge(sem["e_xg"], by("e_xg", n))
                    pe.wait_ge(sem["e_y"], before("e_y", n))
                    for q in range(4):
                        src = e_x if q < 2 else e_xp
                        for i in range(4):
                            ch = (q % 2) * 4 + i
                            mm = turn(bank[:, q, i * P:(i + 1) * P], src[:, ch * P:(ch + 1) * P])
                        mm.then_inc(sem["e_xT"], 1)
                    pe.wait_ge(sem["e_xtd"], by("e_xtd", n))
                    pe.wait_ge(sem["e_xta"], by("e_xta", n))
                    pe.wait_ge(sem["e_wg"], by("e_wg", n))
                    pe.wait_ge(sem["e_wu"], by("e_wu", n))
                    pe.wait_ge(sem["e_h"], before("e_h", n))
                    for f in range(FC):
                        for o, w in ((0, e_wg), (256, e_wu)):
                            for ch in range(DC):
                                mm = pe.matmul(bank[:, 4 + f, o:o + CAP_S + CAP_P], w[:, ch, f * P:(f + 1) * P], e_xt[:, ch, :],
                                               start=(ch == 0), stop=(ch == DC - 1))
                        mm.then_inc(sem["e_gu"], 1)
                    pe.wait_ge(sem["e_h"], by("e_h", n))
                    pe.wait_ge(sem["e_wd"], by("e_wd", n))
                    for q in range(4):
                        lo, hi = (0, CAP_S) if q < 2 else (CAP_S, CAP_S + CAP_P)
                        for f in range(FC):
                            mm = pe.matmul(bank[0:hi - lo, q, :], e_h[:, f, lo:hi], e_wd[:, f, (q % 2) * 512:(q % 2 + 1) * 512],
                                           start=(f == 0), stop=(f == FC - 1))
                        mm.then_inc(sem["e_dn"], 1)
                barrier(pe, l, 6)

        @block.scalar
        def _(act):
            def ev(out, in_, func=ACT.Copy, **kw):
                return act.activation(out, in_, func, **kw)

            act.wait_ge(cond_in, 32)
            ev(cond[:, :, :], cond[:, :, :], ACT.Silu).then_inc(act_once, 1)
            act.wait_ge(dve_once, 3)
            for j in range(DEPTH):
                ev(a_lbt[:, 1 + j, :], a_lbt[:, 1 + j, :], ACT.Exp).then_inc(act_once, 1)
            act.wait_ge(primed, 1)

            def square_x(n):
                act.wait_ge(sem["p_x_in"], by("p_x_in", n))
                act.wait_ge(sem["p_rv"], before("p_rv", n))
                act.wait_ge(sem["p_xT"], before("p_xT", n))
                ev(p_xn, p_x, ACT.Square, accum_out=small[:, 0:1]).then_inc(sem["p_ss"], 1)

            def turn_p(t, n, more):
                act.wait_ge(sem["p_xT"], by("p_xT", n))
                act.wait_ge(sem["p_mm"], before("p_mm", n))
                act.sem_inc(tick, 1)
                for ch in range(4, DC):
                    last = ev(p_h[:, ch, :], bank[:, 1, (ch - 4) * P:(ch - 3) * P], ACT.Identity,
                              scale=scale1[:, t, ch:ch + 1], bias=shift1[:, t, ch:ch + 1])
                last.then_inc(sem["p_hTa"], 1)
                act.wait_ge(sem["p_mm"], by("p_mm", n, 1))
                act.wait_ge(sem["p_u_st"], before("p_u_st", n))
                ev(p_u[:, 0:4, :], bank[:, 0, :].rearrange("p (a b) -> p a b", a=4))
                ev(p_u[:, 4:6, :], bank[:, 1, 0:256].rearrange("p (a b) -> p a b", a=2)).then_inc(sem["p_eva"], 1)
                act.wait_ge(sem["p_mm"], by("p_mm", n, 2))
                act.wait_ge(sem["p_proj_st"], before("p_proj_st", n))
                ev(p_out[:, J_V:J_V + 256], bank[:, 2, 256:512])
                ev(p_out[:, J_Q:J_Q + 256], bank[:, 2, 0:256], ACT.Silu).then_inc(sem["p_eva"], 1)
                act.wait_ge(sem["p_mm"], by("p_mm", n, 3))
                ev(p_out[:, J_Z:J_Z + 512], bank[:, 4, :], ACT.Silu).then_inc(sem["p_eva"], 1)
                if more:
                    square_x(n + 1)
                act.wait_ge(sem["p_mm"], by("p_mm", n, 4))
                ev(p_out[:, J_G:J_G + 512], bank[:, 5, :], ACT.Silu).then_inc(sem["p_eva"], 1)
                act.wait_ge(sem["p_mm"], by("p_mm", n, 5))
                act.wait_ge(sem["p_f2"], before("p_f2", n))
                act.wait_ge(sem["p_fk"], before("p_fk", n))
                ev(p_sig[:, 0, :], bank[:, 3, :], ACT.Sigmoid)
                ev(p_sig[:, 1, :], bank[:, 3, :], ACT.Sigmoid, scale=-1.0).then_inc(sem["p_eva"], 1)

            with act.Fori(0, DEPTH) as l:
                nl = l + 1
                for i in range(4):
                    act.wait_ge(sem["a_rowmm"], by("a_rowmm", nl, i + 1))
                    b0 = 2 + 2 * (i % 2)
                    ev(gate_row[:, i // 2, i % 2, :], bank[:, b0:b0 + 2, :].rearrange("p a b -> p (a b)")).then_inc(sem["a_rowcp"], 1)
                act.wait_ge(sem["rows_in"], by("rows_in", nl))
                ev(small[:, 40:56], head_row[:, 16:32], ACT.Exp).then_inc(act_once, 1)
                barrier(act, l, 1)
                square_x(l * NT + 1)
                with act.Fori(0, NT - 1) as t:
                    turn_p(t, l * NT + t + 1, True)
                turn_p(NT - 1, l * NT + NT, False)
                barrier(act, l, 2)
                act.wait_ge(sem["l_de"], by("l_de", nl))
                ev(l_s[:, 1], l_s[:, 1], ACT.Exp).then_inc(act_once, 1)
                act.wait_ge(sem["l_bmm"], by("l_bmm", nl))
                for d in range(2):
                    ev(eb_all[:, :, 8 * d:8 * d + 8], bank[:, 0, 72 * d:72 * d + 72].rearrange("p (a b) -> p a b", b=8), ACT.Exp)
                    ev(l_s[:, 2, :, 8 * d:8 * d + 8], bank[:, 1, 72 * d:72 * d + 72].rearrange("p (a b) -> p a b", b=8), ACT.Exp)
                ev(etot[:, :, :], bank[:, 2, 0:144].rearrange("p (a b) -> p a b", b=16), ACT.Exp).then_inc(sem["l_bex"], 1)
                with act.Fori(0, NT) as t:
                    n = l * NT + t + 1

                    def levels_exp(d, pair, b0, i):
                        act.wait_ge(sem["l_D"], by("l_D", n, i))
                        ev(l_ex[:, d, pair].rearrange("p a b -> p (a b)"), bank[:, b0:b0 + 2, :].rearrange("p a b -> p (a b)"), ACT.Exp)\
                            .then_inc(sem["l_ex"], 1)

                    act.wait_ge(sem["l_in"], by("l_in", n))
                    act.wait_ge(sem["l_E"], before("l_E", n))
                    ev(l_g, l_in[:, J_F:J_F + 512], ACT.Ln).then_inc(sem["l_g"], 1)
                    act.wait_ge(sem["l_T"], by("l_T", n, 1))
                    act.wait_ge(sem["l_xl"], before("l_xl", n))
                    act.wait_ge(sem["l_qe"], before("l_qe", n))
                    act.wait_ge(sem["l_lv"], before("l_lv", n))
                    ev(l_q, bank[:, 0, 0:256].rearrange("p (a b) -> p a b", a=2), scale=HD ** -0.5)
                    ev(l_k[:, 0], bank[:, 0, 256:512].rearrange("p (a b) -> p a b", a=2)).then_inc(sem["l_ev1"], 1)
                    levels_exp(0, 0, 6, 1)
                    levels_exp(0, 1, 0, 2)
                    act.wait_ge(sem["l_cv"], by("l_cv", n))
                    for b in range(UC):
                        last = ev(l_c[:, b, :], l_c[:, b, :], ACT.Silu, bias=vecs[:, 82 + b:83 + b])
                    last.then_inc(sem["l_silu"], 1)
                    act.wait_ge(sem["l_T"], by("l_T", n, 4))
                    act.wait_ge(sem["l_v"], before("l_v", n))
                    act.wait_ge(sem["l_sk"], before("l_sk", n))
                    act.wait_ge(sem["l_dS"], before("l_dS", n))
                    ev(l_tm[:, 0:4, :], bank[:, 2, :].rearrange("p (a b) -> p a b", a=4)).then_inc(sem["l_ev3"], 1)
                    levels_exp(1, 0, 2, 3)
                    levels_exp(1, 1, 6, 4)
                    act.wait_ge(sem["l_E"], by("l_E", n))
                    act.wait_ge(sem["l_kb"], before("l_kb", n))
                    ev(l_ee, bank[:, 5, :], ACT.Exp).then_inc(sem["l_ee"], 1)
                    for d in range(2):
                        act.wait_ge(sem["l_pm"], by("l_pm", n, d + 1))
                        act.wait_ge(sem["l_oS"], before("l_oS", n))
                        ev(l_at[:, d].rearrange("p a b -> p (a b)"), bank[:, 2 * d:2 * d + 2, :].rearrange("p a b -> p (a b)"), ACT.Exp)\
                            .then_inc(sem["l_pe"], 1)
                    act.wait_ge(sem["l_oR"], by("l_oR", n))
                    act.wait_ge(sem["l_ost"], before("l_ost", n))
                    ev(l_o[:, 0:256], bank[:, 4, 0:256])
                    ev(l_o[:, 768:1024], bank[:, 4, 256:512]).then_inc(sem["l_oeR"], 1)
                    for i in range(2):
                        act.wait_ge(sem["l_dS"], by("l_dS", n, i + 1))
                        act.sem_inc(tick, 1)
                        for g in range(2):
                            src = bank[rows(g), i, :].rearrange("p (d q v) -> p d q v", d=2, q=2)[:, :, :, 64 * g:64 * g + 64]
                            ev(st_f[rows(g), t + 1, 2 * i:2 * i + 2, :], src[:, 0])
                            last = ev(st_b[rows(g), t, 2 * i:2 * i + 2, :], src[:, 1])
                        last.then_inc(sem["l_incA"], 1)
                barrier(act, l, 3)
                with act.Fori(0, NT) as t:
                    n = l * NT + t + 1
                    act.wait_ge(sem["r_o"], by("r_o", n))
                    act.wait_ge(sem["r_red"], before("r_red", n))
                    ev(r_sq, r_o, ACT.Square).then_inc(sem["r_sq"], 1)
                    for half in range(2):
                        act.wait_ge(sem["r_yT"], by("r_yT", n, half + 1))
                        act.wait_ge(sem["r_out"], before("r_out", n))
                        ev(r_yt[:, 4 * half:4 * half + 4, :], bank[:, 3 + half, :].rearrange("p (a b) -> p a b", a=4)).then_inc(sem["r_yt"], 1)
                    act.wait_ge(sem["r_x1"], by("r_x1", n))
                    act.wait_ge(sem["r_rv2"], before("r_rv2", n))
                    act.wait_ge(sem["r_red"], by("r_red", n))
                    ev(r_sq, r_x1, ACT.Square, accum_out=small[:, 0:1]).then_inc(sem["r_ss"], 1)
                    act.wait_ge(sem["r_mx"], by("r_mx", n))
                    act.wait_ge(sem["r_af"], before("r_af", n))
                    ev(small[:, 16:32], bank[:, 4, 0:NE], ACT.Exp, bias=small[:, 13:14], accum_out=small[:, 14:15]).then_inc(sem["r_e"], 1)
                    act.wait_ge(sem["r_aT"], by("r_aT", n))
                    act.sem_inc(tick, 1)
                    ev(aff_t[:, tile_rows(t)], bank[0:NE, 2, 0:P]).then_inc(sem["r_at"], 1)
                barrier(act, l, 4)
                barrier(act, l, 5)
                with act.Fori(0, NE) as e:
                    n = l * NE + e + 1
                    act.wait_ge(sem["e_xT"], by("e_xT", n, 2))
                    act.wait_ge(sem["e_gu"], before("e_gu", n))
                    for ch in range(4, DC):
                        last = ev(e_xt[:, ch, 0:CAP_S], bank[:, 1, (ch - 4) * P:(ch - 3) * P], ACT.Identity,
                                  scale=scale2[:, 1, ch:ch + 1], bias=shift2[:, 1, ch:ch + 1])
                    last.then_inc(sem["e_xta"], 1)
                    for f in range(FC):
                        act.wait_ge(sem["e_gu"], by("e_gu", n, f + 1))
                        act.wait_ge(sem["e_h"], before("e_h", n))
                        ev(e_sg[:, f, :], bank[:, 4 + f, 0:CAP_S + CAP_P], ACT.Silu).then_inc(sem["e_sg"], 1)
                barrier(act, l, 6)
            for t in range(NT):
                n = DEPTH * NT + t + 1
                act.wait_ge(sem["p_x_in"], by("p_x_in", n))
                act.wait_ge(sem["p_rv"], before("p_rv", n))
                ev(f_junk, f_x, ACT.Square, accum_out=small[:, 0:1]).then_inc(sem["p_ss"], 1)

        @block.vector
        def _(dve):
            def tt(out, a, b, op=ALU.mult):
                return dve.tensor_tensor(out, a, b, op)

            def bc(v, n):
                return v.unsqueeze(len(v.shape)).broadcast_to(list(v.shape) + [n])

            once = [0]

            def step(ins):
                once[0] += 1
                ins.then_inc(dve_once, 1)
                dve.wait_ge(dve_once, once[0])

            dve.wait_ge(lb_in, 32)
            step(tt(a_lbt[:, 0, :], a_lb[:, 0, :], a_lb[:, 1, :], ALU.max))
            for j in range(DEPTH):
                step(tt(a_lbt[:, 1 + j, :], a_lb[:, j, :], a_lbt[:, 0, :], ALU.subtract))
            dve.wait_ge(act_once, 3)
            step(tt(a_lbt[:, 3, :], a_lbt[:, 1, :], a_lbt[:, 2, :], ALU.add))
            step(dve.reciprocal(a_lbt[:, 3, :], a_lbt[:, 3, :]))
            for j in range(DEPTH):
                step(tt(a_lbt[:, 1 + j, :], a_lbt[:, 1 + j, :], a_lbt[:, 3, :]))
            step(tt(a_lbt[:, 2, :], a_lbt[:, 1, :], a_lbt[:, 2, :], ALU.add))
            step(tt(lb[:, 0, 0, :], a_lbt[:, 1, :], a_lbt[:, 1, :], ALU.subtract))
            step(tt(lb[:, 1, 0, :], a_lbt[:, 2, :], a_lbt[:, 1, :], ALU.subtract))
            for j in range(DEPTH):
                step(dve.tensor_scalar(lb[:, j, 1, :], lb[:, j, 0, :], -1.0, 1.0, ALU.mult, ALU.add))
            dve.wait_ge(const_in, 32)
            step(dve.tensor_copy(lev_mask[:, :, :].rearrange("p a b -> p (a b)"), a_mask))
            dve.wait_ge(primed, 1)

            def norm_x(n):
                dve.wait_ge(sem["p_rstd"], by("p_rstd", n))
                dve.wait_ge(sem["p_xT"], before("p_xT", n))
                dve.tensor_scalar(p_xn, p_x, small[:, 2:3], None, ALU.mult).then_inc(sem["p_xn"], 1)

            def turn_p(l, t, n, more):
                dve.wait_ge(sem["p_xT"], by("p_xT", n))
                dve.wait_ge(sem["p_mm"], before("p_mm", n))
                for ch in range(4):
                    last = dve.tensor_scalar(p_h[:, ch, :], bank[:, 0, ch * P:(ch + 1) * P], scale1[:, t, ch:ch + 1],
                                             shift1[:, t, ch:ch + 1], ALU.mult, ALU.add)
                last.then_inc(sem["p_hTd"], 1)
                if more:
                    norm_x(n + 1)
                dve.wait_ge(sem["p_eva"], by("p_eva", n, 5))
                dve.wait_ge(sem["p_proj_st"], before("p_proj_st", n))
                tt(p_sig[:, 0, :], p_sig[:, 0, :], lb[:, l, 1, :]).then_inc(sem["p_f1"], 1)
                tt(p_out[:, J_K:J_K + 512], p_sig[:, 1, :], lb[:, l, 1, :]).then_inc(sem["p_fk"], 1)
                dve.wait_ge(sem["p_f1"], by("p_f1", n))
                dve.scalar_tensor_tensor(out=p_out[:, J_F:J_F + 512], in0=p_sig[:, 0, :], scalar=2.0 ** -60, in1=lb[:, l, 0, :],
                                         op0=ALU.max, op1=ALU.add).then_inc(sem["p_f2"], 1)
                dve.wait_ge(sem["p_mm"], by("p_mm", n, 6))
                dve.tensor_copy(p_out[:, J_RQ:J_RQ + 512], bank[:, 6, :]).then_inc(sem["p_evF"], 1)
                dve.wait_ge(sem["p_mm"], by("p_mm", n, 7))
                dve.tensor_copy(p_out[:, J_RV:J_RV + 256], bank[:, 7, 0:256])
                dve.tensor_copy(dt_all[:, t, :], bank[:, 7, 256:272]).then_inc(sem["p_evV"], 1)

            with dve.Fori(0, DEPTH) as l:
                nl = l + 1
                dve.wait_ge(sem["a_vecT"], by("a_vecT", nl))
                dve.tensor_copy(vecs[:, :], bank[:, 0, 0:88]).then_inc(sem["a_vecs"], 1)
                dve.wait_ge(sem["a_used"], by("a_used", nl))
                dve.wait_ge(sem["a_vecs"], by("a_vecs", nl))
                tt(mod[:, :, :], bank[:, 1, 0:96].rearrange("p (a b) -> p a b", b=2), bc(vecs[:, 16:64], 2), ALU.add).then_inc(sem["a_mod"], 1)
                dve.wait_ge(sem["a_mod"], by("a_mod", nl))
                for k0, g0, sc, sh in ((0, 0, scale1, shift1), (24, 8, scale2, shift2)):
                    for tl, w, cd in ((0, 1, 0), (1, NT - 1, 1)):
                        def over(v):
                            return v.unsqueeze(1).broadcast_to([P, w, DC])
                        dve.scalar_tensor_tensor(out=sc[:, tl:tl + w, :], in0=over(mod[:, k0 + 8:k0 + 16, cd]), scalar=1.0,
                                                 in1=over(vecs[:, g0:g0 + 8]), op0=ALU.add, op1=ALU.mult)
                        last = dve.tensor_copy(sh[:, tl:tl + w, :], over(mod[:, k0:k0 + 8, cd]))
                last.then_inc(sem["a_scales"], 1)
                for i in range(4):
                    if i:
                        dve.wait_ge(sem["a_rowmm"], by("a_rowmm", nl, i))
                    k0 = 16 if i < 2 else 40
                    tt(a_diag, ident.unsqueeze(1).broadcast_to([P, DC, P]), bc(mod[:, k0:k0 + 8, i % 2], P)).then_inc(sem["a_diag"], 1)
                barrier(dve, l, 1)
                norm_x(l * NT + 1)
                with dve.Fori(0, NT - 1) as t:
                    turn_p(l, t, l * NT + t + 1, True)
                turn_p(l, NT - 1, l * NT + NT, False)
                barrier(dve, l, 2)

                flat = [l_s[:, i].rearrange("p a b -> p (a b)") for i in range(4)]
                dts = dt_all[:, :, :].rearrange("p a b -> p (a b)")
                bias = head_row[:, 0:16].unsqueeze(1).broadcast_to([P, NT, 16])
                tt(dt_all[:, :, :], dt_all[:, :, :], bias, ALU.add).then_inc(sem["l_de"], 1)
                dve.wait_ge(sem["l_de"], by("l_de", nl, 1))
                dve.scalar_tensor_tensor(out=flat[1], in0=dts, scalar=-1.0, in1=dts, op0=ALU.mult, op1=ALU.min).then_inc(sem["l_de"], 1)
                dve.wait_ge(act_once, (l + 1) * 2 + 3)
                dve.sem_inc(tick, 1)
                ln = Link(dve, "l_dt", nl)
                ln(dve.tensor_scalar(flat[0], flat[1], 2.0, None, ALU.add))
                ln(dve.reciprocal(flat[0], flat[0]))
                ln(tt(flat[0], flat[0], flat[1]))
                ln(tt(flat[3], flat[0], flat[0]))
                ln(dve.tensor_scalar(flat[2], flat[3], 1.0 / 17, None, ALU.mult))
                for odd in (15, 13, 11, 9, 7, 5, 3):
                    ln(dve.scalar_tensor_tensor(out=flat[2], in0=flat[2], scalar=1.0 / odd, in1=flat[3], op0=ALU.add, op1=ALU.mult))
                ln(dve.scalar_tensor_tensor(out=flat[2], in0=flat[2], scalar=1.0, in1=flat[0], op0=ALU.add, op1=ALU.mult))
                ln(dve.tensor_scalar(dts, dts, 0.0, None, ALU.max))
                ln(dve.scalar_tensor_tensor(out=dts, in0=flat[2], scalar=2.0, in1=dts, op0=ALU.mult, op1=ALU.add))
                ln(dve.scalar_tensor_tensor(out=la_all[:, :, :], in0=dt_all[:, :, :], scalar=-1.0,
                                            in1=small[:, 40:56].unsqueeze(1).broadcast_to([P, NT, 16]), op0=ALU.mult, op1=ALU.mult), last=True)
                dve.wait_ge(sem["l_bex"], by("l_bex", nl))
                tt(dtee[:, :, :], dt_all[:, :, :], l_s[:, 2])
                for d in range(2):
                    for g in range(2):
                        dve.tensor_copy(dec[rows(g), :, d, 4:8], etot[rows(g), :, 8 * d + 4 * g:8 * d + 4 * g + 4])
                    last = dve.tensor_copy(dec[:, :, d, 2:4], cst[:, C_RT + 2 * d:C_RT + 2 * d + 2].unsqueeze(1).broadcast_to([P, NT, 2]))
                last.then_inc(sem["l_dec0"], 1)

                with dve.Fori(0, NT) as t:
                    n = l * NT + t + 1
                    dve.wait_ge(sem["l_T"], by("l_T", n, 2))
                    dve.wait_ge(sem["l_xl"], before("l_xl", n))
                    dve.wait_ge(sem["l_lv"], before("l_lv", n))
                    dve.tensor_copy(l_k[:, 1], bank[:, 1, 0:256].rearrange("p (a b) -> p a b", a=2)).then_inc(sem["l_ev2"], 1)
                    dve.wait_ge(sem["l_ev1"], by("l_ev1", n))
                    dve.wait_ge(sem["l_ev2"], by("l_ev2", n))
                    tt(l_kk, l_k[:, 0], l_k[:, 1], ALU.add).then_inc(sem["l_kk"], 1)
                    dve.wait_ge(sem["l_T"], by("l_T", n, 3))
                    dve.tensor_copy(l_rqk, bank[:, 4, :].rearrange("p (a b) -> p a b", a=4)).then_inc(sem["l_ev4"], 1)
                    dve.wait_ge(sem["l_T"], by("l_T", n, 4))
                    dve.wait_ge(sem["l_dS"], before("l_dS", n))
                    dve.tensor_copy(l_tm[:, 4, :], bank[:, 3, 0:P]).then_inc(sem["l_ev3b"], 1)
                    dve.wait_ge(sem["l_RA"], by("l_RA", n))
                    dve.wait_ge(sem["l_at"], before("l_at", n))
                    for g in range(2):
                        last = tt(l_bc[:, :, g, :], bank[:, 5 - g, 0:P].unsqueeze(1).broadcast_to([P, 2, P]), tri[:, LE:LE + 2, :])
                    last.then_inc(sem["l_bcm"], 1)
                    dve.wait_ge(sem["l_oR"], before("l_oR", n))
                    for h in range(2):
                        last = tt(l_ar[:, h:4:2, :], bank[:, 5 - h, 256:512].rearrange("p (a b) -> p a b", a=2),
                                  cst[:, C_RM:C_RM + 512].rearrange("p (a b) -> p a b", a=4)[:, h:4:2, :])
                    last.then_inc(sem["l_ar"], 1)
                    for d in range(2):
                        dve.wait_ge(sem["l_ex"], by("l_ex", n, 2 * d + 2))
                        for level in range(NL):
                            for second in range(2):
                                src = l_q if (second == 1) == (d == 0) else l_k[:, d]
                                last = tt(halves(l_xl[:, d, :, level, :], level, second), halves(l_ex[:, d, :, level, :], level, second),
                                          halves(src, level, second))
                        last.then_inc(sem["l_xl"], 1)
                    dve.wait_ge(sem["l_qst"], before("l_qst", n))
                    for d in range(2):
                        tt(l_qe[:, 4 * d:4 * d + 2, :], l_ex[:, d, :, 7, :], l_q)
                        tt(l_qe[:, 4 * d + 2:4 * d + 4, :], l_rqk[:, 0:2, :],
                           cst[:, C_RQ + d * 256:C_RQ + (d + 1) * 256].rearrange("p (a b) -> p a b", a=2))
                        dve.tensor_copy(dec[:, t, d, 0:2], l_ex[:, d, :, 7, P - 1 if d == 0 else 0]).then_inc(sem["l_qe"], 1)
                    dve.wait_ge(sem["l_ee"], by("l_ee", n))
                    tt(l_kb, l_in[:, J_K:J_K + 512], l_ee).then_inc(sem["l_kb"], 1)
                    dve.wait_ge(sem["l_bcm"], by("l_bcm", n))
                    for d in range(2):
                        dve.wait_ge(sem["l_pe"], by("l_pe", n, d + 1))
                        v = l_at[:, d].rearrange("p (g h) t -> p g h t", g=2)
                        tt(v, v, l_bc[:, d].unsqueeze(2).broadcast_to([P, 2, 4, P])).then_inc(sem["l_at"], 1)
                    for i in range(8):
                        dve.wait_ge(sem["l_lv"], by("l_lv", n, i + 1))
                        b0 = 6 if i % 2 == 0 else 0
                        src = bank[:, b0:b0 + 2, 0:256].rearrange("p h (q t) -> p h q t", q=2)
                        dst = l_ah.rearrange("p (q h) t -> p h q t", h=2)
                        if i == 0:
                            dve.wait_ge(sem["l_oR"], before("l_oR", n))
                            for h in range(2):
                                last = tt(dst[:, h], src[:, h], ident.unsqueeze(1).broadcast_to([P, 2, P]))
                            last.then_inc(sem["l_lc"], 1)
                        else:
                            dve.wait_ge(sem["l_lc"], by("l_lc", n, i))
                            dve.sem_inc(tick, 1)
                            for h in range(2):
                                last = dve.copy_predicated(dst[:, h], lev_mask[:, i - 1, :].unsqueeze(1).broadcast_to([P, 2, P]), src[:, h])
                            last.then_inc(sem["l_lc"], 1)
                    dve.wait_ge(sem["l_oS"], by("l_oS", n))
                    dve.wait_ge(sem["l_sk"], by("l_sk", n))
                    dve.wait_ge(sem["l_ost"], before("l_ost", n))
                    tt(l_o[:, 256:768], bank[:, 5, :], l_sk, ALU.add).then_inc(sem["l_oeS"], 1)
                    for d in range(2):
                        dve.wait_ge(sem["l_dS"], by("l_dS", n, 3 + d))
                        dve.sem_inc(tick, 1)
                        for g in range(2):
                            last = dve.tensor_copy((st_f[:, t + 1] if d == 0 else st_b[:, t])[rows(g), 4:8, :], bank[rows(g), 2 + d, 256 * g:256 * g + 256].rearrange("p (a b) -> p a b", a=4))
                        last.then_inc(sem["l_incD"], 1)
                barrier(dve, l, 3)

                dve.memset(st_f[:, 0], 0.0)
                dve.memset(r_af, 0.0).then_inc(sem["s_init"], 1)
                dve.wait_ge(sem["s_in"], by("s_in", nl))
                ln = Link(dve, "s_fs", nl)
                for tile in range(1, NT - 1):
                    step_f = r_t1.rearrange("p (a b) -> p a b", b=HD)
                    ln(tt(step_f, st_f[:, tile], bc(dec[:, tile, 0, :], HD)))
                    ln(tt(st_f[:, tile + 1], st_f[:, tile + 1], step_f, ALU.add), last=(tile == NT - 2))
                with dve.Fori(0, NT) as t:
                    n = l * NT + t + 1
                    dve.wait_ge(sem["r_i1"], by("r_i1", n))
                    ln = Link(dve, "r_o", n)
                    kv = r_o.rearrange("p (m q h v) -> p m q h v", m=4, q=2, h=2)[:, 0:4:3]
                    for h in range(2):
                        v = kv[:, :, :, h, :]
                        ln(tt(v, v, bank[:, 7 * h, 0:256].rearrange("p (m q v) -> p m q v", m=2, q=2), ALU.add))
                    dve.wait_ge(sem["r_i2"], by("r_i2", n))
                    for g in range(2):
                        ln(tt(r_t.rearrange("p d (g a b) -> p d g a b", g=2, b=HD)[:, :, g], bank[:, 1 + g, :].rearrange("p (d a b) -> p d a b", d=2, b=HD),
                              bc(eb_all[:, t, :].rearrange("p (d g a) -> p d g a", d=2, g=2)[:, :, g, :], HD)))
                    o_s, o_r = r_o[:, 256:768], r_o[:, 768:1024].rearrange("p (a b) -> p a b", b=HD)
                    ln(tt(o_s, o_s, r_t1, ALU.add))
                    ln(tt(o_s, o_s, r_t2, ALU.add))
                    ln(tt(o_s, o_s, r_g[:, 0:512]))
                    ln(dve.tensor_reduce(small[:, 4:8], o_r, AX, ALU.add))
                    ln(dve.tensor_scalar(small[:, 4:8], small[:, 4:8], -1.0 / HD, None, ALU.mult))
                    ln(tt(o_r, o_r, bc(small[:, 4:8], HD), ALU.add), last=True)
                    dve.wait_ge(sem["r_sq"], by("r_sq", n))
                    dve.wait_ge(sem["r_var"], before("r_var", n))
                    dve.tensor_reduce(small[:, 32:48], r_sq.rearrange("p (a b) -> p a b", b=HD), AX, ALU.add).then_inc(sem["r_red"], 1)
                    dve.wait_ge(sem["r_red"], by("r_red", n, 1))
                    dve.tensor_reduce(small[:, 8:9], small[:, 36:44], AX, ALU.add).then_inc(sem["r_red"], 1)
                    dve.wait_ge(sem["r_rs"], by("r_rs", n))
                    dve.wait_ge(sem["r_yT"], before("r_yT", n))
                    v = r_y.rearrange("p (a b) -> p a b", b=HD)
                    tt(v, r_o.rearrange("p (a b) -> p a b", b=HD), bc(small[:, 48:64], HD)).then_inc(sem["r_y"], 1)
                    dve.wait_ge(sem["r_y"], by("r_y", n, 1))
                    dve.wait_ge(sem["r_gg"], by("r_gg", n))
                    tt(r_y, r_y, r_gg).then_inc(sem["r_y"], 1)
                    dve.wait_ge(sem["r_x1"], before("r_x1", n))
                    for half in range(2):
                        dve.wait_ge(sem["r_out"], by("r_out", n, half + 1))
                        tt(r_gy[:, half * 512:(half + 1) * 512], bank[:, 5 + half, :],
                           gate_row[:, 0, (t + 7) // 8, half * 512:(half + 1) * 512]).then_inc(sem["r_gy"], 1)
                    dve.wait_ge(sem["r_rs2"], by("r_rs2", n))
                    dve.wait_ge(sem["r_xT"], before("r_xT", n))
                    dve.wait_ge(sem["r_nst"], before("r_nst", n))
                    dve.tensor_scalar(r_xn, r_x1, small[:, 2:3], None, ALU.mult).then_inc(sem["r_xn"], 1)
                    for ch in range(DC):
                        if ch % 4 == 0:
                            dve.wait_ge(sem["r_xT"], by("r_xT", n, ch // 4 + 1))
                            dve.wait_ge(sem["r_lg"], before("r_lg", n))
                        last = dve.tensor_scalar(r_ht[:, ch, :], bank[:, 7 if ch < 4 else 3, (ch % 4) * P:(ch % 4 + 1) * P],
                                                 scale2[:, t, ch:ch + 1], shift2[:, t, ch:ch + 1], ALU.mult, ALU.add)
                    last.then_inc(sem["r_ht"], 1)
                    dve.wait_ge(sem["r_lg"], by("r_lg", n))
                    dve.tensor_reduce(small[:, 12:13], bank[:, 4, 0:NE], AX, ALU.max).then_inc(sem["r_mx"], 1)
                    dve.wait_ge(sem["r_mx"], by("r_mx", n, 1))
                    dve.tensor_scalar(small[:, 13:14], small[:, 12:13], -1.0, None, ALU.mult).then_inc(sem["r_mx"], 1)
                    dve.wait_ge(sem["r_e"], by("r_e", n))
                    dve.reciprocal(small[:, 15:16], small[:, 14:15]).then_inc(sem["r_ri"], 1)
                    dve.wait_ge(sem["r_ri"], by("r_ri", n))
                    dve.wait_ge(sem["r_aT"], before("r_aT", n))
                    dve.tensor_scalar(r_af[:, 0:NE], small[:, 16:32], small[:, 15:16], None, ALU.mult).then_inc(sem["r_af"], 1)
                barrier(dve, l, 4)

                dve.memset(k_t, 0.0).then_inc(sem["k_z"], 1)
                dve.memset(e_xp, 0.0)
                dve.wait_ge(sem["k_z"], by("k_z", nl))
                dve.sem_inc(tick, 1)

                def round_(src, kind, r, n):
                    ln = Link(dve, "k_r", n)
                    ln.hold(dve.max(k_m8[0:NE, :], src))
                    ln.hold(dve.max_index(k_i8[0:NE, :].bitcast(U32), k_m8[0:NE, :], src))
                    ln.hold(dve.match_replace(src, k_m8[0:NE, :], src, -1.0))
                    ln.hold(dve.tensor_copy(k_t[0:NE, kind, bass.ds(r * 8, 8)], k_i8[0:NE, :].bitcast(U32)))
                    ln.hold(dve.tensor_copy(k_t[0:NE, kind + 1, bass.ds(r * 8, 8)], k_m8[0:NE, :]))

                ROUNDS_S, ROUNDS_P = CAP_S // 8, CAP_P // 8
                with dve.Fori(0, ROUNDS_S) as r:
                    round_(aff_t[:, SEQ:T], 0, r, l * (ROUNDS_S + ROUNDS_P) + r + 1)
                for r in range(ROUNDS_P):
                    round_(aff_t[:, 0:SEQ], 2, r, l * (ROUNDS_S + ROUNDS_P) + ROUNDS_S + r + 1)
                dve.tensor_copy(k_m8[0:NE, :], k_m8[0:NE, :]).then_inc(sem["k_done"], 1)
                dve.wait_ge(sem["k_T"], by("k_T", nl))
                dve.tensor_scalar(k_idx[:, 0, :].bitcast(U32), bank[:, 0, 0:NE], float(SEQ), None, ALU.add)
                dve.tensor_copy(k_idx[0:CAP_P, 1, :].bitcast(U32), bank[0:CAP_P, 0, 256:256 + NE])
                dve.tensor_copy(k_val[:, 0, :], bank[:, 0, P:P + NE])
                dve.tensor_copy(k_val[0:CAP_P, 1, :], bank[0:CAP_P, 0, 384:384 + NE]).then_inc(sem["k_ix"], 1)
                barrier(dve, l, 5)
                with dve.Fori(0, NE) as e:
                    n = l * NE + e + 1
                    dve.wait_ge(sem["e_y"], before("e_y", n))
                    dve.sem_inc(tick, 1)
                    dve.tensor_copy(e_g[:, 0:1], k_val[:, 0, bass.ds(e, 1)])
                    dve.tensor_copy(e_g[0:CAP_P, 1:2], k_val[0:CAP_P, 1, bass.ds(e, 1)]).then_inc(sem["e_gc"], 1)
                    dve.wait_ge(sem["e_xT"], by("e_xT", n, 1))
                    dve.wait_ge(sem["e_gu"], before("e_gu", n))
                    for ch in range(4):
                        dve.tensor_scalar(e_xt[:, ch, 0:CAP_S], bank[:, 0, ch * P:(ch + 1) * P], scale2[:, 1, ch:ch + 1],
                                          shift2[:, 1, ch:ch + 1], ALU.mult, ALU.add)
                    for q in range(2):
                        dve.wait_ge(sem["e_xT"], by("e_xT", n, 3 + q))
                        last = tt(e_xt[:, 4 * q:4 * q + 4, CAP_S:], bank[:, 2 + q, :].rearrange("p (a b) -> p a b", a=4)[:, :, 0:CAP_P],
                                  bc(scale2[:, 0, 4 * q:4 * q + 4], CAP_P))
                    last.then_inc(sem["e_xtd"], 1)
                    dve.wait_ge(sem["e_xtd"], by("e_xtd", n, 1))
                    tt(e_xt[:, :, CAP_S:], e_xt[:, :, CAP_S:], bc(shift2[:, 0, :], CAP_P), ALU.add).then_inc(sem["e_xtd"], 1)
                    for f in range(FC):
                        dve.wait_ge(sem["e_sg"], by("e_sg", n, f + 1))
                        dve.wait_ge(sem["e_dn"], before("e_dn", n))
                        tt(e_h[:, f, :], bank[:, 4 + f, 256:256 + CAP_S + CAP_P], e_sg[:, f, :]).then_inc(sem["e_h"], 1)
                    dve.wait_ge(sem["e_gc"], by("e_gc", n))
                    dve.wait_ge(sem["e_jc"], by("e_jc", n))
                    for q in range(4):
                        dve.wait_ge(sem["e_dn"], by("e_dn", n, q + 1))
                        m, dst = (CAP_S, e_y) if q < 2 else (CAP_P, e_yp)
                        cols = slice((q % 2) * 512, (q % 2 + 1) * 512)
                        dve.scalar_tensor_tensor(out=dst[0:m, cols], in0=bank[0:m, q, :], scalar=e_g[0:m, q // 2:q // 2 + 1],
                                                 in1=gate_row[0:m, 1, 1 - q // 2, cols], op0=ALU.mult, op1=ALU.mult).then_inc(sem["e_y"], 1)
                barrier(dve, l, 6)
            dve.wait_ge(final_g_in, 16)
            for t in range(NT):
                n = DEPTH * NT + t + 1
                dve.wait_ge(sem["p_rstd"], by("p_rstd", n))
                if t:
                    dve.wait_ge(sem["p_u_st"], by("p_u_st", n - 1))
                dve.tensor_scalar(f_y, f_x, small[:, 2:3], None, ALU.mult).then_inc(sem["p_xn"], 1)
                dve.wait_ge(sem["p_xn"], by("p_xn", n))
                tt(f_y, f_y, f_g).then_inc(sem["p_f1"], 1)

        @block.gpsimd
        def _(pool):
            def tt(out, a, b, op=ALU.mult):
                return pool.tensor_tensor(out, a, b, op)

            def bc(v, n):
                return v.unsqueeze(len(v.shape)).broadcast_to(list(v.shape) + [n])

            for name in COUNTS:
                if name not in SWDGE:
                    pool.sem_inc(sem[name], 1)
            pool.memset(minus_half[:, :], -0.5).then_inc(pool_once, 1)
            pool.wait_ge(pool_once, 1)
            pool.sem_inc(primed, 1)
            pool.wait_ge(const_in, 32)

            def rstd(src, mid, out, ss, rv, rs, used, n):
                pool.wait_ge(sem[ss], by(ss, n))
                pool.sem_inc(tick, 1)
                pool.tensor_scalar(small[:, mid:mid + 1], small[:, src:src + 1], 1.0 / D, EPS, ALU.mult, ALU.add).then_inc(sem[rv], 1)
                pool.wait_ge(sem[rv], by(rv, n))
                pool.wait_ge(sem[used], before(used, n))
                pool.sem_inc(tick, 1)
                tt(small[:, out:out + 1], small[:, mid:mid + 1], minus_half[:, 0:1], ALU.pow).then_inc(sem[rs], 1)

            with pool.Fori(0, DEPTH) as l:
                nl = l + 1
                barrier(pool, l, 1)
                with pool.Fori(0, NT) as t:
                    rstd(0, 1, 2, "p_ss", "p_rv", "p_rstd", "p_xn", l * NT + t + 1)
                barrier(pool, l, 2)
                pool.wait_ge(sem["l_dec0"], by("l_dec0", nl))
                pool.sem_inc(tick, 1)
                with pool.Fori(0, NT) as t:
                    n = l * NT + t + 1
                    pool.wait_ge(sem["l_pm"], before("l_pm", n))
                    pool.sem_inc(tick, 1)
                    for d in range(2):
                        last = tt(l_pr[:, d], tri[:, LE + d, :].unsqueeze(1).broadcast_to([P, 8, P]), bc(la_all[:, t, 8 * d:8 * d + 8], P))
                    last.then_inc(sem["l_prf"], 1)
                    pool.wait_ge(sem["l_in"], by("l_in", n))
                    pool.sem_inc(tick, 1)
                    ln = Link(pool, "l_rope", n)
                    x = l_in[:, J_RQ:J_RQ + 512].rearrange("p (j m i) -> p j m i", j=2, i=32)
                    for dst, c0 in ((l_r1, C_COS), (l_r2, C_SIN)):
                        w = cst[:, bass.ds(c0 + t * 64, 64)].rearrange("p (j i) -> p j i", j=2).unsqueeze(2).broadcast_to([P, 2, 8, 32])
                        ln.hold(tt(dst.rearrange("p (j m i) -> p j m i", j=2, i=32), x, w))
                    v1, v2, vo = (v.rearrange("p (m two i) -> p m two i", two=2, i=32) for v in (l_r1, l_r2, l_rot))
                    pool.wait_ge(sem["l_T"], before("l_T", n))
                    pool.sem_inc(tick, 1)
                    ln.hold(tt(vo[:, :, 0, :], v1[:, :, 0, :], v2[:, :, 1, :], ALU.subtract))
                    ln(tt(vo[:, :, 1, :], v2[:, :, 0, :], v1[:, :, 1, :], ALU.add), last=True)
                    pool.wait_ge(sem["l_uin"], by("l_uin", n))
                    pool.sem_inc(tick, 1)
                    edge = l_u[:, :, 0:P + 2:P + 1]
                    tt(edge, edge, cst[:, bass.ds(C_HALO + t * 2, 2)].unsqueeze(1).broadcast_to([P, UC, 2])).then_inc(sem["l_halo"], 1)
                    pool.wait_ge(sem["l_halo"], by("l_halo", n))
                    pool.wait_ge(sem["l_T"], before("l_T", n))
                    pool.wait_ge(sem["l_BC"], before("l_BC", n))
                    pool.sem_inc(tick, 1)
                    pool.wait_ge(sem["l_qc"], before("l_qc", n))
                    pool.sem_inc(tick, 1)
                    ln = Link(pool, "l_cv", n)
                    ln(tt(l_c, l_u[:, :, 0:P], bc(vecs[:, 64:70], P)))
                    ln(tt(l_ct, l_u[:, :, 1:P + 1], bc(vecs[:, 70:76], P)))
                    ln(tt(l_c, l_c, l_ct, ALU.add))
                    ln(tt(l_ct, l_u[:, :, 2:P + 2], bc(vecs[:, 76:82], P)))
                    ln(tt(l_c, l_c, l_ct, ALU.add), last=True)
                    pool.wait_ge(sem["l_rope"], by("l_rope", n))
                    pool.wait_ge(sem["l_dS"], before("l_dS", n))
                    pool.sem_inc(tick, 1)
                    for d in range(2):
                        last = tt(l_rkb[:, d * 256:(d + 1) * 256].rearrange("p (a b) -> p a b", b=HD),
                                  l_rot[:, 256:512].rearrange("p (a b) -> p a b", b=HD), bc(cst[:, C_RK + 4 * d:C_RK + 4 * d + 4], HD))
                    last.then_inc(sem["l_rkb"], 1)
                    pool.wait_ge(sem["l_ev3"], by("l_ev3", n))
                    pool.sem_inc(tick, 1)
                    pool.wait_ge(sem["l_oS"], before("l_oS", n))
                    pool.sem_inc(tick, 1)
                    xs = l_tm[:, 0:4, :].rearrange("p a (h b) -> p (a h) b", b=HD)
                    for d in range(2):
                        tt(l_v1[:, d].rearrange("p (a b) -> p a b", b=HD), xs, bc(dt_all[:, t, 8 * d:8 * d + 8], HD))
                        last = tt(l_v2[:, d].rearrange("p (a b) -> p a b", b=HD), xs, bc(dtee[:, t, 8 * d:8 * d + 8], HD))
                    last.then_inc(sem["l_v"], 1)
                    pool.wait_ge(sem["l_oeS"], before("l_oeS", n))
                    pool.sem_inc(tick, 1)
                    tt(l_sk.rearrange("p (a b) -> p a b", b=HD), xs, bc(head_row[:, 32:40], HD)).then_inc(sem["l_sk"], 1)
                    pool.wait_ge(sem["l_silu"], by("l_silu", n))
                    pool.wait_ge(sem["l_qst"], before("l_qst", n))
                    pool.sem_inc(tick, 1)
                    pool.tensor_copy(l_qe[:, 8, :], l_c[:, 5, :]).then_inc(sem["l_qc"], 1)
                barrier(pool, l, 3)
                pool.wait_ge(sem["s_init"], by("s_init", nl))
                pool.wait_ge(sem["gain_in"], by("gain_in", nl))
                pool.wait_ge(sem["s_in"], by("s_in", nl))
                pool.sem_inc(tick, 1)
                pool.tensor_copy(r_gg[:, 256:768], gain_row[:, 256:768]).then_inc(sem["r_gg0"], 1)
                ln = Link(pool, "s_bs", nl)
                for tile in range(NT - 1, 1, -1):
                    step_b = r_t2.rearrange("p (a b) -> p a b", b=HD)
                    ln(tt(step_b, st_b[:, tile + 1], bc(dec[:, tile, 1, :], HD)))
                    ln(tt(st_b[:, tile], st_b[:, tile], step_b, ALU.add), last=(tile == 2))
                pool.memset(st_b[:, 1], 0.0).then_inc(sem["r_gg0"], 1)
                pool.wait_ge(sem["s_bs"], by("s_bs", nl))
                pool.wait_ge(sem["s_fs"], by("s_fs", nl))
                pool.sem_inc(tick, 1)
                pool.wait_ge(sem["r_gg0"], by("r_gg0", nl))
                pool.sem_inc(tick, 1)
                with pool.Fori(0, NT) as t:
                    n = l * NT + t + 1
                    pool.wait_ge(sem["r_i2"], before("r_i2", n))
                    pool.sem_inc(tick, 1)
                    pool.tensor_copy(r_st[:, 0], st_f[:, t])
                    pool.tensor_copy(r_st[:, 1], st_b[:, t + 1]).then_inc(sem["r_st"], 1)
                    pool.wait_ge(sem["r_in"], by("r_in", n))
                    pool.wait_ge(sem["r_y"], before("r_y", n))
                    pool.sem_inc(tick, 1)
                    tt(r_gg[:, 0:256], r_g[:, 512:768], gain_row[:, 0:256])
                    tt(r_gg[:, 768:1024], r_g[:, 768:1024], gain_row[:, 768:1024]).then_inc(sem["r_gg"], 1)
                    pool.wait_ge(sem["r_red"], by("r_red", n))
                    pool.sem_inc(tick, 1)
                    for dst, src, m in ((small[:, 32:36], small[:, 32:36], HD), (small[:, 36:44], small[:, 8:9].broadcast_to([P, 8]), SSDW),
                                        (small[:, 44:48], small[:, 44:48], HD)):
                        last = pool.tensor_scalar(dst, src, 1.0 / m, EPS, ALU.mult, ALU.add)
                    last.then_inc(sem["r_var"], 1)
                    pool.wait_ge(sem["r_var"], by("r_var", n))
                    pool.wait_ge(sem["r_y"], before("r_y", n))
                    pool.sem_inc(tick, 1)
                    tt(small[:, 48:64], small[:, 32:48], minus_half[:, :], ALU.pow).then_inc(sem["r_rs"], 1)
                    pool.wait_ge(sem["r_gy"], by("r_gy", n))
                    pool.wait_ge(sem["r_x_in"], by("r_x_in", n))
                    pool.wait_ge(sem["r_xst"], before("r_xst", n))
                    pool.wait_ge(sem["r_xn"], before("r_xn", n))
                    pool.wait_ge(sem["r_ss"], before("r_ss", n))
                    pool.sem_inc(tick, 1)
                    tt(r_x1, r_x, r_gy, ALU.add).then_inc(sem["r_x1"], 1)
                    rstd(0, 1, 2, "r_ss", "r_rv2", "r_rs2", "r_xn", n)
                barrier(pool, l, 4)
                barrier(pool, l, 5)

                def gather(e, n):
                    if not isinstance(e, int):
                        pool.wait_ge(sem["e_xg"], by("e_xg", n - 1))
                        pool.sem_inc(tick, 1)
                    pool.tensor_copy(e_i[:, 0:1].bitcast(U32), k_idx[:, 0, bass.ds(e, 1)].bitcast(U32))
                    pool.tensor_copy(e_i[0:CAP_P, 1:2].bitcast(U32), k_idx[0:CAP_P, 1, bass.ds(e, 1)].bitcast(U32)).then_inc(sem["e_ic"], 1)
                    pool.wait_ge(sem["e_ic"], by("e_ic", n))
                    pool.wait_ge(sem["e_xT"], before("e_xT", n))
                    pool.sem_inc(tick, 1)
                    pool.indirect_dma_start(e_x, None, xn_d, bass.IndirectOffsetOnAxis(ap=e_i[:, 0:1].bitcast(U32), axis=0)).then_inc(sem["e_xg"], 16)
                    pool.indirect_dma_start(e_xp[0:CAP_P, :], None, xn_d, bass.IndirectOffsetOnAxis(ap=e_i[0:CAP_P, 1:2].bitcast(U32), axis=0))\
                        .then_inc(sem["e_xg"], 16)

                def scatter(e, n):
                    if not isinstance(e, int) or e > 0:
                        pool.wait_ge(sem["e_sc"], by("e_sc", n - 1))
                        pool.wait_ge(sem["e_scp"], by("e_scp", n - 1))
                        pool.sem_inc(tick, 1)
                    pool.tensor_copy(k_j[:, 0:1].bitcast(U32), k_idx[:, 0, bass.ds(e, 1)].bitcast(U32))
                    pool.tensor_copy(k_j[0:CAP_P, 1:2].bitcast(U32), k_idx[0:CAP_P, 1, bass.ds(e, 1)].bitcast(U32)).then_inc(sem["e_jc"], 1)
                    pool.wait_ge(sem["e_jc"], by("e_jc", n))
                    pool.wait_ge(sem["e_y"], by("e_y", n))
                    pool.sem_inc(tick, 1)
                    pool.indirect_dma_start(x_d, bass.IndirectOffsetOnAxis(ap=k_j[:, 0:1].bitcast(U32), axis=0), e_y, None, compute_op=ALU.add)\
                        .then_inc(sem["e_sc"], 16)
                    pool.indirect_dma_start(x_d, bass.IndirectOffsetOnAxis(ap=k_j[0:CAP_P, 1:2].bitcast(U32), axis=0), e_yp[0:CAP_P, :], None, compute_op=ALU.add)\
                        .then_inc(sem["e_scp"], 16)

                gather(0, l * NE + 1)
                pool.wait_ge(sem["e_xg"], by("e_xg", l * NE + 1))
                pool.sem_inc(tick, 1)
                gather(1, l * NE + 2)
                scatter(0, l * NE + 1)
                with pool.Fori(1, NE - 1) as e:
                    n = l * NE + e + 1
                    gather(e + 1, n + 1)
                    scatter(e, n)
                scatter(NE - 1, l * NE + NE)
                pool.wait_ge(sem["e_sc"], by("e_sc", l * NE + NE))
                pool.wait_ge(sem["e_scp"], by("e_scp", l * NE + NE))
                pool.sem_inc(tick, 1)
                barrier(pool, l, 6)
            for t in range(NT):
                rstd(0, 1, 2, "p_ss", "p_rv", "p_rstd", "p_xn", DEPTH * NT + t + 1)


_INS = ["x_prompt", "x_sample", "state_hgrn", "state_ssd", "state_ret", "c", "c_ctx", "norm1_g", "norm2_g", "final_g",
        "w_ada", "b_ada", "w_in", "w_out", "hg_lb", "hg_norm_g", "ssd_conv_w", "ssd_conv_b", "ssd_dt_bias", "ssd_a_log",
        "ssd_d", "ssd_norm_g", "ret_norm_g", "w_router", "w_gate", "w_up", "w_down"]
_OUTS = [(1, SEQ, D), (1, DEC, D), (1, DEPTH, 2, 4, 64, 64), (1, DEPTH, 2, 8, 64, 64), (1, DEPTH, 2, 4, 64, 64)]


def kernel(**inputs):
    import numpy as _np
    import concourse.bacc as _bacc
    from concourse import mybir as _mybir
    from concourse.bass_utils import run_bass_kernel_spmd as _run

    nc = _bacc.Bacc("TRN2", target_bir_lowering=False, num_devices=1)
    arrays, args = {}, []
    const_f, const_m = shape_constants()
    given = [(name, _np.ascontiguousarray(inputs[name])) for name in _INS] + [("const_f", const_f), ("const_m", const_m)]
    for name, a in given:
        arrays[f"in_{name}_dram"] = a
        args.append(nc.dram_tensor(f"in_{name}_dram", a.shape, _mybir.dt.from_np(a.dtype), kind="ExternalInput").ap())
    for i, shape in enumerate(_OUTS):
        args.append(nc.dram_tensor(f"out_{i}_dram", shape, _mybir.dt.float32, kind="ExternalOutput").ap())
    trunk(nc, *args)
    r = _run(nc, [arrays], core_ids=[0])
    return tuple(r.results[0][f"out_{i}_dram"] for i in range(len(_OUTS)))
```

```python
import math
from contextlib import ExitStack

import numpy as np

import concourse.bass as bass
from concourse import mybir

F32 = mybir.dt.float32
U8 = mybir.dt.uint8
U32 = mybir.dt.uint32
ALU = mybir.AluOpType
ACT = mybir.ActivationFunctionType
AX = mybir.AxisListType.X

P = 128
D = 1024
DC = D // P
DEPTH = 2
SEQ = 128
DEC = 1024
T = SEQ + DEC
NT = T // P
HD = 64
GRID_W = 64
EPS = 1e-6
HGW, SSDW, RETW = 256, 512, 256
D_IN = 3600
NE = 16
DE = 512
FC = DE // P
CAP_S = 2 * DEC // NE
CAP_P = 2 * SEQ // NE
NL = 7
A_EARLY = 2 * D
M_STEP = 2 * D // (NT - 1)
EARLY = 768 + 512 + 1024

W_Q, W_I, W_F, W_G, W_Z, W_X, W_DT, W_RQ, W_RV, W_RG = 0, 256, 512, 1024, 1280, 1792, 2560, 2576, 3088, 3344
J_Q, J_V, J_F, J_K, J_Z, J_G, J_RQ, J_RV, J_N = 0, 256, 512, 1024, 1536, 2048, 2560, 3072, 3328
UC = 6

C_ID, C_ONE = 0, 128
C_TRI = 256
C_LEV = C_TRI + 4 * P
C_RM = C_LEV + 2 * 8 * P
C_RQ = C_RM + 4 * P
C_RK = C_RQ + 4 * P
C_RT = C_RK + 8
C_COS = C_RT + 4
C_SIN = C_COS + NT * 64
C_HALO = C_SIN + NT * 64
C_N = C_HALO + NT * 2


def shape_constants():
    c = np.zeros((P, C_N), np.float64)
    i = np.arange(P)
    r, t = i[:, None], i[None, :]
    c[:, C_ID:C_ID + P] = np.eye(P)
    c[:, C_ONE:C_ONE + P] = 1
    for j, m in enumerate((r <= t, r >= t, r > t, r < t)):
        c[:, C_TRI + j * P:C_TRI + (j + 1) * P] = m
    masks = np.zeros((P, NL, P), np.float32)
    for lev in range(NL):
        half = P >> (lev + 1)
        mid = t // (2 * half) * 2 * half + half
        f = np.where(t >= mid, (r >= mid) & (r <= t), (r > t) & (r < mid))
        b = np.where(t < mid, (r >= t) & (r < mid), (r >= mid) & (r < t))
        for d, m in enumerate((f, b)):
            o = C_LEV + (d * 8 + lev) * P
            c[:, o:o + P] = m
        masks[:, lev] = (r // (2 * half) == t // (2 * half)) & (r // half != t // half)
    c[:, C_LEV + 7 * P:C_LEV + 8 * P] = r <= t
    c[:, C_LEV + 15 * P:C_LEV + 16 * P] = r >= t
    for d in range(2):
        for h in range(4):
            lg = math.log1p(-(2.0 ** (-5.0 - 0.5 * d - h)))
            c[:, C_RM + h * P:C_RM + (h + 1) * P] += np.exp(lg * np.abs(t - r)) * ((r <= t) if d == 0 else (r >= t))
            rows = slice(64 * (h % 2), 64 * (h % 2) + 64)
            o = C_RQ + (d * 2 + h // 2) * P
            c[rows, o:o + P] = np.exp(lg * (t + 1 if d == 0 else P - t))
            c[:, C_RK + d * 4 + h] = np.exp(lg * (127 - i if d == 0 else i))
            c[rows, C_RT + d * 2 + h // 2] = np.exp(lg * P)
    nf = HD // 4
    inv = 10000.0 ** (-np.arange(nf) / nf)
    for tile in range(NT):
        tok = np.arange(P) + (tile - 1) * P
        ang = np.concatenate([(tok // GRID_W)[:, None] * inv, (tok % GRID_W)[:, None] * inv], 1)
        co, si = (np.cos(ang), np.sin(ang)) if tile else (np.ones_like(ang), np.zeros_like(ang))
        for j, sc in enumerate((1.0, HD ** -0.5)):
            c[:, C_COS + tile * 64 + j * 32:][:, :32] = co * sc
            c[:, C_SIN + tile * 64 + j * 32:][:, :32] = si * sc
        c[:, C_HALO + tile * 2] = tile > 1
        c[:, C_HALO + tile * 2 + 1] = 0 < tile < NT - 1
    return c.astype(np.float32), masks.reshape(P, NL * P)


class Signal:

    def __init__(self, k, start=1):
        self.k, self.start = k, start

    def by(self, n, i=None):
        return n * self.k + ((i - self.k if i is not None else 0) + self.start)

    def before(self, n):
        return n * self.k + (1 - self.k)


def trunk(nc, x_prompt, x_sample, state_hgrn, state_ssd, state_ret, c, c_ctx, norm1_g, norm2_g, final_g,
          w_ada, b_ada, w_in, w_out, hg_lb, hg_norm_g, ssd_conv_w, ssd_conv_b, ssd_dt_bias, ssd_a_log,
          ssd_d, ssd_norm_g, ret_norm_g, w_router, w_gate, w_up, w_down, const_f, const_m,
          y_prompt, y_sample, new_hg, new_ssd, new_ret):
    ctx = ExitStack()
    with ctx:
        def sb(name, shape, dt=F32):
            return ctx.enter_context(nc.sbuf_tensor(name, shape, dt))

        x_d = nc.dram_tensor("x_d", (T, D), F32).ap()
        xn_d = nc.dram_tensor("xn_d", (T, D), F32).ap()
        proj_d = nc.dram_tensor("proj_d", (T, J_N), F32).ap()
        u_d = nc.dram_tensor("u_d", (UC, P, T + 2), F32).ap()
        o_d = nc.dram_tensor("o_d", (T, D), F32).ap()
        qe_d = nc.dram_tensor("qe_d", (NT, P, 9 * P), F32).ap()

        cst = sb("cst", [P, C_N])
        lev_mask = sb("lev_mask", [P, NL, P], U8)
        ident = cst[:, C_ID:C_ID + P]
        ones = cst[:, C_ONE:C_ONE + P]
        tri = cst[:, C_TRI:C_TRI + 4 * P].rearrange("p (j t) -> p j t", j=4)
        LE, GE, GT, LT = range(4)
        lev = cst[:, C_LEV:C_RM].rearrange("p (d n t) -> p d n t", d=2, n=8)
        minus_half = sb("minus_half", [P, 16])
        lb = sb("lb", [P, DEPTH, 2, 512])
        cond = sb("cond", [P, DC, 2])
        vecs = sb("vecs", [P, 88])
        mod = sb("mod", [P, 48, 2])
        scale1 = sb("scale1", [P, NT, DC])
        shift1 = sb("shift1", [P, NT, DC])
        scale2 = sb("scale2", [P, NT, DC])
        shift2 = sb("shift2", [P, NT, DC])
        gate_row = sb("gate_row", [P, 2, 2, D])
        head_row = sb("head_row", [P, 40])
        w_r = sb("w_r", [P, DC, NE])
        dt_all = sb("dt_all", [P, NT, 16])
        la_all = sb("la_all", [P, NT, 16])
        eb_all = sb("eb_all", [P, NT, 16])
        dtee = sb("dtee", [P, NT, 16])
        etot = sb("etot", [P, NT, 16])
        dec = sb("dec", [P, NT, 2, 8])
        small = sb("small", [P, 64])
        lg_all = sb("lg_all", [P, NT, NE])
        WORK = 39640
        work = sb("work", [P, WORK])

        def carve(start=0):
            at = [start]

            def take(*shape):
                n = int(np.prod(shape))
                assert at[0] + n <= WORK, (at[0], n, WORK)
                v = work[:, at[0]:at[0] + n]
                at[0] += n
                if len(shape) > 1:
                    names = "abcd"[:len(shape)]
                    v = v.rearrange(f"p ({' '.join(names)}) -> p {' '.join(names)}", **dict(zip(names, shape)))
                return v
            return take

        bank = ctx.enter_context(nc.psum_tensor("bank", [P, 8, 512], F32))

        signals, sem = {}, {}

        def by(name, n, i=None):
            return signals[name].by(n, i)

        def before(name, n):
            return signals[name].before(n)

        take = carve(DC * EARLY)
        a_rows = take(P)
        a_slab = take(DC, A_EARLY)
        a_lb = take(DEPTH, 512)
        a_mask = take(NL * P)
        a_lbt = take(4, 512)

        take = carve()
        W_GROUPS = [[(W_X, 768)], [(W_Q, 512)], [(W_Z, 512), (W_G, 256), (W_RG, 256)], [(W_F, 512)], [(W_RQ, 512), (W_RV, 256), (W_DT, 16)]]
        p_w = {c0: take(DC, w) for group in W_GROUPS for c0, w in group}
        p_x = take(D)
        p_xn = take(D)
        p_h = take(DC, P)
        p_out = take(J_N)
        p_sig = take(2, 512)
        p_u = take(UC, P)
        p_slab = take(DC, M_STEP)

        take = carve()
        st_f = take(NT + 1, 8, HD)
        st_b = take(NT + 1, 8, HD)
        l_in = take(J_N)
        l_u = take(UC, P + 2)
        l_c = take(UC, P)
        l_ct = take(UC, P)
        l_g = take(512)
        l_q = take(2, P)
        l_k = take(2, 2, P)
        l_kk = take(2, P)
        l_ex = take(2, 2, 8, P)
        l_xl = take(2, 2, NL, P)
        l_ee = take(512)
        l_kb = take(512)
        l_tm = take(5, P)
        l_rot = take(512)
        l_r1 = take(512)
        l_r2 = take(512)
        l_rqk = take(4, P)
        l_rkb = take(512)
        l_ah = take(4, P)
        l_ar = take(4, P)
        l_bc = take(2, 2, P)
        l_pr = take(2, 8, P)
        l_at = take(2, 8, P)
        l_v1 = take(2, 512)
        l_v2 = take(2, 512)
        l_sk = take(512)
        l_o = l_in[:, J_Z:J_RQ]
        l_qe = take(9, P)
        l_s = take(4, NT, 16)
        l_lt = l_s

        take = carve()
        take(NT + 1, 8, HD)
        take(NT + 1, 8, HD)
        gain_row = take(D)
        r_w = take(DC, D)
        r_st = take(2, 8, HD)
        r_o = take(D)
        r_qe = take(9, P)
        r_g = take(D)
        r_gg = take(D)
        r_x = take(D)
        r_t = take(2, 512)
        r_t1, r_t2 = r_t[:, 0], r_t[:, 1]
        r_sq = take(D)
        r_y = take(D)
        r_yt = take(DC, P)
        r_gy = take(D)
        r_x1 = take(D)
        r_xn = take(D)
        r_ht = take(DC, P)
        r_junk = take(D)
        s_diag = [v.rearrange("p (a b) -> p a b", b=P) for v in (r_gy, r_xn)]

        take = carve()
        aff_t = take(T)[0:NE, :]
        e_wg = [take(DC, DE) for _ in range(2)]
        e_wu = [take(DC, DE) for _ in range(2)]
        e_wd = [take(FC, D) for _ in range(2)]
        e_x = take(D)
        e_xp = take(D)
        e_xt = take(DC, CAP_S + CAP_P)
        e_sg = take(FC, CAP_S + CAP_P)
        e_h = take(FC, CAP_S + CAP_P)
        e_y = take(D)
        e_yp = take(D)
        e_pt = take(DC, CAP_P)
        k_t = take(4, P)
        k_idx = take(2, NE)
        k_val = take(2, NE)
        e_i = take(2)
        e_g = take(2)
        k_m8 = take(8)
        k_i8 = take(8)
        k_j = take(2)
        k_red = take(NT)

        take = carve()
        f_g = take(D)
        f_x = take(D)
        f_y = take(D)
        f_junk = take(D)

        tick = ctx.enter_context(nc.semaphore("tick"))
        phase_end = ctx.enter_context(nc.semaphore("phase_end"))
        NPH = 6

        def barrier(eng, l, ph):
            eng.drain().then_inc(phase_end, 1)
            eng.wait_ge(phase_end, (l * NPH + ph) * 5)
            eng.sem_inc(tick, 1)

        class Link:

            def __init__(self, eng, name, n):
                self.eng, self.name, self.n, self.i = eng, name, n, 0

            def __call__(self, ins, last=False):
                self.i += 1
                ins.then_inc(sem[self.name], 1)
                if last:
                    assert self.i == signals[self.name].k, (self.name, self.i)
                else:
                    self.eng.wait_ge(sem[self.name], by(self.name, self.n, self.i))
                return ins

            def hold(self, ins):
                self(ins)
                self.eng.sem_inc(tick, 1)

        COUNTS = {
            "a_rows_in": 144, "gain_in": 48, "a_slab_in": 16, "a_used": 1, "m_in": 32, "m_used": 2, "a_vecT": 1, "a_vecs": 1, "a_mod": 1,
            "a_scales": 2, "a_diag": 4, "a_rowmm": 4, "a_rowcp": 4,
            "p_x_in": 16, "p_ss": 1, "p_rv": 1, "p_rstd": 1, "p_xn": 1, "p_xT": 1, "p_hTd": 1, "p_hTa": 1,
            "p_mm": 7,
            "p_eva": 5,
            "p_evF": 1, "p_evV": 1,
            "p_f1": 1, "p_f2": 2, "p_proj_st": 16, "p_u_st": 16,
            "l_dt": 16, "l_de": 2, "l_bmm": 1, "l_bex": 1, "l_dec0": 1,
            "l_in": 32, "l_uin": 16, "l_g": 1, "l_halo": 1, "l_cv": 5, "l_silu": 1, "l_rope": 4, "l_rkb": 1,
            "l_v": 1, "l_sk": 1, "l_prf": 1, "l_T": 4, "l_ev1": 1, "l_ev2": 1,
            "l_ev3": 1, "l_ev3b": 1, "l_ev4": 1, "l_kk": 1, "l_BC": 1, "l_RA": 1, "l_bcm": 1, "l_ar": 1, "l_D": 4,
            "l_ex": 4, "l_E": 1, "l_ee": 1, "l_kb": 1, "l_pm": 2, "l_pe": 2, "l_at": 2, "l_xl": 2, "l_lv": 8,
            "l_lc": 8, "l_oS": 1, "l_oR": 1, "l_oeR": 1, "l_oeS": 1, "l_dS": 4, "l_incA": 2, "l_incD": 2,
            "l_qe": 2, "l_qc": 1, "l_ost": 16, "l_qst": 16,
            "s_in": 128, "s_init": 1, "s_fs": 14, "s_bs": 14, "s_out": 128, "r_w_in": 16, "r_gg0": 2,
            "r_in": 48, "r_x_in": 16, "r_st": 1, "r_gg": 1, "r_i1": 1, "r_i2": 1, "r_o": 8, "r_sq": 1,
            "r_red": 2, "r_var": 1, "r_rs": 1, "r_y": 2, "r_yT": 2, "r_yt": 2, "r_out": 2, "r_gy": 2, "r_x1": 1,
            "r_ss": 1, "r_rv2": 1, "r_rs2": 1, "r_xn": 1, "r_xT": 2, "r_ht": 1, "r_lg": 1, "r_lgc": 1,
            "r_xst": 16, "r_nst": 16,
            "k_mx": 2, "k_e": 1, "k_soft": 3, "k_aT": 1, "k_at": 1, "k_r": 5, "k_z": 1, "k_done": 1, "k_T": 1, "k_ix": 1,
            "e_w0": 32, "e_w1": 32, "e_d0": 16, "e_d1": 16, "e_ic": 1, "e_jc": 1, "e_gc": 1, "e_xg": 32, "e_xT": 3, "e_xtd": 2,
            "e_xta": 1, "e_gu": 4, "e_sg": 4, "e_h": 4, "e_dn": 4, "e_pt": 1, "e_y": 3, "e_sc": 16, "e_scp": 16,
        }
        for j, group in enumerate(W_GROUPS):
            COUNTS[f"w{j}"] = 16 * len(group)
        SWDGE = ("e_xg", "e_sc", "e_scp")
        for name, k in COUNTS.items():
            signals[name] = Signal(k, int(name not in SWDGE))
            sem[name] = ctx.enter_context(nc.semaphore(name))
        const_in, lb_in, cond_in, x_init, final_g_in = (
            ctx.enter_context(nc.semaphore(x)) for x in ("const_in", "lb_in", "cond_in", "x_init", "final_g_in"))
        dve_once, act_once, pool_once, primed = (
            ctx.enter_context(nc.semaphore(x)) for x in ("dve_once", "act_once", "pool_once", "primed"))

        def row_bc(v, n):
            return v.rearrange("(a n) -> a n", a=1).broadcast_to([P, n])

        def rows(h):
            return slice(64 * (h % 2), 64 * (h % 2) + 64)

        def halves(v, level, second):
            half = P >> (level + 1)
            lead = " ".join("xyz"[:len(v.shape) - 2])
            w = v.rearrange(f"p {lead} (n two i) -> p {lead} n two i", two=2, i=half)
            return w[(slice(None),) * (len(v.shape) - 1) + (slice(None), int(second), slice(None))]

        def tile_rows(t):
            return bass.ds(t * P, P)

        block = ctx.enter_context(nc.Block())

        @block.sync
        def _(sp):
            sp.dma_start(cst[:, :], const_f).then_inc(const_in, 16)
            sp.dma_start(a_mask, const_m).then_inc(const_in, 16)
            sp.dma_start(cond[:, :, 0], c_ctx.rearrange("(p c) -> p c", c=DC), allow_slow_non_contiguous=True).then_inc(cond_in, 16)
            sp.dma_start(cond[:, :, 1], c[0].rearrange("(p c) -> p c", c=DC), allow_slow_non_contiguous=True).then_inc(cond_in, 16)
            for l in range(DEPTH):
                sp.dma_start(a_lb[:, l, :], row_bc(hg_lb[l].rearrange("d w -> (d w)"), 512)).then_inc(lb_in, 16)
            sp.dma_start(x_d[0:SEQ, :], x_prompt[0]).then_inc(x_init, 16)
            sp.dma_start(x_d[SEQ:T, :], x_sample[0]).then_inc(x_init, 16)
            sp.wait_ge(const_in, 32)
            for col in (0, T + 1):
                sp.dma_start(u_d.rearrange("u p t -> p u t")[:, :, col:col + 1], cst[:, C_SIN:C_SIN + UC].unsqueeze(2),
                             allow_slow_non_contiguous=True).then_inc(x_init, 16)
            sp.wait_ge(x_init, 64)
            sp.wait_ge(primed, 1)

            def load_x(t, n):
                sp.wait_ge(sem["p_xn"], before("p_xn", n))
                sp.sem_inc(tick, 1)
                sp.dma_start(p_x, x_d[tile_rows(t), :]).then_inc(sem["p_x_in"], 16)

            def store_u(t, n):
                sp.wait_ge(sem["p_eva"], by("p_eva", n, 1))
                sp.sem_inc(tick, 1)
                sp.dma_start(u_d.rearrange("u p t -> p u t")[:, :, bass.ds(t * P + 1, P)], p_u).then_inc(sem["p_u_st"], 16)

            def store_proj(t, n):
                sp.wait_ge(sem["p_f2"], by("p_f2", n))
                sp.sem_inc(tick, 1)
                sp.wait_ge(sem["p_evV"], by("p_evV", n))
                sp.sem_inc(tick, 1)
                sp.wait_ge(sem["p_eva"], by("p_eva", n, 4))
                sp.sem_inc(tick, 1)
                sp.dma_start(proj_d[tile_rows(t), :], p_out).then_inc(sem["p_proj_st"], 16)

            def load_w_in(l, g0, g1):
                for j in range(g0, g1):
                    for c0, w in W_GROUPS[j]:
                        sp.dma_start(p_w[c0], w_in[l].rearrange("(c p) n -> p c n", p=P)[:, :, c0:c0 + w]).then_inc(sem[f"w{j}"], 16)

            def load_slab(l, t, i):
                m = l * (NT - 1) + t + 1
                if i:
                    sp.wait_ge(sem["m_used"], by("m_used", m, 1))
                else:
                    sp.wait_ge(sem["m_used"], before("m_used", m))
                sp.sem_inc(tick, 1)
                sp.dma_start(p_slab, w_ada[l].rearrange("(p c) n -> p c n", c=DC)[:, :, bass.ds(t * (2 * M_STEP) + (A_EARLY + i * M_STEP), M_STEP)])\
                    .then_inc(sem["m_in"], 16)

            def load_gate_up(l, e, p):
                sp.dma_start(e_wg[p], w_gate[l, e].rearrange("(c p) n -> p c n", p=P)).then_inc(sem[f"e_w{p}"], 16)
                sp.dma_start(e_wu[p], w_up[l, e].rearrange("(c p) n -> p c n", p=P)).then_inc(sem[f"e_w{p}"], 16)

            def load_down(l, e, p):
                sp.dma_start(e_wd[p], w_down[l, e].rearrange("(c p) n -> p c n", p=P)).then_inc(sem[f"e_d{p}"], 16)

            def load_mix(t, n):
                sp.wait_ge(sem["r_i2"], before("r_i2", n))
                sp.sem_inc(tick, 1)
                sp.wait_ge(sem["r_gg"], before("r_gg", n))
                sp.sem_inc(tick, 1)
                sp.wait_ge(sem["r_y"], before("r_y", n))
                sp.sem_inc(tick, 1)
                sp.dma_start(r_o, o_d[tile_rows(t), :]).then_inc(sem["r_in"], 16)
                sp.dma_start(r_qe.rearrange("p a b -> p (a b)"), qe_d[t]).then_inc(sem["r_in"], 16)
                sp.dma_start(r_g, proj_d[tile_rows(t), J_Z:J_RQ]).then_inc(sem["r_in"], 16)

            def load_res(t, n):
                sp.wait_ge(sem["r_x1"], before("r_x1", n))
                sp.sem_inc(tick, 1)
                sp.dma_start(r_x, x_d[tile_rows(t), :]).then_inc(sem["r_x_in"], 16)

            def store_rows(t, n):
                sp.wait_ge(sem["r_x1"], by("r_x1", n))
                sp.sem_inc(tick, 1)
                sp.dma_start(x_d[tile_rows(t), :], r_x1).then_inc(sem["r_xst"], 16)
                sp.wait_ge(sem["r_xn"], by("r_xn", n))
                sp.sem_inc(tick, 1)
                sp.dma_start(xn_d[tile_rows(t), :], r_xn).then_inc(sem["r_nst"], 16)

            with sp.Fori(0, DEPTH) as l:
                nl = l + 1
                for r0, r1, src in ((0, 8, norm1_g[l].rearrange("(b p) -> b p", p=P)), (8, 16, norm2_g[l].rearrange("(b p) -> b p", p=P)),
                                    (16, 64, b_ada[l].rearrange("(b p) -> b p", p=P)),
                                    (64, 82, ssd_conv_w[l].rearrange("j (b p) -> (j b) p", p=P)),
                                    (82, 88, ssd_conv_b[l].rearrange("(b p) -> b p", p=P))):
                    sp.dma_start(a_rows[r0:r1, :], src).then_inc(sem["a_rows_in"], 16)
                for dst, src, m in ((head_row[:, 0:16], ssd_dt_bias[l].rearrange("d h -> (d h)"), 16),
                                    (head_row[:, 16:32], ssd_a_log[l].rearrange("d h -> (d h)"), 16),
                                    (head_row[:, 32:40], ssd_d[l], 8)):
                    sp.dma_start(dst, row_bc(src, m)).then_inc(sem["a_rows_in"], 16)
                sp.dma_start(w_r[:, :, :], w_router[l].rearrange("(c p) e -> p c e", p=P)).then_inc(sem["a_rows_in"], 16)
                sp.dma_start(a_slab, w_ada[l].rearrange("(p c) n -> p c n", c=DC)[:, :, 0:A_EARLY]).then_inc(sem["a_slab_in"], 16)
                load_w_in(l, 0, 3)
                sp.wait_ge(sem["a_rows_in"], by("a_rows_in", nl))
                sp.sem_inc(tick, 1)
                barrier(sp, l, 1)
                load_w_in(l, 3, 5)
                load_x(0, l * NT + 1)
                with sp.Fori(0, NT - 1) as t:
                    n = l * NT + t + 1
                    load_slab(l, t, 0)
                    store_u(t, n)
                    load_x(t + 1, n + 1)
                    load_slab(l, t, 1)
                    store_proj(t, n)
                store_u(NT - 1, l * NT + NT)
                store_proj(NT - 1, l * NT + NT)
                sp.wait_ge(sem["p_u_st"], by("p_u_st", l * NT + NT))
                sp.sem_inc(tick, 1)
                sp.wait_ge(sem["p_proj_st"], by("p_proj_st", l * NT + NT))
                sp.sem_inc(tick, 1)
                barrier(sp, l, 2)
                with sp.Fori(0, NT) as t:
                    n = l * NT + t + 1
                    sp.wait_ge(sem["l_dS"], before("l_dS", n))
                    sp.sem_inc(tick, 1)
                    sp.dma_start(l_in[:, 0:J_Z], proj_d[tile_rows(t), 0:J_Z]).then_inc(sem["l_in"], 16)
                    sp.dma_start(l_in[:, J_RQ:J_N], proj_d[tile_rows(t), J_RQ:J_N]).then_inc(sem["l_in"], 16)
                    sp.dma_start(l_u, u_d.rearrange("u p t -> p u t")[:, :, bass.ds(t * P, P + 2)]).then_inc(sem["l_uin"], 16)
                    sp.wait_ge(sem["l_qe"], by("l_qe", n))
                    sp.sem_inc(tick, 1)
                    sp.wait_ge(sem["l_qc"], by("l_qc", n))
                    sp.sem_inc(tick, 1)
                    sp.dma_start(qe_d[t], l_qe.rearrange("p a b -> p (a b)")).then_inc(sem["l_qst"], 16)
                    sp.wait_ge(sem["l_oeR"], by("l_oeR", n))
                    sp.sem_inc(tick, 1)
                    sp.wait_ge(sem["l_oeS"], by("l_oeS", n))
                    sp.sem_inc(tick, 1)
                    sp.dma_start(o_d[tile_rows(t), :], l_o).then_inc(sem["l_ost"], 16)
                sp.wait_ge(sem["l_qst"], by("l_qst", l * NT + NT))
                sp.sem_inc(tick, 1)
                sp.wait_ge(sem["l_ost"], by("l_ost", l * NT + NT))
                sp.sem_inc(tick, 1)
                barrier(sp, l, 3)
                for d, slots, slot in ((0, st_f, 1), (1, st_b, 0)):
                    for b0, st in ((0, new_hg), (2, new_ret)):
                        sp.dma_start(st[0, l, d].rearrange("(q h) k v -> (h k) q v", h=2), slots[:, slot, b0:b0 + 2, :]).then_inc(sem["s_out"], 16)
                    for g in range(2):
                        sp.dma_start(new_ssd[0, l, d][4 * g:4 * g + 4].rearrange("a n p -> n a p"), slots[64 * g:64 * g + 64, slot, 4:8, :])\
                            .then_inc(sem["s_out"], 16)
                for dst, src, m in ((gain_row[:, 0:256], hg_norm_g[l], 256), (gain_row[:, 256:768], ssd_norm_g[l], 512),
                                    (gain_row[:, 768:1024], ret_norm_g[l], 256)):
                    sp.dma_start(dst, row_bc(src, m)).then_inc(sem["gain_in"], 16)
                sp.wait_ge(sem["s_out"], by("s_out", nl))
                sp.sem_inc(tick, 1)
                for d, slots, slot in ((0, st_f, 1), (1, st_b, NT)):
                    for b0, st in ((0, state_hgrn), (2, state_ret)):
                        sp.dma_start(slots[:, slot, b0:b0 + 2, :], st[0, l, d].rearrange("(q h) k v -> (h k) q v", h=2)).then_inc(sem["s_in"], 16)
                    for g in range(2):
                        sp.dma_start(slots[64 * g:64 * g + 64, slot, 4:8, :], state_ssd[0, l, d][4 * g:4 * g + 4].rearrange("a n p -> n a p"))\
                            .then_inc(sem["s_in"], 16)
                sp.dma_start(r_w, w_out[l].rearrange("(c p) n -> p c n", p=P)).then_inc(sem["r_w_in"], 16)
                load_mix(0, l * NT + 1)
                load_mix(1, l * NT + 2)
                load_res(0, l * NT + 1)
                with sp.Fori(1, NT - 1) as t:
                    n = l * NT + t + 1
                    load_mix(t + 1, n + 1)
                    load_res(t, n)
                    store_rows(t - 1, n - 1)
                load_res(NT - 1, l * NT + NT)
                store_rows(NT - 2, l * NT + NT - 1)
                store_rows(NT - 1, l * NT + NT)
                sp.wait_ge(sem["r_xst"], by("r_xst", l * NT + NT))
                sp.sem_inc(tick, 1)
                sp.wait_ge(sem["r_nst"], by("r_nst", l * NT + NT))
                sp.sem_inc(tick, 1)
                barrier(sp, l, 4)
                for p in range(2):
                    load_gate_up(l, p, p)
                    load_down(l, p, p)
                barrier(sp, l, 5)
                with sp.Fori(1, NE // 2) as j:
                    for p in range(2):
                        n = l * NE + 2 * j + p + 1
                        sp.wait_ge(sem["e_gu"], before("e_gu", n - 1))
                        sp.sem_inc(tick, 1)
                        load_gate_up(l, 2 * j + p, p)
                        sp.wait_ge(sem["e_dn"], before("e_dn", n - 1))
                        sp.sem_inc(tick, 1)
                        load_down(l, 2 * j + p, p)
                barrier(sp, l, 6)
            sp.dma_start(f_g, row_bc(final_g, D)).then_inc(final_g_in, 16)
            for t in range(NT):
                n = DEPTH * NT + t + 1
                sp.wait_ge(sem["p_xn"], before("p_xn", n))
                sp.sem_inc(tick, 1)
                sp.dma_start(f_x, x_d[tile_rows(t), :]).then_inc(sem["p_x_in"], 16)
                sp.wait_ge(sem["p_f1"], by("p_f1", n))
                sp.sem_inc(tick, 1)
                dst = y_prompt[0] if t == 0 else y_sample[0][(t - 1) * P:t * P, :]
                sp.dma_start(dst, f_y).then_inc(sem["p_u_st"], 16)
            sp.wait_ge(sem["p_u_st"], by("p_u_st", DEPTH * NT + NT))
            sp.sem_inc(tick, 1)

        @block.tensor
        def _(pe):
            def turn(out, in_, k=P):
                return pe.transpose(out, in_, cst[0:k, C_ID:C_ID + k])

            def condition(slab, width, bk, c0):
                for b in range(width // P):
                    for ch in range(DC):
                        mm = pe.matmul(bank[:, bk, c0 + 2 * b:c0 + 2 * b + 2], slab[:, ch, b * P:(b + 1) * P], cond[:, ch, :],
                                       start=(ch == 0), stop=(ch == DC - 1))
                return mm

            def tile_p(nl, n, m):
                pe.wait_ge(sem["p_xn"], by("p_xn", n))
                pe.wait_ge(sem["p_eva"], before("p_eva", n))
                for ch in range(DC):
                    mm = turn(bank[:, ch // 4, (ch % 4) * P:(ch % 4 + 1) * P], p_xn[:, ch * P:(ch + 1) * P])
                mm.then_inc(sem["p_xT"], 1)
                pe.wait_ge(sem["p_hTd"], by("p_hTd", n))
                pe.wait_ge(sem["p_hTa"], by("p_hTa", n))
                pe.wait_ge(sem["w0"], by("w0", nl))
                for b in range(UC):
                    for ch in range(DC):
                        mm = pe.matmul(bank[:, b // 4, (b % 4) * P:(b % 4 + 1) * P], p_w[W_X][:, ch, b * P:(b + 1) * P],
                                       p_h[:, ch, :], start=(ch == 0), stop=(ch == DC - 1))
                mm.then_inc(sem["p_mm"], 1)
                for bk, tag, group, segs in ((2, "A", 1, [(W_Q, 512)]), (4, "C", 2, [(W_Z, 512)]), (5, "G", 2, [(W_G, 256), (W_RG, 256)]),
                                             (3, "B", 3, [(W_F, 512)]), (6, "F", 4, [(W_RQ, 512)]), (7, "V", 4, [(W_RV, 256), (W_DT, 16)])):
                    taken = "p_ev" + tag if tag in "FV" else "p_eva"
                    pe.wait_ge(sem[taken], before(taken, n))
                    if m is not None and tag in "GV":
                        pe.wait_ge(sem["m_in"], by("m_in", m, 16 if tag == "G" else 32))
                        if tag == "G":
                            pe.wait_ge(sem["p_evV"], before("p_evV", n))
                        condition(p_slab, M_STEP, 7, 272 + 4 * int(tag == "V")).then_inc(sem["m_used"], 1)
                    o = 0
                    pe.wait_ge(sem[f"w{group}"], by(f"w{group}", nl))
                    for c0, w in segs:
                        for ch in range(DC):
                            mm = pe.matmul(bank[:, bk, o:o + w], p_h[:, ch, :], p_w[c0][:, ch, :], start=(ch == 0), stop=(ch == DC - 1))
                        o += w
                    mm.then_inc(sem["p_mm"], 1)

            def turn_rows(n):
                pe.wait_ge(sem["e_xg"], by("e_xg", n))
                for q in range(2):
                    for i in range(4):
                        mm = turn(bank[:, q, i * P:(i + 1) * P], e_x[:, (4 * q + i) * P:(4 * q + i + 1) * P])
                    mm.then_inc(sem["e_xT"], 1)
                for ch in range(DC):
                    mm = turn(bank[:, 2, ch * CAP_P:(ch + 1) * CAP_P], e_xp[0:CAP_P, ch * P:(ch + 1) * P], CAP_P)
                mm.then_inc(sem["e_xT"], 1)

            def gate_up(n, m, p):
                pe.wait_ge(sem["e_xtd"], by("e_xtd", n))
                pe.wait_ge(sem["e_xta"], by("e_xta", n))
                pe.wait_ge(sem[f"e_w{p}"], by(f"e_w{p}", m))
                pe.wait_ge(sem["e_h"], before("e_h", n))
                for f in range(FC):
                    if f == 2:
                        pe.wait_ge(sem["e_pt"], before("e_pt", n))
                    if f == 3:
                        pe.wait_ge(sem["e_y"], before("e_y", n))
                    for o, w in ((0, e_wg[p]), (256, e_wu[p])):
                        for ch in range(DC):
                            mm = pe.matmul(bank[:, 4 + f, o:o + CAP_S + CAP_P], w[:, ch, f * P:(f + 1) * P], e_xt[:, ch, :],
                                           start=(ch == 0), stop=(ch == DC - 1))
                    mm.then_inc(sem["e_gu"], 1)

            def down(n, m, p, next_n):
                pe.wait_ge(sem["e_h"], by("e_h", n))
                pe.wait_ge(sem[f"e_d{p}"], by(f"e_d{p}", m))
                for ch in range(DC):
                    for f in range(FC):
                        mm = pe.matmul(bank[:, 6, ch * CAP_P:(ch + 1) * CAP_P], e_wd[p][:, f, ch * P:(ch + 1) * P], e_h[:, f, CAP_S:],
                                       start=(f == 0), stop=(f == FC - 1))
                mm.then_inc(sem["e_dn"], 1)
                for half in range(2):
                    for f in range(FC):
                        mm = pe.matmul(bank[:, 3 + 4 * half, :], e_h[:, f, 0:CAP_S], e_wd[p][:, f, half * 512:(half + 1) * 512],
                                       start=(f == 0), stop=(f == FC - 1))
                    mm.then_inc(sem["e_dn"], 1)
                pe.wait_ge(sem["e_pt"], by("e_pt", n))
                pe.wait_ge(sem["e_xta"], by("e_xta", next_n))
                pe.wait_ge(sem["e_xtd"], by("e_xtd", next_n))
                for ch in range(DC):
                    mm = turn(bank[0:CAP_P, ch // 4, (ch % 4) * P:(ch % 4 + 1) * P], e_pt[:, ch, :])
                mm.then_inc(sem["e_dn"], 1)

            def inter(n):
                pe.wait_ge(sem["r_in"], by("r_in", n))
                pe.wait_ge(sem["r_st"], by("r_st", n))
                pe.wait_ge(sem["r_o"], before("r_o", n))
                for b in range(4):
                    for h in range(2):
                        for d in range(2):
                            mm = pe.matmul(bank[:, 7 * h, b * HD:(b + 1) * HD], r_qe[rows(h), d * 4 + b, :], r_st[rows(h), d, b, :],
                                           start=(d == 0), stop=(d == 1))
                mm.then_inc(sem["r_i1"], 1)
                for d in range(2):
                    for g in range(2):
                        mm = pe.matmul(bank[:, 1 + g, d * 256:(d + 1) * 256], r_qe[rows(g), 8, :], r_st[rows(g), d, 4:8, :], start=True, stop=True)
                mm.then_inc(sem["r_i2"], 1)

            def turn_y(n):
                pe.wait_ge(sem["r_y"], by("r_y", n))
                pe.wait_ge(sem["r_yt"], before("r_yt", n))
                for half in range(2):
                    for i in range(4):
                        ch = half * 4 + i
                        mm = turn(bank[:, 3 + half, i * P:(i + 1) * P], r_y[:, ch * P:(ch + 1) * P])
                    mm.then_inc(sem["r_yT"], 1)

            def project(n, half):
                pe.wait_ge(sem["r_yt"], by("r_yt", n))
                pe.wait_ge(sem["r_gy"], before("r_gy", n))
                for ch in range(DC):
                    mm = pe.matmul(bank[:, 5 + half, :], r_yt[:, ch, :], r_w[:, ch, half * 512:(half + 1) * 512], start=(ch == 0), stop=(ch == DC - 1))
                mm.then_inc(sem["r_out"], 1)

            def turn_xn(n):
                pe.wait_ge(sem["r_xn"], by("r_xn", n))
                for half in range(2):
                    for i in range(4):
                        ch = half * 4 + i
                        mm = turn(bank[:, 7 * half, i * P:(i + 1) * P], r_xn[:, ch * P:(ch + 1) * P])
                    mm.then_inc(sem["r_xT"], 1)

            def router(n):
                pe.wait_ge(sem["r_ht"], by("r_ht", n))
                for ch in range(DC):
                    mm = pe.matmul(bank[:, 1, 0:NE], r_ht[:, ch, :], w_r[:, ch, :], start=(ch == 0), stop=(ch == DC - 1))
                mm.then_inc(sem["r_lg"], 1)

            pe.wait_ge(const_in, 32)
            pe.wait_ge(act_once, 1)
            pe.wait_ge(primed, 1)
            with pe.Fori(0, DEPTH) as l:
                nl = l + 1
                pe.wait_ge(sem["a_rows_in"], by("a_rows_in", nl))
                turn(bank[:, 0, 0:88], a_rows[0:88, :], 88).then_inc(sem["a_vecT"], 1)
                pe.wait_ge(sem["a_slab_in"], by("a_slab_in", nl))
                condition(a_slab, A_EARLY, 1, 0).then_inc(sem["a_used"], 1)
                barrier(pe, l, 1)

                with pe.Fori(0, NT - 1) as t:
                    tile_p(nl, l * NT + t + 1, l * (NT - 1) + t + 1)
                tile_p(nl, l * NT + NT, None)
                barrier(pe, l, 2)

                pe.wait_ge(sem["l_dt"], by("l_dt", nl))
                pe.matmul(bank[:, 0, 0:72], tri[:, LE, :], la_all[:, :, 0:8], start=True, stop=True)
                pe.matmul(bank[:, 0, 72:144], tri[:, GE, :], la_all[:, :, 8:16], start=True, stop=True)
                pe.matmul(bank[:, 1, 0:72], tri[:, GT, :], la_all[:, :, 0:8], start=True, stop=True)
                pe.matmul(bank[:, 1, 72:144], tri[:, LT, :], la_all[:, :, 8:16], start=True, stop=True)
                pe.matmul(bank[:, 2, 0:144], ones, la_all[:, :, :], start=True, stop=True).then_inc(sem["l_bmm"], 1)
                pe.wait_ge(sem["l_bex"], by("l_bex", nl))
                pe.sem_inc(tick, 1)
                with pe.Fori(0, NT) as t:
                    n = l * NT + t + 1
                    pe.wait_ge(sem["l_in"], by("l_in", n))
                    pe.wait_ge(sem["l_incA"], before("l_incA", n))
                    for i in range(4):
                        mm = turn(bank[:, 0, i * P:(i + 1) * P], l_in[:, (J_Q if i < 2 else J_K - 256) + i * P:][:, :P])
                    mm.then_inc(sem["l_T"], 1)
                    for i in range(2):
                        mm = turn(bank[:, 1, i * P:(i + 1) * P], l_in[:, J_K + 256 + i * P:][:, :P])
                    mm.then_inc(sem["l_T"], 1)

                    def levels(d, pair, b0):
                        for half in range(2):
                            mm = pe.matmul(bank[:, b0 + half, :], l_g[:, d * 256 + pair * P:][:, :P], lev[:, d, 4 * half:4 * half + 4, :],
                                           start=True, stop=True)
                        mm.then_inc(sem["l_D"], 1)

                    pe.wait_ge(sem["l_g"], by("l_g", n))
                    pe.wait_ge(sem["l_lc"], before("l_lc", n))
                    levels(0, 0, 6)
                    pe.wait_ge(sem["l_ev1"], by("l_ev1", n))
                    pe.wait_ge(sem["l_ev2"], by("l_ev2", n))
                    levels(0, 1, 0)
                    pe.wait_ge(sem["l_rope"], by("l_rope", n))
                    pe.wait_ge(sem["l_oeR"], before("l_oeR", n))
                    for i in range(4):
                        mm = turn(bank[:, 4, i * P:(i + 1) * P], l_rot[:, i * P:(i + 1) * P])
                    mm.then_inc(sem["l_T"], 1)
                    pe.wait_ge(sem["l_silu"], by("l_silu", n))
                    pe.wait_ge(sem["l_incD"], before("l_incD", n))
                    for i in range(5):
                        mm = turn(bank[:, 2 + i // 4, (i % 4) * P:(i % 4 + 1) * P], l_c[:, i, :])
                    mm.then_inc(sem["l_T"], 1)
                    pe.wait_ge(sem["l_oeS"], before("l_oeS", n))
                    pe.wait_ge(sem["l_ev4"], by("l_ev4", n))
                    for g in range(2):
                        mm = pe.matmul(bank[:, 5 - g, 0:P], l_c[rows(g), 4, :], l_c[rows(g), 5, :], start=True, stop=True)
                    mm.then_inc(sem["l_BC"], 1)
                    for h in range(4):
                        mm = pe.matmul(bank[:, 5 - h % 2, (2 + h // 2) * P:(3 + h // 2) * P], l_rqk[rows(h), 2 + h // 2, :], l_rqk[rows(h), h // 2, :],
                                       start=True, stop=True)
                    mm.then_inc(sem["l_RA"], 1)
                    pe.wait_ge(sem["l_ev3"], by("l_ev3", n))
                    pe.wait_ge(sem["l_ev3b"], by("l_ev3b", n))
                    levels(1, 0, 2)
                    pe.wait_ge(sem["l_ex"], by("l_ex", n, 1))
                    levels(1, 1, 6)
                    pe.wait_ge(sem["l_ar"], by("l_ar", n))
                    pe.matmul(bank[:, 5, 0:256], tri[:, GT, :], l_g[:, 0:256], start=True, stop=True)
                    pe.matmul(bank[:, 5, 256:512], tri[:, LT, :], l_g[:, 256:512], start=True, stop=True).then_inc(sem["l_E"], 1)
                    pe.wait_ge(sem["l_prf"], by("l_prf", n))
                    for d in range(2):
                        pe.wait_ge(sem["l_ex"], by("l_ex", n, 2 + d))
                        for g in range(2):
                            mm = pe.matmul(bank[:, 2 * d + g, :], tri[:, GT + d, :], l_pr[:, d, 4 * g:4 * g + 4, :], start=True, stop=True)
                        mm.then_inc(sem["l_pm"], 1)
                    pe.wait_ge(sem["l_ex"], by("l_ex", n, 4))
                    pe.wait_ge(sem["l_kk"], by("l_kk", n))
                    for i in range(8):
                        bk = 6 if i % 2 == 0 else 0
                        if i == 1:
                            pe.wait_ge(sem["l_pe"], by("l_pe", n, 1))
                        if i >= 2:
                            pe.wait_ge(sem["l_lc"], by("l_lc", n, i - 1))
                        if i == 1:
                            pe.wait_ge(sem["l_xl"], by("l_xl", n))
                        for h in range(4):
                            out = bank[:, bk + h % 2, (h // 2) * P:(h // 2 + 1) * P]
                            if i == 0:
                                mm = pe.matmul(out, l_kk[rows(h), h // 2, :], l_q[rows(h), h // 2, :], start=True, stop=True)
                                continue
                            for d in range(2):
                                x = l_xl[rows(h), d, h // 2, i - 1, :]
                                mm = pe.matmul(halves(out, i - 1, d == 0), x, halves(x, i - 1, d == 0), start=True, stop=True)
                        mm.then_inc(sem["l_lv"], 1)
                    pe.wait_ge(sem["l_lc"], by("l_lc", n))
                    for h in range(8):
                        a, v = (l_ah, J_V) if h < 4 else (l_ar, J_RV)
                        mm = pe.matmul(bank[:, 4, h * HD:(h + 1) * HD], a[:, h % 4, :], l_in[:, v + (h % 4) * HD:][:, :HD], start=True, stop=True)
                    mm.then_inc(sem["l_oR"], 1)
                    pe.wait_ge(sem["l_ee"], by("l_ee", n))
                    pe.wait_ge(sem["l_at"], by("l_at", n))
                    pe.wait_ge(sem["l_v"], by("l_v", n))
                    for h in range(8):
                        for d in range(2):
                            mm = pe.matmul(bank[:, 5, h * HD:(h + 1) * HD], l_at[:, d, h, :], l_v1[:, d, h * HD:(h + 1) * HD], start=(d == 0), stop=(d == 1))
                    mm.then_inc(sem["l_oS"], 1)
                    pe.wait_ge(sem["l_kb"], by("l_kb", n))
                    pe.wait_ge(sem["l_rkb"], by("l_rkb", n))
                    for bk, kb, v in ((0, l_kb, J_V), (1, l_rkb, J_RV)):
                        for i in range(4):
                            mm = pe.matmul(bank[:, bk, i * P:(i + 1) * P], kb[:, i * P:(i + 1) * P], l_in[:, v + (i % 2) * P:][:, :P], start=True, stop=True)
                        mm.then_inc(sem["l_dS"], 1)
                    for d in range(2):
                        pe.matmul(bank[:, 2 + d, :], l_tm[:, 4, :], l_v2[:, d, :], start=True, stop=True).then_inc(sem["l_dS"], 1)
                barrier(pe, l, 3)

                for i in range(4):
                    pe.wait_ge(sem["a_diag"], by("a_diag", nl, i + 1))
                    if i >= 2:
                        pe.wait_ge(sem["a_rowcp"], by("a_rowcp", nl, i - 1))
                    for half in range(2):
                        mm = pe.matmul(bank[:, 2 + 2 * (i % 2) + half, :], ones, s_diag[i % 2][:, 4 * half:4 * half + 4, :], start=True, stop=True)
                    mm.then_inc(sem["a_rowmm"], 1)
                pe.wait_ge(sem["r_w_in"], by("r_w_in", nl))
                pe.wait_ge(sem["a_rowcp"], by("a_rowcp", nl))
                inter(l * NT + 1)
                inter(l * NT + 2)
                turn_y(l * NT + 1)
                project(l * NT + 1, 0)
                project(l * NT + 1, 1)
                with pe.Fori(1, NT - 1) as t:
                    n = l * NT + t + 1
                    pe.wait_ge(sem["r_lgc"], before("r_lgc", n - 1))
                    inter(n + 1)
                    turn_y(n)
                    project(n, 0)
                    turn_xn(n - 1)
                    project(n, 1)
                    router(n - 1)
                turn_y(l * NT + NT)
                project(l * NT + NT, 0)
                turn_xn(l * NT + NT - 1)
                project(l * NT + NT, 1)
                router(l * NT + NT - 1)
                turn_xn(l * NT + NT)
                router(l * NT + NT)
                barrier(pe, l, 4)

                pe.wait_ge(sem["k_soft"], by("k_soft", nl))
                for i in range(NT):
                    mm = turn(bank[0:NE, 1 + i // 4, (i % 4) * P:(i % 4 + 1) * P], lg_all[:, i, :])
                mm.then_inc(sem["k_aT"], 1)
                pe.wait_ge(sem["k_done"], by("k_done", nl))
                for i in range(4):
                    mm = turn(bank[:, 0, i * P:(i + 1) * P], k_t[:, i, :])
                mm.then_inc(sem["k_T"], 1)
                barrier(pe, l, 5)

                turn_rows(l * NE + 1)
                with pe.Fori(0, NE // 2 - 1) as j:
                    for p in range(2):
                        n, m = l * NE + 2 * j + p + 1, l * (NE // 2) + j + 1
                        gate_up(n, m, p)
                        turn_rows(n + 1)
                        down(n, m, p, n + 1)
                gate_up(l * NE + NE - 1, (l + 1) * (NE // 2), 0)
                turn_rows(l * NE + NE)
                down(l * NE + NE - 1, (l + 1) * (NE // 2), 0, l * NE + NE)
                gate_up(l * NE + NE, (l + 1) * (NE // 2), 1)
                down(l * NE + NE, (l + 1) * (NE // 2), 1, l * NE + NE)
                barrier(pe, l, 6)

        @block.scalar
        def _(act):
            def ev(out, in_, func=ACT.Copy, **kw):
                return act.activation(out, in_, func, **kw)

            act.wait_ge(cond_in, 32)
            ev(cond[:, :, :], cond[:, :, :], ACT.Silu).then_inc(act_once, 1)
            act.wait_ge(dve_once, 3)
            for j in range(DEPTH):
                ev(a_lbt[:, 1 + j, :], a_lbt[:, 1 + j, :], ACT.Exp).then_inc(act_once, 1)
            act.wait_ge(primed, 1)

            def square_x(n):
                act.wait_ge(sem["p_x_in"], by("p_x_in", n))
                act.wait_ge(sem["p_rv"], before("p_rv", n))
                act.wait_ge(sem["p_xT"], before("p_xT", n))
                ev(p_xn, p_x, ACT.Square, accum_out=small[:, 0:1]).then_inc(sem["p_ss"], 1)

            def turn_p(t, n, more):
                act.wait_ge(sem["p_xT"], by("p_xT", n))
                act.wait_ge(sem["p_mm"], before("p_mm", n))
                act.sem_inc(tick, 1)
                for ch in range(4, DC):
                    last = ev(p_h[:, ch, :], bank[:, 1, (ch - 4) * P:(ch - 3) * P], ACT.Identity,
                              scale=scale1[:, t, ch:ch + 1], bias=shift1[:, t, ch:ch + 1])
                last.then_inc(sem["p_hTa"], 1)
                act.wait_ge(sem["p_mm"], by("p_mm", n, 1))
                act.wait_ge(sem["p_u_st"], before("p_u_st", n))
                ev(p_u[:, 0:4, :], bank[:, 0, :].rearrange("p (a b) -> p a b", a=4))
                ev(p_u[:, 4:6, :], bank[:, 1, 0:256].rearrange("p (a b) -> p a b", a=2)).then_inc(sem["p_eva"], 1)
                act.wait_ge(sem["p_mm"], by("p_mm", n, 2))
                act.wait_ge(sem["p_proj_st"], before("p_proj_st", n))
                ev(p_out[:, J_V:J_V + 256], bank[:, 2, 256:512])
                ev(p_out[:, J_Q:J_Q + 256], bank[:, 2, 0:256], ACT.Silu).then_inc(sem["p_eva"], 1)
                act.wait_ge(sem["p_mm"], by("p_mm", n, 3))
                ev(p_out[:, J_Z:J_Z + 512], bank[:, 4, :], ACT.Silu).then_inc(sem["p_eva"], 1)
                if more:
                    square_x(n + 1)
                act.wait_ge(sem["p_mm"], by("p_mm", n, 4))
                ev(p_out[:, J_G:J_G + 512], bank[:, 5, :], ACT.Silu).then_inc(sem["p_eva"], 1)
                act.wait_ge(sem["p_mm"], by("p_mm", n, 5))
                act.wait_ge(sem["p_f2"], before("p_f2", n))
                ev(p_sig[:, 0, :], bank[:, 3, :], ACT.Sigmoid)
                ev(p_sig[:, 1, :], bank[:, 3, :], ACT.Sigmoid, scale=-1.0).then_inc(sem["p_eva"], 1)

            def modulate_a(n):
                act.wait_ge(sem["e_xT"], by("e_xT", n, 2))
                act.wait_ge(sem["e_gu"], before("e_gu", n))
                for ch in range(4, DC):
                    last = ev(e_xt[:, ch, 0:CAP_S], bank[:, 1, (ch - 4) * P:(ch - 3) * P], ACT.Identity,
                              scale=scale2[:, 1, ch:ch + 1], bias=shift2[:, 1, ch:ch + 1])
                last.then_inc(sem["e_xta"], 1)

            def silu_gate(n):
                for f in range(FC):
                    act.wait_ge(sem["e_gu"], by("e_gu", n, f + 1))
                    act.wait_ge(sem["e_h"], before("e_h", n))
                    ev(e_sg[:, f, :], bank[:, 4 + f, 0:CAP_S + CAP_P], ACT.Silu).then_inc(sem["e_sg"], 1)

            def take_prompt(n):
                act.wait_ge(sem["e_dn"], by("e_dn", n, 1))
                ev(e_pt, bank[:, 6, 0:DC * CAP_P].rearrange("p (a b) -> p a b", b=CAP_P)).then_inc(sem["e_pt"], 1)

            def squares_o(n):
                act.wait_ge(sem["r_o"], by("r_o", n))
                act.wait_ge(sem["r_red"], before("r_red", n))
                ev(r_sq, r_o, ACT.Square).then_inc(sem["r_sq"], 1)

            def take_yT(n):
                for half in range(2):
                    act.wait_ge(sem["r_yT"], by("r_yT", n, half + 1))
                    act.wait_ge(sem["r_out"], before("r_out", n))
                    ev(r_yt[:, 4 * half:4 * half + 4, :], bank[:, 3 + half, :].rearrange("p (a b) -> p a b", a=4)).then_inc(sem["r_yt"], 1)

            def squares_x(n):
                act.wait_ge(sem["r_x1"], by("r_x1", n))
                act.wait_ge(sem["r_rv2"], before("r_rv2", n))
                ev(r_junk, r_x1, ACT.Square, accum_out=small[:, 0:1]).then_inc(sem["r_ss"], 1)

            with act.Fori(0, DEPTH) as l:
                nl = l + 1
                act.wait_ge(sem["a_rows_in"], by("a_rows_in", nl))
                ev(small[:, 40:56], head_row[:, 16:32], ACT.Exp).then_inc(act_once, 1)
                barrier(act, l, 1)
                square_x(l * NT + 1)
                with act.Fori(0, NT - 1) as t:
                    turn_p(t, l * NT + t + 1, True)
                turn_p(NT - 1, l * NT + NT, False)
                barrier(act, l, 2)
                act.wait_ge(sem["l_de"], by("l_de", nl))
                ev(l_s[:, 1], l_s[:, 1], ACT.Exp).then_inc(act_once, 1)
                act.wait_ge(sem["l_bmm"], by("l_bmm", nl))
                for d in range(2):
                    ev(eb_all[:, :, 8 * d:8 * d + 8], bank[:, 0, 72 * d:72 * d + 72].rearrange("p (a b) -> p a b", b=8), ACT.Exp)
                    ev(l_s[:, 2, :, 8 * d:8 * d + 8], bank[:, 1, 72 * d:72 * d + 72].rearrange("p (a b) -> p a b", b=8), ACT.Exp)
                ev(etot[:, :, :], bank[:, 2, 0:144].rearrange("p (a b) -> p a b", b=16), ACT.Exp).then_inc(sem["l_bex"], 1)
                with act.Fori(0, NT) as t:
                    n = l * NT + t + 1

                    def levels_exp(d, pair, b0, i):
                        act.wait_ge(sem["l_D"], by("l_D", n, i))
                        ev(l_ex[:, d, pair].rearrange("p a b -> p (a b)"), bank[:, b0:b0 + 2, :].rearrange("p a b -> p (a b)"), ACT.Exp)\
                            .then_inc(sem["l_ex"], 1)

                    act.wait_ge(sem["l_in"], by("l_in", n))
                    act.wait_ge(sem["l_E"], before("l_E", n))
                    ev(l_g, l_in[:, J_F:J_F + 512], ACT.Ln).then_inc(sem["l_g"], 1)
                    act.wait_ge(sem["l_T"], by("l_T", n, 1))
                    act.wait_ge(sem["l_xl"], before("l_xl", n))
                    act.wait_ge(sem["l_qe"], before("l_qe", n))
                    act.wait_ge(sem["l_lv"], before("l_lv", n))
                    ev(l_q, bank[:, 0, 0:256].rearrange("p (a b) -> p a b", a=2), scale=HD ** -0.5)
                    ev(l_k[:, 0], bank[:, 0, 256:512].rearrange("p (a b) -> p a b", a=2)).then_inc(sem["l_ev1"], 1)
                    levels_exp(0, 0, 6, 1)
                    levels_exp(0, 1, 0, 2)
                    act.wait_ge(sem["l_cv"], by("l_cv", n))
                    for b in range(UC):
                        last = ev(l_c[:, b, :], l_c[:, b, :], ACT.Silu, bias=vecs[:, 82 + b:83 + b])
                    last.then_inc(sem["l_silu"], 1)
                    act.wait_ge(sem["l_T"], by("l_T", n, 4))
                    act.wait_ge(sem["l_v"], before("l_v", n))
                    act.wait_ge(sem["l_sk"], before("l_sk", n))
                    act.wait_ge(sem["l_dS"], before("l_dS", n))
                    ev(l_tm[:, 0:4, :], bank[:, 2, :].rearrange("p (a b) -> p a b", a=4)).then_inc(sem["l_ev3"], 1)
                    levels_exp(1, 0, 2, 3)
                    levels_exp(1, 1, 6, 4)
                    act.wait_ge(sem["l_E"], by("l_E", n))
                    act.wait_ge(sem["l_kb"], before("l_kb", n))
                    ev(l_ee, bank[:, 5, :], ACT.Exp).then_inc(sem["l_ee"], 1)
                    for d in range(2):
                        act.wait_ge(sem["l_pm"], by("l_pm", n, d + 1))
                        act.wait_ge(sem["l_oS"], before("l_oS", n))
                        ev(l_at[:, d].rearrange("p a b -> p (a b)"), bank[:, 2 * d:2 * d + 2, :].rearrange("p a b -> p (a b)"), ACT.Exp)\
                            .then_inc(sem["l_pe"], 1)
                    act.wait_ge(sem["l_oR"], by("l_oR", n))
                    act.wait_ge(sem["l_ost"], before("l_ost", n))
                    ev(l_o[:, 0:256], bank[:, 4, 0:256])
                    ev(l_o[:, 768:1024], bank[:, 4, 256:512]).then_inc(sem["l_oeR"], 1)
                    for i in range(2):
                        act.wait_ge(sem["l_dS"], by("l_dS", n, i + 1))
                        act.sem_inc(tick, 1)
                        for g in range(2):
                            src = bank[rows(g), i, :].rearrange("p (d q v) -> p d q v", d=2, q=2)[:, :, :, 64 * g:64 * g + 64]
                            ev(st_f[rows(g), t + 1, 2 * i:2 * i + 2, :], src[:, 0])
                            last = ev(st_b[rows(g), t, 2 * i:2 * i + 2, :], src[:, 1])
                        last.then_inc(sem["l_incA"], 1)
                barrier(act, l, 3)
                for i in range(4):
                    act.wait_ge(sem["a_rowmm"], by("a_rowmm", nl, i + 1))
                    b0 = 2 + 2 * (i % 2)
                    ev(gate_row[:, i // 2, i % 2, :], bank[:, b0:b0 + 2, :].rearrange("p a b -> p (a b)")).then_inc(sem["a_rowcp"], 1)
                squares_o(l * NT + 1)
                take_yT(l * NT + 1)
                squares_o(l * NT + 2)
                squares_x(l * NT + 1)
                with act.Fori(1, NT - 1) as t:
                    n = l * NT + t + 1
                    take_yT(n)
                    squares_o(n + 1)
                    squares_x(n)
                take_yT(l * NT + NT)
                squares_x(l * NT + NT)
                barrier(act, l, 4)
                act.wait_ge(sem["k_mx"], by("k_mx", nl))
                ev(lg_all[:, :, :], lg_all[:, :, :], ACT.Exp).then_inc(sem["k_e"], 1)
                act.wait_ge(sem["k_aT"], by("k_aT", nl))
                ev(aff_t[:, 0:1024], bank[0:NE, 1:3, :].rearrange("p a b -> p (a b)"))
                ev(aff_t[:, 1024:T], bank[0:NE, 3, 0:P]).then_inc(sem["k_at"], 1)
                barrier(act, l, 5)
                modulate_a(l * NE + 1)
                with act.Fori(0, NE - 1) as e:
                    n = l * NE + e + 1
                    silu_gate(n)
                    modulate_a(n + 1)
                    take_prompt(n)
                silu_gate(l * NE + NE)
                take_prompt(l * NE + NE)
                barrier(act, l, 6)
            for t in range(NT):
                n = DEPTH * NT + t + 1
                act.wait_ge(sem["p_x_in"], by("p_x_in", n))
                act.wait_ge(sem["p_rv"], before("p_rv", n))
                ev(f_junk, f_x, ACT.Square, accum_out=small[:, 0:1]).then_inc(sem["p_ss"], 1)

        @block.vector
        def _(dve):
            def tt(out, a, b, op=ALU.mult):
                return dve.tensor_tensor(out, a, b, op)

            def bc(v, n):
                return v.unsqueeze(len(v.shape)).broadcast_to(list(v.shape) + [n])

            once = [0]

            def step(ins):
                once[0] += 1
                ins.then_inc(dve_once, 1)
                dve.wait_ge(dve_once, once[0])

            dve.wait_ge(lb_in, 32)
            step(tt(a_lbt[:, 0, :], a_lb[:, 0, :], a_lb[:, 1, :], ALU.max))
            for j in range(DEPTH):
                step(tt(a_lbt[:, 1 + j, :], a_lb[:, j, :], a_lbt[:, 0, :], ALU.subtract))
            dve.wait_ge(act_once, 3)
            step(tt(a_lbt[:, 3, :], a_lbt[:, 1, :], a_lbt[:, 2, :], ALU.add))
            step(dve.reciprocal(a_lbt[:, 3, :], a_lbt[:, 3, :]))
            for j in range(DEPTH):
                step(tt(a_lbt[:, 1 + j, :], a_lbt[:, 1 + j, :], a_lbt[:, 3, :]))
            step(tt(a_lbt[:, 2, :], a_lbt[:, 1, :], a_lbt[:, 2, :], ALU.add))
            step(tt(lb[:, 0, 0, :], a_lbt[:, 1, :], a_lbt[:, 1, :], ALU.subtract))
            step(tt(lb[:, 1, 0, :], a_lbt[:, 2, :], a_lbt[:, 1, :], ALU.subtract))
            for j in range(DEPTH):
                step(dve.tensor_scalar(lb[:, j, 1, :], lb[:, j, 0, :], -1.0, 1.0, ALU.mult, ALU.add))
            dve.wait_ge(const_in, 32)
            step(dve.tensor_copy(lev_mask[:, :, :].rearrange("p a b -> p (a b)"), a_mask))
            dve.wait_ge(primed, 1)

            def norm_x(n):
                dve.wait_ge(sem["p_rstd"], by("p_rstd", n))
                dve.wait_ge(sem["p_xT"], before("p_xT", n))
                dve.tensor_scalar(p_xn, p_x, small[:, 2:3], None, ALU.mult).then_inc(sem["p_xn"], 1)

            def turn_p(l, t, n, more):
                dve.wait_ge(sem["p_xT"], by("p_xT", n))
                dve.wait_ge(sem["p_mm"], before("p_mm", n))
                for ch in range(4):
                    last = dve.tensor_scalar(p_h[:, ch, :], bank[:, 0, ch * P:(ch + 1) * P], scale1[:, t, ch:ch + 1],
                                             shift1[:, t, ch:ch + 1], ALU.mult, ALU.add)
                last.then_inc(sem["p_hTd"], 1)
                if more:
                    norm_x(n + 1)
                dve.wait_ge(sem["p_eva"], by("p_eva", n, 5))
                dve.wait_ge(sem["p_proj_st"], before("p_proj_st", n))
                tt(p_sig[:, 0, :], p_sig[:, 0, :], lb[:, l, 1, :]).then_inc(sem["p_f1"], 1)
                tt(p_out[:, J_K:J_K + 512], p_sig[:, 1, :], lb[:, l, 1, :]).then_inc(sem["p_f2"], 1)
                dve.wait_ge(sem["p_f1"], by("p_f1", n))
                dve.scalar_tensor_tensor(out=p_out[:, J_F:J_F + 512], in0=p_sig[:, 0, :], scalar=2.0 ** -60, in1=lb[:, l, 0, :],
                                         op0=ALU.max, op1=ALU.add).then_inc(sem["p_f2"], 1)
                dve.wait_ge(sem["p_mm"], by("p_mm", n, 6))
                dve.tensor_copy(p_out[:, J_RQ:J_RQ + 512], bank[:, 6, :]).then_inc(sem["p_evF"], 1)
                dve.wait_ge(sem["p_mm"], by("p_mm", n, 7))
                dve.tensor_copy(p_out[:, J_RV:J_RV + 256], bank[:, 7, 0:256])
                if more:
                    tt(mod[:, bass.ds(t * 4 + 16, 4), :], bank[:, 7, 272:280].rearrange("p (a b) -> p a b", b=2), bc(vecs[:, bass.ds(t * 4 + 32, 4)], 2), ALU.add)
                dve.tensor_copy(dt_all[:, t, :], bank[:, 7, 256:272]).then_inc(sem["p_evV"], 1)

            def modulate_d(n):
                dve.wait_ge(sem["e_xT"], by("e_xT", n, 1))
                dve.wait_ge(sem["e_gu"], before("e_gu", n))
                for ch in range(4):
                    dve.tensor_scalar(e_xt[:, ch, 0:CAP_S], bank[:, 0, ch * P:(ch + 1) * P], scale2[:, 1, ch:ch + 1],
                                      shift2[:, 1, ch:ch + 1], ALU.mult, ALU.add)
                dve.wait_ge(sem["e_xT"], by("e_xT", n, 3))
                tt(e_xt[:, :, CAP_S:], bank[:, 2, 0:DC * CAP_P].rearrange("p (a b) -> p a b", b=CAP_P), bc(scale2[:, 0, :], CAP_P))\
                    .then_inc(sem["e_xtd"], 1)
                dve.wait_ge(sem["e_xtd"], by("e_xtd", n, 1))
                tt(e_xt[:, :, CAP_S:], e_xt[:, :, CAP_S:], bc(shift2[:, 0, :], CAP_P), ALU.add).then_inc(sem["e_xtd"], 1)

            def times_up(n):
                for f in range(FC):
                    dve.wait_ge(sem["e_sg"], by("e_sg", n, f + 1))
                    dve.wait_ge(sem["e_dn"], before("e_dn", n))
                    tt(e_h[:, f, :], bank[:, 4 + f, 256:256 + CAP_S + CAP_P], e_sg[:, f, :]).then_inc(sem["e_h"], 1)

            def weighted(e, n):
                dve.wait_ge(sem["e_y"], before("e_y", n))
                dve.sem_inc(tick, 1)
                dve.tensor_copy(e_g[:, 0:1], k_val[:, 0, bass.ds(e, 1)])
                dve.tensor_copy(e_g[0:CAP_P, 1:2], k_val[0:CAP_P, 1, bass.ds(e, 1)]).then_inc(sem["e_gc"], 1)
                dve.wait_ge(sem["e_gc"], by("e_gc", n))
                dve.wait_ge(sem["e_jc"], by("e_jc", n))
                for half in range(2):
                    cols = slice(half * 512, (half + 1) * 512)
                    dve.wait_ge(sem["e_dn"], by("e_dn", n, 2 + half))
                    dve.scalar_tensor_tensor(out=e_y[:, cols], in0=bank[:, 3 + 4 * half, :], scalar=e_g[:, 0:1],
                                             in1=gate_row[:, 1, 1, cols], op0=ALU.mult, op1=ALU.mult).then_inc(sem["e_y"], 1)
                dve.wait_ge(sem["e_dn"], by("e_dn", n))
                dve.scalar_tensor_tensor(out=e_yp[0:CAP_P, :], in0=bank[0:CAP_P, 0:2, :].rearrange("p a b -> p (a b)"), scalar=e_g[0:CAP_P, 1:2],
                                         in1=gate_row[0:CAP_P, 1, 0, :], op0=ALU.mult, op1=ALU.mult).then_inc(sem["e_y"], 1)

            def spread(k0, g0, sc, sh):
                for tl, w, cd in ((0, 1, 0), (1, NT - 1, 1)):
                    def over(v):
                        return v.unsqueeze(1).broadcast_to([P, w, DC])
                    dve.scalar_tensor_tensor(out=sc[:, tl:tl + w, :], in0=over(mod[:, k0 + 8:k0 + 16, cd]), scalar=1.0,
                                             in1=over(vecs[:, g0:g0 + 8]), op0=ALU.add, op1=ALU.mult)
                    last = dve.tensor_copy(sh[:, tl:tl + w, :], over(mod[:, k0:k0 + 8, cd]))
                return last

            def diagonal(i, nl):
                k0 = 16 if i < 2 else 40
                tt(s_diag[i % 2], ident.unsqueeze(1).broadcast_to([P, DC, P]), bc(mod[:, k0:k0 + 8, i % 2], P)).then_inc(sem["a_diag"], 1)

            def mix(t, n):
                dve.wait_ge(sem["r_i1"], by("r_i1", n))
                ln = Link(dve, "r_o", n)
                kv = r_o.rearrange("p (m q h v) -> p m q h v", m=4, q=2, h=2)[:, 0:4:3]
                for h in range(2):
                    v = kv[:, :, :, h, :]
                    last = tt(v, v, bank[:, 7 * h, 0:256].rearrange("p (m q v) -> p m q v", m=2, q=2), ALU.add)
                ln(last)
                dve.wait_ge(sem["r_i2"], by("r_i2", n))
                for g in range(2):
                    last = tt(r_t.rearrange("p d (g a b) -> p d g a b", g=2, b=HD)[:, :, g], bank[:, 1 + g, :].rearrange("p (d a b) -> p d a b", d=2, b=HD),
                              bc(eb_all[:, t, :].rearrange("p (d g a) -> p d g a", d=2, g=2)[:, :, g, :], HD))
                ln(last)
                o_s, o_r = r_o[:, 256:768], r_o[:, 768:1024].rearrange("p (a b) -> p a b", b=HD)
                ln(tt(o_s, o_s, r_t1, ALU.add))
                ln(tt(o_s, o_s, r_t2, ALU.add))
                ln(tt(o_s, o_s, r_g[:, 0:512]))
                ln(dve.tensor_reduce(small[:, 4:8], o_r, AX, ALU.add))
                ln(dve.tensor_scalar(small[:, 4:8], small[:, 4:8], -1.0 / HD, None, ALU.mult))
                ln(tt(o_r, o_r, bc(small[:, 4:8], HD), ALU.add), last=True)

            def sums(n):
                dve.wait_ge(sem["r_sq"], by("r_sq", n))
                dve.wait_ge(sem["r_var"], before("r_var", n))
                dve.tensor_reduce(small[:, 32:48], r_sq.rearrange("p (a b) -> p a b", b=HD), AX, ALU.add).then_inc(sem["r_red"], 1)
                dve.wait_ge(sem["r_red"], by("r_red", n, 1))
                dve.tensor_reduce(small[:, 8:9], small[:, 36:44], AX, ALU.add).then_inc(sem["r_red"], 1)

            def normed(n):
                dve.wait_ge(sem["r_rs"], by("r_rs", n))
                dve.wait_ge(sem["r_yT"], before("r_yT", n))
                v = r_y.rearrange("p (a b) -> p a b", b=HD)
                tt(v, r_o.rearrange("p (a b) -> p a b", b=HD), bc(small[:, 48:64], HD)).then_inc(sem["r_y"], 1)
                dve.wait_ge(sem["r_y"], by("r_y", n, 1))
                dve.wait_ge(sem["r_gg"], by("r_gg", n))
                tt(r_y, r_y, r_gg).then_inc(sem["r_y"], 1)

            def gated(kind, n):
                dve.wait_ge(sem["r_x1"], before("r_x1", n))
                for half in range(2):
                    dve.wait_ge(sem["r_out"], by("r_out", n, half + 1))
                    tt(r_gy[:, half * 512:(half + 1) * 512], bank[:, 5 + half, :],
                       gate_row[:, 0, kind, half * 512:(half + 1) * 512]).then_inc(sem["r_gy"], 1)

            def second_norm(n):
                dve.wait_ge(sem["r_rs2"], by("r_rs2", n))
                dve.wait_ge(sem["r_xT"], before("r_xT", n))
                dve.wait_ge(sem["r_nst"], before("r_nst", n))
                dve.tensor_scalar(r_xn, r_x1, small[:, 2:3], None, ALU.mult).then_inc(sem["r_xn"], 1)

            def modulated(t, n):
                for ch in range(DC):
                    if ch % 4 == 0:
                        dve.wait_ge(sem["r_xT"], by("r_xT", n, ch // 4 + 1))
                        dve.wait_ge(sem["r_lg"], before("r_lg", n))
                    last = dve.tensor_scalar(r_ht[:, ch, :], bank[:, 7 * (ch // 4), (ch % 4) * P:(ch % 4 + 1) * P],
                                             scale2[:, t, ch:ch + 1], shift2[:, t, ch:ch + 1], ALU.mult, ALU.add)
                last.then_inc(sem["r_ht"], 1)

            def logits(t, n):
                dve.wait_ge(sem["r_lg"], by("r_lg", n))
                dve.tensor_copy(lg_all[:, t, :], bank[:, 1, 0:NE]).then_inc(sem["r_lgc"], 1)

            with dve.Fori(0, DEPTH) as l:
                nl = l + 1
                dve.wait_ge(sem["a_vecT"], by("a_vecT", nl))
                dve.tensor_copy(vecs[:, :], bank[:, 0, 0:88]).then_inc(sem["a_vecs"], 1)
                dve.wait_ge(sem["a_used"], by("a_used", nl))
                dve.wait_ge(sem["a_vecs"], by("a_vecs", nl))
                tt(mod[:, 0:16, :], bank[:, 1, 0:32].rearrange("p (a b) -> p a b", b=2), bc(vecs[:, 16:32], 2), ALU.add).then_inc(sem["a_mod"], 1)
                dve.wait_ge(sem["a_mod"], by("a_mod", nl))
                spread(0, 0, scale1, shift1).then_inc(sem["a_scales"], 1)
                barrier(dve, l, 1)
                norm_x(l * NT + 1)
                with dve.Fori(0, NT - 1) as t:
                    turn_p(l, t, l * NT + t + 1, True)
                turn_p(l, NT - 1, l * NT + NT, False)
                barrier(dve, l, 2)

                flat = [l_s[:, i].rearrange("p a b -> p (a b)") for i in range(4)]
                dts = dt_all[:, :, :].rearrange("p a b -> p (a b)")
                bias = head_row[:, 0:16].unsqueeze(1).broadcast_to([P, NT, 16])
                tt(dt_all[:, :, :], dt_all[:, :, :], bias, ALU.add).then_inc(sem["l_de"], 1)
                dve.wait_ge(sem["l_de"], by("l_de", nl, 1))
                dve.scalar_tensor_tensor(out=flat[1], in0=dts, scalar=-1.0, in1=dts, op0=ALU.mult, op1=ALU.min).then_inc(sem["l_de"], 1)
                dve.wait_ge(act_once, (l + 1) * 2 + 3)
                dve.sem_inc(tick, 1)
                ln = Link(dve, "l_dt", nl)
                ln(dve.tensor_scalar(flat[0], flat[1], 2.0, None, ALU.add))
                ln(dve.reciprocal(flat[0], flat[0]))
                ln(tt(flat[0], flat[0], flat[1]))
                ln(tt(flat[3], flat[0], flat[0]))
                ln(dve.tensor_scalar(flat[2], flat[3], 1.0 / 17, None, ALU.mult))
                for odd in (15, 13, 11, 9, 7, 5, 3):
                    ln(dve.scalar_tensor_tensor(out=flat[2], in0=flat[2], scalar=1.0 / odd, in1=flat[3], op0=ALU.add, op1=ALU.mult))
                ln(dve.scalar_tensor_tensor(out=flat[2], in0=flat[2], scalar=1.0, in1=flat[0], op0=ALU.add, op1=ALU.mult))
                ln(dve.tensor_scalar(dts, dts, 0.0, None, ALU.max))
                ln(dve.scalar_tensor_tensor(out=dts, in0=flat[2], scalar=2.0, in1=dts, op0=ALU.mult, op1=ALU.add))
                ln(dve.scalar_tensor_tensor(out=la_all[:, :, :], in0=dt_all[:, :, :], scalar=-1.0,
                                            in1=small[:, 40:56].unsqueeze(1).broadcast_to([P, NT, 16]), op0=ALU.mult, op1=ALU.mult), last=True)
                dve.wait_ge(sem["l_bex"], by("l_bex", nl))
                tt(dtee[:, :, :], dt_all[:, :, :], l_s[:, 2])
                for d in range(2):
                    for g in range(2):
                        dve.tensor_copy(dec[rows(g), :, d, 4:8], etot[rows(g), :, 8 * d + 4 * g:8 * d + 4 * g + 4])
                    last = dve.tensor_copy(dec[:, :, d, 2:4], cst[:, C_RT + 2 * d:C_RT + 2 * d + 2].unsqueeze(1).broadcast_to([P, NT, 2]))
                last.then_inc(sem["l_dec0"], 1)

                with dve.Fori(0, NT) as t:
                    n = l * NT + t + 1
                    dve.wait_ge(sem["l_T"], by("l_T", n, 2))
                    dve.wait_ge(sem["l_xl"], before("l_xl", n))
                    dve.wait_ge(sem["l_lv"], before("l_lv", n))
                    dve.tensor_copy(l_k[:, 1], bank[:, 1, 0:256].rearrange("p (a b) -> p a b", a=2)).then_inc(sem["l_ev2"], 1)
                    dve.wait_ge(sem["l_ev1"], by("l_ev1", n))
                    dve.wait_ge(sem["l_ev2"], by("l_ev2", n))
                    tt(l_kk, l_k[:, 0], l_k[:, 1], ALU.add).then_inc(sem["l_kk"], 1)
                    dve.wait_ge(sem["l_T"], by("l_T", n, 3))
                    dve.tensor_copy(l_rqk, bank[:, 4, :].rearrange("p (a b) -> p a b", a=4)).then_inc(sem["l_ev4"], 1)
                    dve.wait_ge(sem["l_T"], by("l_T", n, 4))
                    dve.wait_ge(sem["l_dS"], before("l_dS", n))
                    dve.tensor_copy(l_tm[:, 4, :], bank[:, 3, 0:P]).then_inc(sem["l_ev3b"], 1)
                    dve.wait_ge(sem["l_RA"], by("l_RA", n))
                    dve.wait_ge(sem["l_at"], before("l_at", n))
                    for g in range(2):
                        last = tt(l_bc[:, :, g, :], bank[:, 5 - g, 0:P].unsqueeze(1).broadcast_to([P, 2, P]), tri[:, LE:LE + 2, :])
                    last.then_inc(sem["l_bcm"], 1)
                    dve.wait_ge(sem["l_oR"], before("l_oR", n))
                    for h in range(2):
                        last = tt(l_ar[:, h:4:2, :], bank[:, 5 - h, 256:512].rearrange("p (a b) -> p a b", a=2),
                                  cst[:, C_RM:C_RM + 512].rearrange("p (a b) -> p a b", a=4)[:, h:4:2, :])
                    last.then_inc(sem["l_ar"], 1)
                    for d in range(2):
                        dve.wait_ge(sem["l_ex"], by("l_ex", n, 2 * d + 2))
                        for level in range(NL):
                            for second in range(2):
                                src = l_q if (second == 1) == (d == 0) else l_k[:, d]
                                last = tt(halves(l_xl[:, d, :, level, :], level, second), halves(l_ex[:, d, :, level, :], level, second),
                                          halves(src, level, second))
                        last.then_inc(sem["l_xl"], 1)
                    dve.wait_ge(sem["l_qst"], before("l_qst", n))
                    for d in range(2):
                        tt(l_qe[:, 4 * d:4 * d + 2, :], l_ex[:, d, :, 7, :], l_q)
                        tt(l_qe[:, 4 * d + 2:4 * d + 4, :], l_rqk[:, 0:2, :],
                           cst[:, C_RQ + d * 256:C_RQ + (d + 1) * 256].rearrange("p (a b) -> p a b", a=2))
                        dve.tensor_copy(dec[:, t, d, 0:2], l_ex[:, d, :, 7, P - 1 if d == 0 else 0]).then_inc(sem["l_qe"], 1)
                    dve.wait_ge(sem["l_ee"], by("l_ee", n))
                    tt(l_kb, l_in[:, J_K:J_K + 512], l_ee).then_inc(sem["l_kb"], 1)
                    dve.wait_ge(sem["l_bcm"], by("l_bcm", n))
                    for d in range(2):
                        dve.wait_ge(sem["l_pe"], by("l_pe", n, d + 1))
                        v = l_at[:, d].rearrange("p (g h) t -> p g h t", g=2)
                        tt(v, v, l_bc[:, d].unsqueeze(2).broadcast_to([P, 2, 4, P])).then_inc(sem["l_at"], 1)
                    for i in range(8):
                        dve.wait_ge(sem["l_lv"], by("l_lv", n, i + 1))
                        b0 = 6 if i % 2 == 0 else 0
                        src = bank[:, b0:b0 + 2, 0:256].rearrange("p h (q t) -> p h q t", q=2)
                        dst = l_ah.rearrange("p (q h) t -> p h q t", h=2)
                        if i == 0:
                            dve.wait_ge(sem["l_oR"], before("l_oR", n))
                            for h in range(2):
                                last = tt(dst[:, h], src[:, h], ident.unsqueeze(1).broadcast_to([P, 2, P]))
                            last.then_inc(sem["l_lc"], 1)
                        else:
                            dve.wait_ge(sem["l_lc"], by("l_lc", n, i))
                            dve.sem_inc(tick, 1)
                            for h in range(2):
                                last = dve.copy_predicated(dst[:, h], lev_mask[:, i - 1, :].unsqueeze(1).broadcast_to([P, 2, P]), src[:, h])
                            last.then_inc(sem["l_lc"], 1)
                    dve.wait_ge(sem["l_oS"], by("l_oS", n))
                    dve.wait_ge(sem["l_sk"], by("l_sk", n))
                    dve.wait_ge(sem["l_ost"], before("l_ost", n))
                    tt(l_o[:, 256:768], bank[:, 5, :], l_sk, ALU.add).then_inc(sem["l_oeS"], 1)
                    for d in range(2):
                        dve.wait_ge(sem["l_dS"], by("l_dS", n, 3 + d))
                        dve.sem_inc(tick, 1)
                        for g in range(2):
                            last = dve.tensor_copy((st_f[:, t + 1] if d == 0 else st_b[:, t])[rows(g), 4:8, :], bank[rows(g), 2 + d, 256 * g:256 * g + 256].rearrange("p (a b) -> p a b", a=4))
                        last.then_inc(sem["l_incD"], 1)
                barrier(dve, l, 3)

                dve.memset(st_f[:, 0], 0.0).then_inc(sem["s_init"], 1)
                spread(24, 8, scale2, shift2).then_inc(sem["a_scales"], 1)
                diagonal(0, nl)
                diagonal(1, nl)
                dve.wait_ge(sem["s_in"], by("s_in", nl))
                ln = Link(dve, "s_fs", nl)
                for tile in range(1, NT - 1):
                    step_f = r_t1.rearrange("p (a b) -> p a b", b=HD)
                    ln(tt(step_f, st_f[:, tile], bc(dec[:, tile, 0, :], HD)))
                    ln(tt(st_f[:, tile + 1], st_f[:, tile + 1], step_f, ALU.add), last=(tile == NT - 2))
                for i in range(2, 4):
                    dve.wait_ge(sem["a_rowmm"], by("a_rowmm", nl, i - 1))
                    diagonal(i, nl)
                dve.wait_ge(sem["a_rowmm"], by("a_rowmm", nl))
                mix(0, l * NT + 1)
                sums(l * NT + 1)
                normed(l * NT + 1)
                mix(1, l * NT + 2)
                sums(l * NT + 2)
                normed(l * NT + 2)
                gated(0, l * NT + 1)
                with dve.Fori(1, NT - 1) as t:
                    n = l * NT + t + 1
                    mix(t + 1, n + 1)
                    second_norm(n - 1)
                    sums(n + 1)
                    modulated(t - 1, n - 1)
                    normed(n + 1)
                    gated((t + 7) // 8, n)
                    logits(t - 1, n - 1)
                second_norm(l * NT + NT - 1)
                modulated(NT - 2, l * NT + NT - 1)
                gated(1, l * NT + NT)
                logits(NT - 2, l * NT + NT - 1)
                second_norm(l * NT + NT)
                modulated(NT - 1, l * NT + NT)
                logits(NT - 1, l * NT + NT)
                barrier(dve, l, 4)

                dve.memset(k_t, 0.0).then_inc(sem["k_z"], 1)
                ln = Link(dve, "k_mx", nl)
                ln(dve.tensor_reduce(k_red, lg_all[:, :, :], AX, ALU.max))
                ln(tt(lg_all[:, :, :], lg_all[:, :, :], bc(k_red, NE), ALU.subtract), last=True)
                dve.wait_ge(sem["k_e"], by("k_e", nl))
                ln = Link(dve, "k_soft", nl)
                ln(dve.tensor_reduce(k_red, lg_all[:, :, :], AX, ALU.add))
                ln(dve.reciprocal(k_red, k_red))
                ln(tt(lg_all[:, :, :], lg_all[:, :, :], bc(k_red, NE)), last=True)
                dve.wait_ge(sem["k_at"], by("k_at", nl))
                dve.sem_inc(tick, 1)
                dve.wait_ge(sem["k_z"], by("k_z", nl))
                dve.sem_inc(tick, 1)

                def round_(src, kind, r, n):
                    ln = Link(dve, "k_r", n)
                    ln.hold(dve.max(k_m8[0:NE, :], src))
                    ln.hold(dve.max_index(k_i8[0:NE, :].bitcast(U32), k_m8[0:NE, :], src))
                    ln.hold(dve.match_replace(src, k_m8[0:NE, :], src, -1.0))
                    ln.hold(dve.tensor_copy(k_t[0:NE, kind, bass.ds(r * 8, 8)], k_i8[0:NE, :].bitcast(U32)))
                    ln.hold(dve.tensor_copy(k_t[0:NE, kind + 1, bass.ds(r * 8, 8)], k_m8[0:NE, :]))

                ROUNDS_S, ROUNDS_P = CAP_S // 8, CAP_P // 8
                with dve.Fori(0, ROUNDS_S) as r:
                    round_(aff_t[:, SEQ:T], 0, r, l * (ROUNDS_S + ROUNDS_P) + r + 1)
                for r in range(ROUNDS_P):
                    round_(aff_t[:, 0:SEQ], 2, r, l * (ROUNDS_S + ROUNDS_P) + ROUNDS_S + r + 1)
                dve.tensor_copy(k_m8[0:NE, :], k_m8[0:NE, :]).then_inc(sem["k_done"], 1)
                dve.wait_ge(sem["k_T"], by("k_T", nl))
                dve.tensor_scalar(k_idx[:, 0, :].bitcast(U32), bank[:, 0, 0:NE], float(SEQ), None, ALU.add)
                dve.tensor_copy(k_idx[0:CAP_P, 1, :].bitcast(U32), bank[0:CAP_P, 0, 256:256 + NE])
                dve.tensor_copy(k_val[:, 0, :], bank[:, 0, P:P + NE])
                dve.tensor_copy(k_val[0:CAP_P, 1, :], bank[0:CAP_P, 0, 384:384 + NE]).then_inc(sem["k_ix"], 1)
                barrier(dve, l, 5)
                modulate_d(l * NE + 1)
                with dve.Fori(0, NE - 1) as e:
                    n = l * NE + e + 1
                    times_up(n)
                    modulate_d(n + 1)
                    weighted(e, n)
                times_up(l * NE + NE)
                weighted(NE - 1, l * NE + NE)
                barrier(dve, l, 6)
            dve.wait_ge(final_g_in, 16)
            for t in range(NT):
                n = DEPTH * NT + t + 1
                dve.wait_ge(sem["p_rstd"], by("p_rstd", n))
                if t:
                    dve.wait_ge(sem["p_u_st"], by("p_u_st", n - 1))
                dve.tensor_scalar(f_y, f_x, small[:, 2:3], None, ALU.mult).then_inc(sem["p_xn"], 1)
                dve.wait_ge(sem["p_xn"], by("p_xn", n))
                tt(f_y, f_y, f_g).then_inc(sem["p_f1"], 1)

        @block.gpsimd
        def _(pool):
            def tt(out, a, b, op=ALU.mult):
                return pool.tensor_tensor(out, a, b, op)

            def bc(v, n):
                return v.unsqueeze(len(v.shape)).broadcast_to(list(v.shape) + [n])

            for name in COUNTS:
                if name not in SWDGE:
                    pool.sem_inc(sem[name], 1)
            pool.memset(minus_half[:, :], -0.5).then_inc(pool_once, 1)
            pool.wait_ge(pool_once, 1)
            pool.sem_inc(primed, 1)
            pool.wait_ge(const_in, 32)

            def rstd(src, mid, out, ss, rv, rs, used, n):
                pool.wait_ge(sem[ss], by(ss, n))
                pool.sem_inc(tick, 1)
                pool.tensor_scalar(small[:, mid:mid + 1], small[:, src:src + 1], 1.0 / D, EPS, ALU.mult, ALU.add).then_inc(sem[rv], 1)
                pool.wait_ge(sem[rv], by(rv, n))
                pool.wait_ge(sem[used], before(used, n))
                pool.sem_inc(tick, 1)
                tt(small[:, out:out + 1], small[:, mid:mid + 1], minus_half[:, 0:1], ALU.pow).then_inc(sem[rs], 1)

            def entering(t, n):
                pool.wait_ge(sem["r_i2"], before("r_i2", n))
                pool.sem_inc(tick, 1)
                pool.tensor_copy(r_st[:, 0], st_f[:, t])
                pool.tensor_copy(r_st[:, 1], st_b[:, t + 1]).then_inc(sem["r_st"], 1)

            def gates(n):
                pool.wait_ge(sem["r_in"], by("r_in", n))
                pool.wait_ge(sem["r_y"], before("r_y", n))
                pool.sem_inc(tick, 1)
                tt(r_gg[:, 0:256], r_g[:, 512:768], gain_row[:, 0:256])
                tt(r_gg[:, 768:1024], r_g[:, 768:1024], gain_row[:, 768:1024]).then_inc(sem["r_gg"], 1)

            def variances(n):
                pool.wait_ge(sem["r_red"], by("r_red", n))
                pool.sem_inc(tick, 1)
                for dst, src, m in ((small[:, 32:36], small[:, 32:36], HD), (small[:, 36:44], small[:, 8:9].broadcast_to([P, 8]), SSDW),
                                    (small[:, 44:48], small[:, 44:48], HD)):
                    last = pool.tensor_scalar(dst, src, 1.0 / m, EPS, ALU.mult, ALU.add)
                last.then_inc(sem["r_var"], 1)
                pool.wait_ge(sem["r_var"], by("r_var", n))
                pool.wait_ge(sem["r_y"], before("r_y", n))
                pool.sem_inc(tick, 1)
                tt(small[:, 48:64], small[:, 32:48], minus_half[:, :], ALU.pow).then_inc(sem["r_rs"], 1)

            def residual(n):
                pool.wait_ge(sem["r_gy"], by("r_gy", n))
                pool.wait_ge(sem["r_x_in"], by("r_x_in", n))
                pool.wait_ge(sem["r_xst"], before("r_xst", n))
                pool.wait_ge(sem["r_xn"], before("r_xn", n))
                pool.wait_ge(sem["r_ss"], before("r_ss", n))
                pool.sem_inc(tick, 1)
                tt(r_x1, r_x, r_gy, ALU.add).then_inc(sem["r_x1"], 1)
                rstd(0, 1, 2, "r_ss", "r_rv2", "r_rs2", "r_xn", n)

            with pool.Fori(0, DEPTH) as l:
                nl = l + 1
                barrier(pool, l, 1)
                with pool.Fori(0, NT) as t:
                    rstd(0, 1, 2, "p_ss", "p_rv", "p_rstd", "p_xn", l * NT + t + 1)
                barrier(pool, l, 2)
                pool.wait_ge(sem["l_dec0"], by("l_dec0", nl))
                pool.sem_inc(tick, 1)
                with pool.Fori(0, NT) as t:
                    n = l * NT + t + 1
                    pool.wait_ge(sem["l_pm"], before("l_pm", n))
                    pool.sem_inc(tick, 1)
                    for d in range(2):
                        last = tt(l_pr[:, d], tri[:, LE + d, :].unsqueeze(1).broadcast_to([P, 8, P]), bc(la_all[:, t, 8 * d:8 * d + 8], P))
                    last.then_inc(sem["l_prf"], 1)
                    pool.wait_ge(sem["l_in"], by("l_in", n))
                    pool.sem_inc(tick, 1)
                    ln = Link(pool, "l_rope", n)
                    x = l_in[:, J_RQ:J_RQ + 512].rearrange("p (j m i) -> p j m i", j=2, i=32)
                    for dst, c0 in ((l_r1, C_COS), (l_r2, C_SIN)):
                        w = cst[:, bass.ds(c0 + t * 64, 64)].rearrange("p (j i) -> p j i", j=2).unsqueeze(2).broadcast_to([P, 2, 8, 32])
                        ln.hold(tt(dst.rearrange("p (j m i) -> p j m i", j=2, i=32), x, w))
                    v1, v2, vo = (v.rearrange("p (m two i) -> p m two i", two=2, i=32) for v in (l_r1, l_r2, l_rot))
                    pool.wait_ge(sem["l_T"], before("l_T", n))
                    pool.sem_inc(tick, 1)
                    ln.hold(tt(vo[:, :, 0, :], v1[:, :, 0, :], v2[:, :, 1, :], ALU.subtract))
                    ln(tt(vo[:, :, 1, :], v2[:, :, 0, :], v1[:, :, 1, :], ALU.add), last=True)
                    pool.wait_ge(sem["l_uin"], by("l_uin", n))
                    pool.sem_inc(tick, 1)
                    edge = l_u[:, :, 0:P + 2:P + 1]
                    tt(edge, edge, cst[:, bass.ds(C_HALO + t * 2, 2)].unsqueeze(1).broadcast_to([P, UC, 2])).then_inc(sem["l_halo"], 1)
                    pool.wait_ge(sem["l_halo"], by("l_halo", n))
                    pool.wait_ge(sem["l_T"], before("l_T", n))
                    pool.wait_ge(sem["l_BC"], before("l_BC", n))
                    pool.sem_inc(tick, 1)
                    pool.wait_ge(sem["l_qc"], before("l_qc", n))
                    pool.sem_inc(tick, 1)
                    ln = Link(pool, "l_cv", n)
                    ln(tt(l_c, l_u[:, :, 0:P], bc(vecs[:, 64:70], P)))
                    ln(tt(l_ct, l_u[:, :, 1:P + 1], bc(vecs[:, 70:76], P)))
                    ln(tt(l_c, l_c, l_ct, ALU.add))
                    ln(tt(l_ct, l_u[:, :, 2:P + 2], bc(vecs[:, 76:82], P)))
                    ln(tt(l_c, l_c, l_ct, ALU.add), last=True)
                    pool.wait_ge(sem["l_rope"], by("l_rope", n))
                    pool.wait_ge(sem["l_dS"], before("l_dS", n))
                    pool.sem_inc(tick, 1)
                    for d in range(2):
                        last = tt(l_rkb[:, d * 256:(d + 1) * 256].rearrange("p (a b) -> p a b", b=HD),
                                  l_rot[:, 256:512].rearrange("p (a b) -> p a b", b=HD), bc(cst[:, C_RK + 4 * d:C_RK + 4 * d + 4], HD))
                    last.then_inc(sem["l_rkb"], 1)
                    pool.wait_ge(sem["l_ev3"], by("l_ev3", n))
                    pool.sem_inc(tick, 1)
                    pool.wait_ge(sem["l_oS"], before("l_oS", n))
                    pool.sem_inc(tick, 1)
                    xs = l_tm[:, 0:4, :].rearrange("p a (h b) -> p (a h) b", b=HD)
                    for d in range(2):
                        tt(l_v1[:, d].rearrange("p (a b) -> p a b", b=HD), xs, bc(dt_all[:, t, 8 * d:8 * d + 8], HD))
                        last = tt(l_v2[:, d].rearrange("p (a b) -> p a b", b=HD), xs, bc(dtee[:, t, 8 * d:8 * d + 8], HD))
                    last.then_inc(sem["l_v"], 1)
                    pool.wait_ge(sem["l_oeS"], before("l_oeS", n))
                    pool.sem_inc(tick, 1)
                    tt(l_sk.rearrange("p (a b) -> p a b", b=HD), xs, bc(head_row[:, 32:40], HD)).then_inc(sem["l_sk"], 1)
                    pool.wait_ge(sem["l_silu"], by("l_silu", n))
                    pool.wait_ge(sem["l_qst"], before("l_qst", n))
                    pool.sem_inc(tick, 1)
                    pool.tensor_copy(l_qe[:, 8, :], l_c[:, 5, :]).then_inc(sem["l_qc"], 1)
                barrier(pool, l, 3)
                pool.wait_ge(sem["s_init"], by("s_init", nl))
                pool.wait_ge(sem["gain_in"], by("gain_in", nl))
                pool.wait_ge(sem["s_in"], by("s_in", nl))
                pool.sem_inc(tick, 1)
                pool.tensor_copy(r_gg[:, 256:768], gain_row[:, 256:768]).then_inc(sem["r_gg0"], 1)
                ln = Link(pool, "s_bs", nl)
                for tile in range(NT - 1, 1, -1):
                    step_b = r_t2.rearrange("p (a b) -> p a b", b=HD)
                    ln(tt(step_b, st_b[:, tile + 1], bc(dec[:, tile, 1, :], HD)))
                    ln(tt(st_b[:, tile], st_b[:, tile], step_b, ALU.add), last=(tile == 2))
                pool.memset(st_b[:, 1], 0.0).then_inc(sem["r_gg0"], 1)
                pool.wait_ge(sem["s_bs"], by("s_bs", nl))
                pool.wait_ge(sem["s_fs"], by("s_fs", nl))
                pool.sem_inc(tick, 1)
                pool.wait_ge(sem["r_gg0"], by("r_gg0", nl))
                pool.sem_inc(tick, 1)
                entering(0, l * NT + 1)
                gates(l * NT + 1)
                entering(1, l * NT + 2)
                variances(l * NT + 1)
                with pool.Fori(0, NT - 2) as t:
                    n = l * NT + t + 1
                    gates(n + 1)
                    entering(t + 2, n + 2)
                    variances(n + 1)
                    residual(n)
                gates(l * NT + NT)
                variances(l * NT + NT)
                residual(l * NT + NT - 1)
                residual(l * NT + NT)
                barrier(pool, l, 4)
                barrier(pool, l, 5)

                def gather(e, n):
                    if not isinstance(e, int):
                        pool.wait_ge(sem["e_xg"], by("e_xg", n - 1))
                        pool.sem_inc(tick, 1)
                    pool.tensor_copy(e_i[:, 0:1].bitcast(U32), k_idx[:, 0, bass.ds(e, 1)].bitcast(U32))
                    pool.tensor_copy(e_i[0:CAP_P, 1:2].bitcast(U32), k_idx[0:CAP_P, 1, bass.ds(e, 1)].bitcast(U32)).then_inc(sem["e_ic"], 1)
                    pool.wait_ge(sem["e_ic"], by("e_ic", n))
                    pool.wait_ge(sem["e_xT"], before("e_xT", n))
                    pool.sem_inc(tick, 1)
                    pool.indirect_dma_start(e_x, None, xn_d, bass.IndirectOffsetOnAxis(ap=e_i[:, 0:1].bitcast(U32), axis=0)).then_inc(sem["e_xg"], 16)
                    pool.indirect_dma_start(e_xp[0:CAP_P, :], None, xn_d, bass.IndirectOffsetOnAxis(ap=e_i[0:CAP_P, 1:2].bitcast(U32), axis=0))\
                        .then_inc(sem["e_xg"], 16)

                def scatter(e, n):
                    if not isinstance(e, int) or e > 0:
                        pool.wait_ge(sem["e_sc"], by("e_sc", n - 1))
                        pool.wait_ge(sem["e_scp"], by("e_scp", n - 1))
                        pool.sem_inc(tick, 1)
                    pool.tensor_copy(k_j[:, 0:1].bitcast(U32), k_idx[:, 0, bass.ds(e, 1)].bitcast(U32))
                    pool.tensor_copy(k_j[0:CAP_P, 1:2].bitcast(U32), k_idx[0:CAP_P, 1, bass.ds(e, 1)].bitcast(U32)).then_inc(sem["e_jc"], 1)
                    pool.wait_ge(sem["e_jc"], by("e_jc", n))
                    pool.wait_ge(sem["e_y"], by("e_y", n))
                    pool.sem_inc(tick, 1)
                    pool.indirect_dma_start(x_d, bass.IndirectOffsetOnAxis(ap=k_j[:, 0:1].bitcast(U32), axis=0), e_y, None, compute_op=ALU.add)\
                        .then_inc(sem["e_sc"], 16)
                    pool.indirect_dma_start(x_d, bass.IndirectOffsetOnAxis(ap=k_j[0:CAP_P, 1:2].bitcast(U32), axis=0), e_yp[0:CAP_P, :], None, compute_op=ALU.add)\
                        .then_inc(sem["e_scp"], 16)

                gather(0, l * NE + 1)
                pool.wait_ge(sem["e_xg"], by("e_xg", l * NE + 1))
                pool.sem_inc(tick, 1)
                gather(1, l * NE + 2)
                scatter(0, l * NE + 1)
                with pool.Fori(1, NE - 1) as e:
                    n = l * NE + e + 1
                    gather(e + 1, n + 1)
                    scatter(e, n)
                scatter(NE - 1, l * NE + NE)
                pool.wait_ge(sem["e_sc"], by("e_sc", l * NE + NE))
                pool.wait_ge(sem["e_scp"], by("e_scp", l * NE + NE))
                pool.sem_inc(tick, 1)
                barrier(pool, l, 6)
            for t in range(NT):
                rstd(0, 1, 2, "p_ss", "p_rv", "p_rstd", "p_xn", DEPTH * NT + t + 1)


_INS = ["x_prompt", "x_sample", "state_hgrn", "state_ssd", "state_ret", "c", "c_ctx", "norm1_g", "norm2_g", "final_g",
        "w_ada", "b_ada", "w_in", "w_out", "hg_lb", "hg_norm_g", "ssd_conv_w", "ssd_conv_b", "ssd_dt_bias", "ssd_a_log",
        "ssd_d", "ssd_norm_g", "ret_norm_g", "w_router", "w_gate", "w_up", "w_down"]
_OUTS = [(1, SEQ, D), (1, DEC, D), (1, DEPTH, 2, 4, 64, 64), (1, DEPTH, 2, 8, 64, 64), (1, DEPTH, 2, 4, 64, 64)]


def kernel(**inputs):
    import numpy as _np
    import concourse.bacc as _bacc
    from concourse import mybir as _mybir
    from concourse.bass_utils import run_bass_kernel_spmd as _run

    nc = _bacc.Bacc("TRN2", target_bir_lowering=False, num_devices=1)
    arrays, args = {}, []
    const_f, const_m = shape_constants()
    given = [(name, _np.ascontiguousarray(inputs[name])) for name in _INS] + [("const_f", const_f), ("const_m", const_m)]
    for name, a in given:
        arrays[f"in_{name}_dram"] = a
        args.append(nc.dram_tensor(f"in_{name}_dram", a.shape, _mybir.dt.from_np(a.dtype), kind="ExternalInput").ap())
    for i, shape in enumerate(_OUTS):
        args.append(nc.dram_tensor(f"out_{i}_dram", shape, _mybir.dt.float32, kind="ExternalOutput").ap())
    trunk(nc, *args)
    r = _run(nc, [arrays], core_ids=[0])
    return tuple(r.results[0][f"out_{i}_dram"] for i in range(len(_OUTS)))
```

```python
import math
from contextlib import ExitStack

import numpy as np

import concourse.bass as bass
from concourse import mybir

F32 = mybir.dt.float32
U8 = mybir.dt.uint8
U32 = mybir.dt.uint32
ALU = mybir.AluOpType
ACT = mybir.ActivationFunctionType
AX = mybir.AxisListType.X

P = 128
D = 1024
DC = D // P
DEPTH = 2
SEQ = 128
DEC = 1024
T = SEQ + DEC
NT = T // P
HD = 64
GRID_W = 64
EPS = 1e-6
HGW, SSDW, RETW = 256, 512, 256
D_IN = 3600
NE = 16
DE = 512
FC = DE // P
CAP_S = 2 * DEC // NE
CAP_P = 2 * SEQ // NE
NL = 7
A_EARLY = 2 * D
M_STEP = 2 * D // (NT - 1)
EARLY = 768 + 512 + 1024

W_Q, W_I, W_F, W_G, W_Z, W_X, W_DT, W_RQ, W_RV, W_RG = 0, 256, 512, 1024, 1280, 1792, 2560, 2576, 3088, 3344
J_Q, J_V, J_F, J_K, J_Z, J_G, J_RQ, J_RV, J_N = 0, 256, 512, 1024, 1536, 2048, 2560, 3072, 3328
UC = 6

C_ID, C_ONE = 0, 128
C_TRI = 256
C_LEV = C_TRI + 4 * P
C_RM = C_LEV + 2 * 8 * P
C_RQ = C_RM + 4 * P
C_RK = C_RQ + 4 * P
C_RT = C_RK + 8
C_COS = C_RT + 4
C_SIN = C_COS + NT * 64
C_HALO = C_SIN + NT * 64
C_N = C_HALO + NT * 2


def shape_constants():
    c = np.zeros((P, C_N), np.float64)
    i = np.arange(P)
    r, t = i[:, None], i[None, :]
    c[:, C_ID:C_ID + P] = np.eye(P)
    c[:, C_ONE:C_ONE + P] = 1
    for j, m in enumerate((r <= t, r >= t, r > t, r < t)):
        c[:, C_TRI + j * P:C_TRI + (j + 1) * P] = m
    masks = np.zeros((P, 2, NL, P), np.float32)
    for lev in range(NL):
        half = P >> (lev + 1)
        mid = t // (2 * half) * 2 * half + half
        f = np.where(t >= mid, (r >= mid) & (r <= t), (r > t) & (r < mid))
        b = np.where(t < mid, (r >= t) & (r < mid), (r >= mid) & (r < t))
        for d, m in enumerate((f, b)):
            o = C_LEV + (d * 8 + lev) * P
            c[:, o:o + P] = m
        masks[:, 0, lev] = (r // (2 * half) == t // (2 * half)) & (r < mid) & (t >= mid)
        masks[:, 1, lev] = (r // (2 * half) == t // (2 * half)) & (r >= mid) & (t < mid)
    c[:, C_LEV + 7 * P:C_LEV + 8 * P] = r <= t
    c[:, C_LEV + 15 * P:C_LEV + 16 * P] = r >= t
    for d in range(2):
        for h in range(4):
            lg = math.log1p(-(2.0 ** (-5.0 - 0.5 * d - h)))
            c[:, C_RM + h * P:C_RM + (h + 1) * P] += np.exp(lg * np.abs(t - r)) * ((r <= t) if d == 0 else (r >= t))
            rows = slice(64 * (h % 2), 64 * (h % 2) + 64)
            o = C_RQ + (d * 2 + h // 2) * P
            c[rows, o:o + P] = np.exp(lg * (t + 1 if d == 0 else P - t))
            c[:, C_RK + d * 4 + h] = np.exp(lg * (127 - i if d == 0 else i))
            c[rows, C_RT + d * 2 + h // 2] = np.exp(lg * P)
    nf = HD // 4
    inv = 10000.0 ** (-np.arange(nf) / nf)
    for tile in range(NT):
        tok = np.arange(P) + (tile - 1) * P
        ang = np.concatenate([(tok // GRID_W)[:, None] * inv, (tok % GRID_W)[:, None] * inv], 1)
        co, si = (np.cos(ang), np.sin(ang)) if tile else (np.ones_like(ang), np.zeros_like(ang))
        for j, sc in enumerate((1.0, HD ** -0.5)):
            c[:, C_COS + tile * 64 + j * 32:][:, :32] = co * sc
            c[:, C_SIN + tile * 64 + j * 32:][:, :32] = si * sc
        c[:, C_HALO + tile * 2] = tile > 1
        c[:, C_HALO + tile * 2 + 1] = 0 < tile < NT - 1
    return c.astype(np.float32), masks.reshape(P, 2 * NL * P)


class Signal:

    def __init__(self, k, start=1):
        self.k, self.start = k, start

    def by(self, n, i=None):
        return n * self.k + ((i - self.k if i is not None else 0) + self.start)

    def before(self, n):
        return n * self.k + (1 - self.k)


def trunk(nc, x_prompt, x_sample, state_hgrn, state_ssd, state_ret, c, c_ctx, norm1_g, norm2_g, final_g,
          w_ada, b_ada, w_in, w_out, hg_lb, hg_norm_g, ssd_conv_w, ssd_conv_b, ssd_dt_bias, ssd_a_log,
          ssd_d, ssd_norm_g, ret_norm_g, w_router, w_gate, w_up, w_down, const_f, const_m,
          y_prompt, y_sample, new_hg, new_ssd, new_ret):
    ctx = ExitStack()
    with ctx:
        def sb(name, shape, dt=F32):
            return ctx.enter_context(nc.sbuf_tensor(name, shape, dt))

        x_d = nc.dram_tensor("x_d", (T, D), F32).ap()
        xn_d = nc.dram_tensor("xn_d", (T, D), F32).ap()
        proj_d = nc.dram_tensor("proj_d", (T, J_N), F32).ap()
        u_d = nc.dram_tensor("u_d", (UC, P, T + 2), F32).ap()
        o_d = nc.dram_tensor("o_d", (T, D), F32).ap()
        qe_d = nc.dram_tensor("qe_d", (NT, P, 9 * P), F32).ap()

        cst = sb("cst", [P, C_N])
        lev_mask = sb("lev_mask", [P, 2, NL, P], U8)
        ident = cst[:, C_ID:C_ID + P]
        ones = cst[:, C_ONE:C_ONE + P]
        tri = cst[:, C_TRI:C_TRI + 4 * P].rearrange("p (j t) -> p j t", j=4)
        LE, GE, GT, LT = range(4)
        lev = cst[:, C_LEV:C_RM].rearrange("p (d n t) -> p d n t", d=2, n=8)
        minus_half = sb("minus_half", [P, 16])
        lb = sb("lb", [P, DEPTH, 2, 512])
        cond = sb("cond", [P, DC, 2])
        vecs = sb("vecs", [P, 88])
        mod = sb("mod", [P, 48, 2])
        scale1 = sb("scale1", [P, NT, DC])
        shift1 = sb("shift1", [P, NT, DC])
        scale2 = sb("scale2", [P, NT, DC])
        shift2 = sb("shift2", [P, NT, DC])
        gate_row = sb("gate_row", [P, 2, 2, D])
        head_row = sb("head_row", [P, 40])
        w_r = sb("w_r", [P, DC, NE])
        dt_all = sb("dt_all", [P, NT, 16])
        la_all = sb("la_all", [P, NT, 16])
        eb_all = sb("eb_all", [P, NT, 16])
        dtee = sb("dtee", [P, NT, 16])
        etot = sb("etot", [P, NT, 16])
        dec = sb("dec", [P, NT, 2, 8])
        small = sb("small", [P, 64])
        lg_all = sb("lg_all", [P, NT, NE])
        WORK = 39400
        work = sb("work", [P, WORK])

        def carve(start=0):
            at = [start]

            def take(*shape):
                n = int(np.prod(shape))
                assert at[0] + n <= WORK, (at[0], n, WORK)
                v = work[:, at[0]:at[0] + n]
                at[0] += n
                if len(shape) > 1:
                    names = "abcd"[:len(shape)]
                    v = v.rearrange(f"p ({' '.join(names)}) -> p {' '.join(names)}", **dict(zip(names, shape)))
                return v
            return take

        bank = ctx.enter_context(nc.psum_tensor("bank", [P, 8, 512], F32))

        signals, sem = {}, {}

        def by(name, n, i=None):
            return signals[name].by(n, i)

        def before(name, n):
            return signals[name].before(n)

        take = carve(DC * EARLY)
        a_rows = take(P)
        a_slab = [take(DC, D) for _ in range(2)]
        a_lb = take(DEPTH, 512)
        a_mask = gate_row[:, :, :, :].rearrange("p a b c -> p (a b c)")[:, 0:2 * NL * P]
        a_lbt = take(4, 512)
        a_row = gate_row[0:2, 1, :, :].rearrange("p b c -> p (b c)")

        take = carve()
        W_BLOCKS = {"U": [(W_X, 768)], "A": [(W_Q, 512)], "C": [(W_Z, 512)], "G": [(W_G, 256), (W_RG, 256)],
                    "B": [(W_F, 512)], "F": [(W_RQ, 512)], "V": [(W_RV, 256), (W_DT, 16)]}
        W_GROUPS = ["U", "A", "CG", "B", "FV"]
        p_w = {tag: take(DC, sum(w for _, w in segs)) for tag, segs in W_BLOCKS.items()}
        p_x = take(D)
        p_xn = take(D)
        p_h = [take(DC, P) for _ in range(2)]
        p_out = take(J_N)
        p_u = take(UC, P)
        p_slab = take(DC, M_STEP)

        take = carve()
        st_f = take(NT + 1, 8, HD)
        st_b = take(NT + 1, 8, HD)
        l_in = take(J_N)
        l_u = take(UC, P + 2)
        l_c = take(UC, P)
        l_ct = take(UC, P)
        l_g = take(512)
        l_q = take(2, P)
        l_k = take(2, 2, P)
        l_kk = take(2, P)
        l_ex = take(2, 2, 8, P)
        l_xl = take(2, 2, NL, P)
        l_ee = take(512)
        l_kb = take(512)
        l_tm = take(5, P)
        l_rot = take(512)
        l_r1 = take(512)
        l_r2 = take(512)
        l_rqk = take(4, P)
        l_rkb = take(512)
        l_ah = take(4, P)
        l_ar = take(4, P)
        l_bc = take(2, 2, P)
        l_pr = take(2, 8, P)
        l_at = take(2, 8, P)
        l_v1 = take(2, 512)
        l_v2 = take(2, 512)
        l_sk = take(512)
        l_o = l_in[:, J_Z:J_RQ]
        l_qe = take(9, P)
        l_s = take(4, NT, 16)

        take = carve()
        take(NT + 1, 8, HD)
        take(NT + 1, 8, HD)
        gain_row = take(D)
        r_w = take(DC, D)
        r_st = take(2, 8, HD)
        r_o = take(D)
        r_qe = take(9, P)
        r_g = take(D)
        r_gg = take(D)
        r_x = take(D)
        r_t = take(2, 512)
        r_t1, r_t2 = r_t[:, 0], r_t[:, 1]
        r_sq = take(D)
        r_y = take(D)
        r_yt = take(DC, P)
        r_gy = take(D)
        r_x1 = take(D)
        r_xn = take(D)
        r_ht = take(DC, P)
        r_junk = take(D)
        s_diag = [v.rearrange("p (a b) -> p a b", b=P) for v in (r_gy, r_xn)]

        DOWN_BANK = (3, 6, 7)
        take = carve()
        aff_t = take(T)[0:NE, :]
        e_wg = [take(DC, DE) for _ in range(2)]
        e_wu = [take(DC, DE) for _ in range(2)]
        e_wd = [take(FC, D) for _ in range(2)]
        e_x = take(D)
        e_xp = take(D)
        e_xt = take(DC, CAP_S + CAP_P)
        e_sg = take(FC, CAP_S + CAP_P)
        e_h = take(FC, CAP_S + CAP_P)
        e_y = take(D)
        e_yp = take(D)
        e_yt = take(DC, CAP_S + CAP_P)
        k_t = take(4, P)
        k_idx = take(2, NE)
        k_val = take(2, NE)
        e_i = take(2)
        e_g = take(2)
        k_m8 = take(8)
        k_i8 = take(8)
        k_j = take(2)
        k_red = take(NT)

        take = carve()
        f_g = take(D)
        f_x = take(2, D)
        f_y = take(2, D)
        f_junk = take(D)

        tick = ctx.enter_context(nc.semaphore("tick"))
        phase_end = ctx.enter_context(nc.semaphore("phase_end"))
        NPH = 6

        def barrier(eng, l, ph):
            eng.drain().then_inc(phase_end, 1)
            eng.wait_ge(phase_end, (l * NPH + ph) * 5)
            eng.sem_inc(tick, 1)

        class Link:

            def __init__(self, eng, name, n):
                self.eng, self.name, self.n, self.i = eng, name, n, 0

            def __call__(self, ins, last=False):
                self.i += 1
                ins.then_inc(sem[self.name], 1)
                if last:
                    assert self.i == signals[self.name].k, (self.name, self.i)
                else:
                    self.eng.wait_ge(sem[self.name], by(self.name, self.n, self.i))
                return ins

            def hold(self, ins):
                self(ins)
                self.eng.sem_inc(tick, 1)

        COUNTS = {
            "a_rows_in": 144, "gain_in": 48, "a_slab0_in": 16, "a_slab1_in": 16, "a_used": 2, "m_in": 32, "m_used": 2, "a_vecT": 1, "a_vecs": 1, "a_mod": 1,
            "a_scales": 2, "a_diag": 4, "a_rowmm": 4, "a_rowcp": 5,
            "p_x_in": 16, "p_ss": 1, "p_rv": 1, "p_rstd": 1, "p_xn": 1, "p_xT": 1, "p_hTd": 1, "p_hTa": 1,
            "p_mm": 7,
            "p_eva": 5,
            "p_evF": 1, "p_evV": 1,
            "p_f": 3, "p_proj_st": 16, "p_u_st": 16,
            "l_dt": 16, "l_de": 2, "l_bmm": 1, "l_bex": 1, "l_dec0": 1,
            "l_in": 32, "l_uin": 32, "l_g": 1, "l_halo": 1, "l_cv": 5, "l_silu": 1, "l_rope": 4, "l_rkb": 1,
            "l_v": 1, "l_sk": 1, "l_prf": 1, "l_T": 4, "l_ev1": 1, "l_ev2": 1,
            "l_ev3": 1, "l_ev3b": 1, "l_ev4": 1, "l_kk": 1, "l_BC": 1, "l_RA": 1, "l_bcm": 1, "l_ar": 1, "l_D": 4,
            "l_ex": 4, "l_E": 1, "l_ee": 1, "l_kb": 1, "l_pm": 2, "l_pe": 2, "l_at": 2, "l_xl": 2, "l_lv": 8,
            "l_lc": 15, "l_oS": 1, "l_oR": 1, "l_oeR": 1, "l_oeS": 1, "l_dS": 4, "l_incA": 2, "l_incD": 2,
            "l_qe": 2, "l_qc": 1, "l_ost": 16, "l_qst": 16,
            "s_in": 128, "s_init": 1, "s_fs": 14, "s_bs": 14, "s_out": 128, "r_w_in": 16, "s_zero": 1,
            "r_in": 48, "r_x_in": 16, "r_st": 1, "r_gg": 1, "r_i1": 1, "r_i2": 1, "r_o": 8, "r_sq": 1,
            "r_red": 2, "r_var": 1, "r_rs": 1, "r_y": 2, "r_yT": 2, "r_yt": 2, "r_out": 2, "r_gy": 2, "r_x1": 1,
            "r_ss": 1, "r_rv2": 1, "r_rs2": 1, "r_xn": 1, "r_xT": 2, "r_ht": 1, "r_lg": 1, "r_lgc": 1,
            "r_xst": 16, "r_nst": 16,
            "k_mx": 3, "k_e": 1, "k_soft": 3, "k_aT": 1, "k_at": 1, "k_r": 3, "k_done": 1, "k_T": 1, "k_ix": 1,
            "e_w0": 32, "e_w1": 32, "e_d0": 16, "e_d1": 16, "e_ic": 1, "e_jc": 1, "e_gc": 1, "e_xg": 32, "e_xT": 3, "e_xtd": 2,
            "e_xta": 1, "e_gu": 4, "e_sg": 4, "e_h": 4, "e_dn": 3, "e_yt": 3, "e_bk": 3, "e_y": 3, "e_sc": 16, "e_scp": 16,
        }
        for j, group in enumerate(W_GROUPS):
            COUNTS[f"w{j}"] = 16 * sum(len(W_BLOCKS[tag]) for tag in group)
        SWDGE = ("e_xg", "e_sc", "e_scp")
        for name, k in COUNTS.items():
            signals[name] = Signal(k, int(name not in SWDGE))
            sem[name] = ctx.enter_context(nc.semaphore(name))
        const_in, lb_in, cond_in, x_init, final_g_in = (
            ctx.enter_context(nc.semaphore(x)) for x in ("const_in", "lb_in", "cond_in", "x_init", "final_g_in"))
        dve_once, act_once, pool_once, primed = (
            ctx.enter_context(nc.semaphore(x)) for x in ("dve_once", "act_once", "pool_once", "primed"))

        def row_bc(v, n):
            return v.rearrange("(a n) -> a n", a=1).broadcast_to([P, n])

        def rows(h):
            return slice(64 * (h % 2), 64 * (h % 2) + 64)

        def halves(v, level, second):
            half = P >> (level + 1)
            lead = " ".join("xyz"[:len(v.shape) - 2])
            w = v.rearrange(f"p {lead} (n two i) -> p {lead} n two i", two=2, i=half)
            return w[(slice(None),) * (len(v.shape) - 1) + (slice(None), int(second), slice(None))]

        def tile_rows(t):
            return bass.ds(t * P, P)

        block = ctx.enter_context(nc.Block())

        @block.sync
        def _(sp):
            sp.dma_start(cst[:, :], const_f).then_inc(const_in, 16)
            sp.dma_start(a_mask, const_m).then_inc(const_in, 16)
            sp.dma_start(cond[:, :, 0], c_ctx.rearrange("(p c) -> p c", c=DC), allow_slow_non_contiguous=True).then_inc(cond_in, 16)
            sp.dma_start(cond[:, :, 1], c[0].rearrange("(p c) -> p c", c=DC), allow_slow_non_contiguous=True).then_inc(cond_in, 16)
            for l in range(DEPTH):
                sp.dma_start(a_lb[:, l, :], row_bc(hg_lb[l].rearrange("d w -> (d w)"), 512)).then_inc(lb_in, 16)
            sp.wait_ge(primed, 1)

            def load_x(t, n):
                sp.wait_ge(sem["p_xn"], before("p_xn", n))
                sp.sem_inc(tick, 1)
                sp.dma_start(p_x, x_d[tile_rows(t), :]).then_inc(sem["p_x_in"], 16)

            def store_u(t, n):
                sp.wait_ge(sem["p_eva"], by("p_eva", n, 1))
                sp.sem_inc(tick, 1)
                sp.dma_start(u_d.rearrange("u p t -> p u t")[:, :, bass.ds(t * P + 1, P)], p_u).then_inc(sem["p_u_st"], 16)

            def store_proj(t, n):
                sp.wait_ge(sem["p_f"], by("p_f", n))
                sp.sem_inc(tick, 1)
                sp.wait_ge(sem["p_evV"], by("p_evV", n))
                sp.sem_inc(tick, 1)
                sp.wait_ge(sem["p_eva"], by("p_eva", n, 4))
                sp.sem_inc(tick, 1)
                sp.dma_start(proj_d[tile_rows(t), :], p_out).then_inc(sem["p_proj_st"], 16)

            def load_w_in(l, g0, g1):
                for j in range(g0, g1):
                    for tag in W_GROUPS[j]:
                        o = 0
                        for c0, w in W_BLOCKS[tag]:
                            sp.dma_start(p_w[tag][:, :, o:o + w], w_in[l].rearrange("(c p) n -> p c n", p=P)[:, :, c0:c0 + w]).then_inc(sem[f"w{j}"], 16)
                            o += w

            def load_slab(l, t, i):
                m = l * (NT - 1) + t + 1
                if i:
                    sp.wait_ge(sem["m_used"], by("m_used", m, 1))
                else:
                    sp.wait_ge(sem["m_used"], before("m_used", m))
                sp.sem_inc(tick, 1)
                sp.dma_start(p_slab, w_ada[l].rearrange("(p c) n -> p c n", c=DC)[:, :, bass.ds(t * (2 * M_STEP) + (A_EARLY + i * M_STEP), M_STEP)])\
                    .then_inc(sem["m_in"], 16)

            def load_gate_up(l, e, p):
                sp.dma_start(e_wg[p], w_gate[l, e].rearrange("(c p) n -> p c n", p=P)).then_inc(sem[f"e_w{p}"], 16)
                sp.dma_start(e_wu[p], w_up[l, e].rearrange("(c p) n -> p c n", p=P)).then_inc(sem[f"e_w{p}"], 16)

            def load_down(l, e, p):
                sp.dma_start(e_wd[p], w_down[l, e].rearrange("(c p) n -> p c n", p=P)).then_inc(sem[f"e_d{p}"], 16)

            def load_early(t):
                sp.dma_start(l_in[:, J_RQ:J_RV], proj_d[tile_rows(t), J_RQ:J_RV]).then_inc(sem["l_uin"], 16)
                sp.dma_start(l_u, u_d.rearrange("u p t -> p u t")[:, :, bass.ds(t * P, P + 2)]).then_inc(sem["l_uin"], 16)

            def load_late(t):
                sp.dma_start(l_in[:, 0:J_Z], proj_d[tile_rows(t), 0:J_Z]).then_inc(sem["l_in"], 16)
                sp.dma_start(l_in[:, J_RV:J_N], proj_d[tile_rows(t), J_RV:J_N]).then_inc(sem["l_in"], 16)

            def store_queries(t, n):
                sp.wait_ge(sem["l_qe"], by("l_qe", n))
                sp.sem_inc(tick, 1)
                sp.wait_ge(sem["l_qc"], by("l_qc", n))
                sp.sem_inc(tick, 1)
                sp.dma_start(qe_d[t], l_qe.rearrange("p a b -> p (a b)")).then_inc(sem["l_qst"], 16)

            def store_local(t, n):
                sp.wait_ge(sem["l_oeR"], by("l_oeR", n))
                sp.sem_inc(tick, 1)
                sp.wait_ge(sem["l_oeS"], by("l_oeS", n))
                sp.sem_inc(tick, 1)
                sp.dma_start(o_d[tile_rows(t), :], l_o).then_inc(sem["l_ost"], 16)

            def load_mix(t, n):
                sp.wait_ge(sem["r_i2"], before("r_i2", n))
                sp.sem_inc(tick, 1)
                sp.wait_ge(sem["r_gg"], before("r_gg", n))
                sp.sem_inc(tick, 1)
                sp.wait_ge(sem["r_y"], before("r_y", n))
                sp.sem_inc(tick, 1)
                sp.dma_start(r_o, o_d[tile_rows(t), :]).then_inc(sem["r_in"], 16)
                sp.dma_start(r_qe.rearrange("p a b -> p (a b)"), qe_d[t]).then_inc(sem["r_in"], 16)
                sp.dma_start(r_g, proj_d[tile_rows(t), J_Z:J_RQ]).then_inc(sem["r_in"], 16)

            def load_res(t, n):
                sp.wait_ge(sem["r_x1"], before("r_x1", n))
                sp.sem_inc(tick, 1)
                sp.dma_start(r_x, x_d[tile_rows(t), :]).then_inc(sem["r_x_in"], 16)

            def store_rows(t, n):
                sp.wait_ge(sem["r_x1"], by("r_x1", n))
                sp.sem_inc(tick, 1)
                sp.dma_start(x_d[tile_rows(t), :], r_x1).then_inc(sem["r_xst"], 16)
                sp.wait_ge(sem["r_xn"], by("r_xn", n))
                sp.sem_inc(tick, 1)
                sp.dma_start(xn_d[tile_rows(t), :], r_xn).then_inc(sem["r_nst"], 16)

            with sp.Fori(0, DEPTH) as l:
                nl = l + 1
                for r0, r1, src in ((0, 8, norm1_g[l].rearrange("(b p) -> b p", p=P)), (8, 16, norm2_g[l].rearrange("(b p) -> b p", p=P)),
                                    (16, 64, b_ada[l].rearrange("(b p) -> b p", p=P)),
                                    (64, 82, ssd_conv_w[l].rearrange("j (b p) -> (j b) p", p=P)),
                                    (82, 88, ssd_conv_b[l].rearrange("(b p) -> b p", p=P))):
                    sp.dma_start(a_rows[r0:r1, :], src).then_inc(sem["a_rows_in"], 16)
                for dst, src, m in ((head_row[:, 0:16], ssd_dt_bias[l].rearrange("d h -> (d h)"), 16),
                                    (head_row[:, 16:32], ssd_a_log[l].rearrange("d h -> (d h)"), 16),
                                    (head_row[:, 32:40], ssd_d[l], 8)):
                    sp.dma_start(dst, row_bc(src, m)).then_inc(sem["a_rows_in"], 16)
                sp.dma_start(w_r[:, :, :], w_router[l].rearrange("(c p) e -> p c e", p=P)).then_inc(sem["a_rows_in"], 16)
                for i in range(2):
                    sp.dma_start(a_slab[i], w_ada[l].rearrange("(p c) n -> p c n", c=DC)[:, :, i * D:(i + 1) * D]).then_inc(sem[f"a_slab{i}_in"], 16)
                load_w_in(l, 0, 3)
                sp.wait_ge(sem["a_rows_in"], by("a_rows_in", nl))
                sp.sem_inc(tick, 1)
                sp.wait_ge(x_init, 64)
                sp.sem_inc(tick, 1)
                barrier(sp, l, 1)
                load_x(0, l * NT + 1)
                load_w_in(l, 3, 5)
                with sp.Fori(0, NT - 1) as t:
                    n = l * NT + t + 1
                    load_slab(l, t, 0)
                    store_u(t, n)
                    load_x(t + 1, n + 1)
                    load_slab(l, t, 1)
                    store_proj(t, n)
                store_u(NT - 1, l * NT + NT)
                store_proj(NT - 1, l * NT + NT)
                sp.wait_ge(sem["p_u_st"], by("p_u_st", l * NT + NT))
                sp.sem_inc(tick, 1)
                sp.wait_ge(sem["p_proj_st"], by("p_proj_st", l * NT + NT))
                sp.sem_inc(tick, 1)
                barrier(sp, l, 2)
                load_early(0)
                load_late(0)
                with sp.Fori(0, NT - 1) as t:
                    n = l * NT + t + 1
                    sp.wait_ge(sem["l_rope"], by("l_rope", n))
                    sp.sem_inc(tick, 1)
                    sp.wait_ge(sem["l_cv"], by("l_cv", n))
                    sp.sem_inc(tick, 1)
                    load_early(t + 1)
                    store_queries(t, n)
                    sp.wait_ge(sem["l_dS"], by("l_dS", n, 2))
                    sp.sem_inc(tick, 1)
                    load_late(t + 1)
                    store_local(t, n)
                store_queries(NT - 1, l * NT + NT)
                store_local(NT - 1, l * NT + NT)
                sp.wait_ge(sem["l_qst"], by("l_qst", l * NT + NT))
                sp.sem_inc(tick, 1)
                sp.wait_ge(sem["l_ost"], by("l_ost", l * NT + NT))
                sp.sem_inc(tick, 1)
                barrier(sp, l, 3)
                load_mix(0, l * NT + 1)
                for dst, src, m in ((gain_row[:, 0:256], hg_norm_g[l], 256), (gain_row[:, 256:768], ssd_norm_g[l], 512),
                                    (gain_row[:, 768:1024], ret_norm_g[l], 256)):
                    sp.dma_start(dst, row_bc(src, m)).then_inc(sem["gain_in"], 16)
                for d, slots, slot in ((0, st_f, 1), (1, st_b, 0)):
                    for b0, st in ((0, new_hg), (2, new_ret)):
                        sp.dma_start(st[0, l, d].rearrange("(q h) k v -> (h k) q v", h=2), slots[:, slot, b0:b0 + 2, :]).then_inc(sem["s_out"], 16)
                    for g in range(2):
                        sp.dma_start(new_ssd[0, l, d][4 * g:4 * g + 4].rearrange("a n p -> n a p"), slots[64 * g:64 * g + 64, slot, 4:8, :])\
                            .then_inc(sem["s_out"], 16)
                sp.wait_ge(sem["s_out"], by("s_out", nl))
                sp.sem_inc(tick, 1)
                for d, slots, slot in ((0, st_f, 1), (1, st_b, NT)):
                    for b0, st in ((0, state_hgrn), (2, state_ret)):
                        sp.dma_start(slots[:, slot, b0:b0 + 2, :], st[0, l, d].rearrange("(q h) k v -> (h k) q v", h=2)).then_inc(sem["s_in"], 16)
                    for g in range(2):
                        sp.dma_start(slots[64 * g:64 * g + 64, slot, 4:8, :], state_ssd[0, l, d][4 * g:4 * g + 4].rearrange("a n p -> n a p"))\
                            .then_inc(sem["s_in"], 16)
                sp.dma_start(r_w, w_out[l].rearrange("(c p) n -> p c n", p=P)).then_inc(sem["r_w_in"], 16)
                load_mix(1, l * NT + 2)
                load_res(0, l * NT + 1)
                with sp.Fori(1, NT - 1) as t:
                    n = l * NT + t + 1
                    load_mix(t + 1, n + 1)
                    load_res(t, n)
                    store_rows(t - 1, n - 1)
                load_res(NT - 1, l * NT + NT)
                store_rows(NT - 2, l * NT + NT - 1)
                store_rows(NT - 1, l * NT + NT)
                sp.wait_ge(sem["r_xst"], by("r_xst", l * NT + NT))
                sp.sem_inc(tick, 1)
                sp.wait_ge(sem["r_nst"], by("r_nst", l * NT + NT))
                sp.sem_inc(tick, 1)
                barrier(sp, l, 4)
                for p in range(2):
                    load_gate_up(l, p, p)
                    load_down(l, p, p)
                barrier(sp, l, 5)
                with sp.Fori(1, NE // 2) as j:
                    for p in range(2):
                        n = l * NE + 2 * j + p + 1
                        sp.wait_ge(sem["e_gu"], before("e_gu", n - 1))
                        sp.sem_inc(tick, 1)
                        load_gate_up(l, 2 * j + p, p)
                        sp.wait_ge(sem["e_dn"], before("e_dn", n - 1))
                        sp.sem_inc(tick, 1)
                        load_down(l, 2 * j + p, p)
                barrier(sp, l, 6)
            sp.dma_start(f_g, row_bc(final_g, D)).then_inc(final_g_in, 16)
            sp.dma_start(f_x[:, 0], x_d[tile_rows(0), :]).then_inc(sem["p_x_in"], 16)
            for t in range(NT):
                n = DEPTH * NT + t + 1
                if t + 1 < NT:
                    sp.wait_ge(sem["p_ss"], by("p_ss", n))
                    sp.sem_inc(tick, 1)
                    sp.wait_ge(sem["p_evF"], before("p_evF", n))
                    sp.sem_inc(tick, 1)
                    sp.dma_start(f_x[:, (t + 1) % 2], x_d[tile_rows(t + 1), :]).then_inc(sem["p_x_in"], 16)
                sp.wait_ge(sem["p_evF"], by("p_evF", n))
                sp.sem_inc(tick, 1)
                dst = y_prompt[0] if t == 0 else y_sample[0][(t - 1) * P:t * P, :]
                sp.dma_start(dst, f_y[:, t % 2]).then_inc(sem["p_u_st"], 16)
            sp.wait_ge(sem["p_u_st"], by("p_u_st", DEPTH * NT + NT))
            sp.sem_inc(tick, 1)

        @block.tensor
        def _(pe):
            def turn(out, in_, k=P):
                return pe.transpose(out, in_, cst[0:k, C_ID:C_ID + k])

            def condition(slab, width, bk, c0):
                for b in range(width // P):
                    for ch in range(DC):
                        mm = pe.matmul(bank[:, bk, c0 + 2 * b:c0 + 2 * b + 2], slab[:, ch, b * P:(b + 1) * P], cond[:, ch, :],
                                       start=(ch == 0), stop=(ch == DC - 1))
                return mm

            def turn_x(n):
                pe.wait_ge(sem["p_xn"], by("p_xn", n))
                for ch in range(DC):
                    mm = turn(bank[:, ch // 4, (ch % 4) * P:(ch % 4 + 1) * P], p_xn[:, ch * P:(ch + 1) * P])
                mm.then_inc(sem["p_xT"], 1)

            def tile_p(nl, n, m, p):
                pe.wait_ge(sem["p_hTd"], by("p_hTd", n))
                pe.wait_ge(sem["p_hTa"], by("p_hTa", n))
                pe.wait_ge(sem["w0"], by("w0", nl))
                for b in range(UC):
                    for ch in range(DC):
                        mm = pe.matmul(bank[:, b // 4, (b % 4) * P:(b % 4 + 1) * P], p_w["U"][:, ch, b * P:(b + 1) * P],
                                       p_h[p][:, ch, :], start=(ch == 0), stop=(ch == DC - 1))
                mm.then_inc(sem["p_mm"], 1)
                for bk, tag in ((2, "A"), (4, "C"), (5, "G"), (3, "B"), (6, "F"), (7, "V")):
                    group = [tag in g for g in W_GROUPS].index(True)
                    taken = "p_ev" + tag if tag in "FV" else "p_eva"
                    pe.wait_ge(sem[taken], before(taken, n))
                    if m is not None and tag in "GV":
                        pe.wait_ge(sem["m_in"], by("m_in", m, 16 if tag == "G" else 32))
                        if tag == "G":
                            pe.wait_ge(sem["p_evV"], before("p_evV", n))
                        condition(p_slab, M_STEP, 7, 272 + 4 * int(tag == "V")).then_inc(sem["m_used"], 1)
                    if m is not None and tag == "V":
                        pe.wait_ge(sem["p_eva"], by("p_eva", n, 1))
                        turn_x(n + 1)
                    pe.wait_ge(sem[f"w{group}"], by(f"w{group}", nl))
                    for ch in range(DC):
                        w = p_w[tag][:, ch, :]
                        mm = pe.matmul(bank[:, bk, 0:w.shape[-1]], p_h[p][:, ch, :], w, start=(ch == 0), stop=(ch == DC - 1))
                    mm.then_inc(sem["p_mm"], 1)

            def turn_rows(n):
                pe.wait_ge(sem["e_xg"], by("e_xg", n))
                for q in range(2):
                    for i in range(4):
                        mm = turn(bank[:, q, i * P:(i + 1) * P], e_x[:, (4 * q + i) * P:(4 * q + i + 1) * P])
                    mm.then_inc(sem["e_xT"], 1)
                for ch in range(DC):
                    mm = turn(bank[:, 2, ch * CAP_P:(ch + 1) * CAP_P], e_xp[0:CAP_P, ch * P:(ch + 1) * P], CAP_P)
                mm.then_inc(sem["e_xT"], 1)

            def gate_up(n, m, p):
                pe.wait_ge(sem["e_xtd"], by("e_xtd", n))
                pe.wait_ge(sem["e_xta"], by("e_xta", n))
                pe.wait_ge(sem[f"e_w{p}"], by(f"e_w{p}", m))
                pe.wait_ge(sem["e_h"], before("e_h", n))
                for f in range(FC):
                    if f == 0:
                        pe.wait_ge(sem["e_yt"], before("e_yt", n))
                    if f == 3:
                        pe.wait_ge(sem["e_y"], before("e_y", n))
                    for o, w in ((0, e_wg[p]), (256, e_wu[p])):
                        for ch in range(DC):
                            mm = pe.matmul(bank[:, 4 + f, o:o + CAP_S + CAP_P], w[:, ch, f * P:(f + 1) * P], e_xt[:, ch, :],
                                           start=(ch == 0), stop=(ch == DC - 1))
                    mm.then_inc(sem["e_gu"], 1)

            def down(n, m, p, next_n):
                pe.wait_ge(sem["e_h"], by("e_h", n))
                pe.wait_ge(sem[f"e_d{p}"], by(f"e_d{p}", m))
                for ch in range(DC):
                    for f in range(FC):
                        o = (ch % 3) * (CAP_S + CAP_P)
                        mm = pe.matmul(bank[:, DOWN_BANK[ch // 3], o:o + CAP_S + CAP_P], e_wd[p][:, f, ch * P:(ch + 1) * P], e_h[:, f, :],
                                       start=(f == 0), stop=(f == FC - 1))
                    if ch % 3 == 2 or ch == DC - 1:
                        mm.then_inc(sem["e_dn"], 1)
                pe.wait_ge(sem["e_xta"], by("e_xta", next_n))
                pe.wait_ge(sem["e_xtd"], by("e_xtd", next_n))
                for ch in range(DC):
                    if ch % 3 == 0:
                        pe.wait_ge(sem["e_yt"], by("e_yt", n, ch // 3 + 1))
                    mm = turn(bank[:, ch // 4, (ch % 4) * P:(ch % 4 + 1) * P], e_yt[:, ch, 0:CAP_S])
                    if ch % 4 == 3:
                        mm.then_inc(sem["e_bk"], 1)
                for ch in range(DC):
                    mm = turn(bank[0:CAP_P, 2 + ch // 4, (ch % 4) * P:(ch % 4 + 1) * P], e_yt[:, ch, CAP_S:])
                mm.then_inc(sem["e_bk"], 1)

            def inter(n):
                pe.wait_ge(sem["r_in"], by("r_in", n))
                pe.wait_ge(sem["r_st"], by("r_st", n))
                pe.wait_ge(sem["r_o"], before("r_o", n))
                for b in range(4):
                    for h in range(2):
                        for d in range(2):
                            mm = pe.matmul(bank[:, 7 * h, b * HD:(b + 1) * HD], r_qe[rows(h), d * 4 + b, :], r_st[rows(h), d, b, :],
                                           start=(d == 0), stop=(d == 1))
                mm.then_inc(sem["r_i1"], 1)
                for d in range(2):
                    for g in range(2):
                        mm = pe.matmul(bank[:, 1 + g, d * 256:(d + 1) * 256], r_qe[rows(g), 8, :], r_st[rows(g), d, 4:8, :], start=True, stop=True)
                mm.then_inc(sem["r_i2"], 1)

            def turn_y(n):
                pe.wait_ge(sem["r_y"], by("r_y", n))
                pe.wait_ge(sem["r_yt"], before("r_yt", n))
                for half in range(2):
                    for i in range(4):
                        ch = half * 4 + i
                        mm = turn(bank[:, 3 + half, i * P:(i + 1) * P], r_y[:, ch * P:(ch + 1) * P])
                    mm.then_inc(sem["r_yT"], 1)

            def project(n, half):
                pe.wait_ge(sem["r_yt"], by("r_yt", n))
                pe.wait_ge(sem["r_gy"], before("r_gy", n))
                for ch in range(DC):
                    mm = pe.matmul(bank[:, 5 + half, :], r_yt[:, ch, :], r_w[:, ch, half * 512:(half + 1) * 512], start=(ch == 0), stop=(ch == DC - 1))
                mm.then_inc(sem["r_out"], 1)

            def turn_xn(n):
                pe.wait_ge(sem["r_xn"], by("r_xn", n))
                for half in range(2):
                    for i in range(4):
                        ch = half * 4 + i
                        mm = turn(bank[:, 7 * half, i * P:(i + 1) * P], r_xn[:, ch * P:(ch + 1) * P])
                    mm.then_inc(sem["r_xT"], 1)

            def router(n):
                pe.wait_ge(sem["r_ht"], by("r_ht", n))
                for ch in range(DC):
                    mm = pe.matmul(bank[:, 1, 0:NE], r_ht[:, ch, :], w_r[:, ch, :], start=(ch == 0), stop=(ch == DC - 1))
                mm.then_inc(sem["r_lg"], 1)

            pe.wait_ge(const_in, 32)
            pe.wait_ge(act_once, 1)
            pe.wait_ge(primed, 1)
            with pe.Fori(0, DEPTH) as l:
                nl = l + 1
                pe.wait_ge(sem["a_rows_in"], by("a_rows_in", nl))
                turn(bank[:, 0, 0:88], a_rows[0:88, :], 88).then_inc(sem["a_vecT"], 1)
                for q in range(4):
                    if q % 2 == 0:
                        pe.wait_ge(sem[f"a_slab{q // 2}_in"], by(f"a_slab{q // 2}_in", nl))
                    for ch in range(DC):
                        mm = pe.matmul(bank[0:2, 2 + q, :], cond[:, ch, :], a_slab[q // 2][:, ch, (q % 2) * 512:(q % 2 + 1) * 512],
                                       start=(ch == 0), stop=(ch == DC - 1))
                mm.then_inc(sem["a_used"], 1)
                pe.wait_ge(sem["a_rowcp"], by("a_rowcp", nl, 1))
                pe.sem_inc(tick, 1)
                for b in range(A_EARLY // P):
                    mm = turn(bank[:, 1, 2 * b:2 * b + 2], a_row[:, b * P:(b + 1) * P], 2)
                mm.then_inc(sem["a_used"], 1)
                barrier(pe, l, 1)

                turn_x(l * NT + 1)
                with pe.Fori(0, NT // 2) as j:
                    for p in range(2):
                        tile_p(nl, l * NT + 2 * j + p + 1, l * (NT - 1) + 2 * j + p + 1, p)
                tile_p(nl, l * NT + NT, None, 0)
                barrier(pe, l, 2)

                pe.wait_ge(sem["l_dt"], by("l_dt", nl))
                pe.matmul(bank[:, 0, 0:72], tri[:, LE, :], la_all[:, :, 0:8], start=True, stop=True)
                pe.matmul(bank[:, 0, 72:144], tri[:, GE, :], la_all[:, :, 8:16], start=True, stop=True)
                pe.matmul(bank[:, 1, 0:72], tri[:, GT, :], la_all[:, :, 0:8], start=True, stop=True)
                pe.matmul(bank[:, 1, 72:144], tri[:, LT, :], la_all[:, :, 8:16], start=True, stop=True)
                pe.matmul(bank[:, 2, 0:144], ones, la_all[:, :, :], start=True, stop=True).then_inc(sem["l_bmm"], 1)
                pe.wait_ge(sem["l_bex"], by("l_bex", nl))
                pe.sem_inc(tick, 1)
                with pe.Fori(0, NT) as t:
                    n = l * NT + t + 1
                    pe.wait_ge(sem["l_in"], by("l_in", n))
                    pe.wait_ge(sem["l_incA"], before("l_incA", n))
                    for i in range(4):
                        mm = turn(bank[:, 0, i * P:(i + 1) * P], l_in[:, (J_Q if i < 2 else J_K - 256) + i * P:][:, :P])
                    mm.then_inc(sem["l_T"], 1)
                    for i in range(2):
                        mm = turn(bank[:, 1, i * P:(i + 1) * P], l_in[:, J_K + 256 + i * P:][:, :P])
                    mm.then_inc(sem["l_T"], 1)

                    def levels(d, pair, b0):
                        for half in range(2):
                            mm = pe.matmul(bank[:, b0 + half, :], l_g[:, d * 256 + pair * P:][:, :P], lev[:, d, 4 * half:4 * half + 4, :],
                                           start=True, stop=True)
                        mm.then_inc(sem["l_D"], 1)

                    pe.wait_ge(sem["l_g"], by("l_g", n))
                    pe.wait_ge(sem["l_lc"], before("l_lc", n))
                    levels(0, 0, 6)
                    pe.wait_ge(sem["l_ev1"], by("l_ev1", n))
                    pe.wait_ge(sem["l_ev2"], by("l_ev2", n))
                    levels(0, 1, 0)
                    pe.wait_ge(sem["l_rope"], by("l_rope", n))
                    pe.wait_ge(sem["l_oeR"], before("l_oeR", n))
                    for i in range(4):
                        mm = turn(bank[:, 4, i * P:(i + 1) * P], l_rot[:, i * P:(i + 1) * P])
                    mm.then_inc(sem["l_T"], 1)
                    pe.wait_ge(sem["l_incD"], before("l_incD", n))
                    levels(1, 0, 2)
                    pe.wait_ge(sem["l_ex"], by("l_ex", n, 1))
                    levels(1, 1, 6)
                    pe.wait_ge(sem["l_silu"], by("l_silu", n))
                    pe.wait_ge(sem["l_ex"], by("l_ex", n, 2))
                    for i in range(5):
                        mm = turn(bank[:, i // 4, (i % 4) * P:(i % 4 + 1) * P], l_c[:, i, :])
                    mm.then_inc(sem["l_T"], 1)
                    pe.wait_ge(sem["l_oeS"], before("l_oeS", n))
                    pe.wait_ge(sem["l_ev4"], by("l_ev4", n))
                    for g in range(2):
                        mm = pe.matmul(bank[:, 5 - g, 0:P], l_c[rows(g), 4, :], l_c[rows(g), 5, :], start=True, stop=True)
                    mm.then_inc(sem["l_BC"], 1)
                    for h in range(4):
                        mm = pe.matmul(bank[:, 5 - h % 2, (2 + h // 2) * P:(3 + h // 2) * P], l_rqk[rows(h), 2 + h // 2, :], l_rqk[rows(h), h // 2, :],
                                       start=True, stop=True)
                    mm.then_inc(sem["l_RA"], 1)
                    pe.wait_ge(sem["l_prf"], by("l_prf", n))
                    pe.wait_ge(sem["l_ev3"], by("l_ev3", n))
                    pe.wait_ge(sem["l_ev3b"], by("l_ev3b", n))
                    for d in range(2):
                        if d:
                            pe.wait_ge(sem["l_ex"], by("l_ex", n, 3))
                        for g in range(2):
                            mm = pe.matmul(bank[:, 2 * d + g, :], tri[:, GT + d, :], l_pr[:, d, 4 * g:4 * g + 4, :], start=True, stop=True)
                        mm.then_inc(sem["l_pm"], 1)
                    pe.wait_ge(sem["l_ar"], by("l_ar", n))
                    pe.matmul(bank[:, 5, 0:256], tri[:, GT, :], l_g[:, 0:256], start=True, stop=True)
                    pe.matmul(bank[:, 5, 256:512], tri[:, LT, :], l_g[:, 256:512], start=True, stop=True).then_inc(sem["l_E"], 1)
                    pe.wait_ge(sem["l_ex"], by("l_ex", n, 4))
                    pe.wait_ge(sem["l_kk"], by("l_kk", n))
                    for i in range(8):
                        bk = 6 if i % 2 == 0 else 0
                        if i == 1:
                            pe.wait_ge(sem["l_pe"], by("l_pe", n, 1))
                            pe.wait_ge(sem["l_xl"], by("l_xl", n))
                        if i >= 2:
                            pe.wait_ge(sem["l_lc"], by("l_lc", n, 2 * i - 3))
                        for h in range(4):
                            if i == 0:
                                mm = pe.matmul(bank[:, bk + h % 2, (h // 2) * P:(h // 2 + 1) * P], l_kk[rows(h), h // 2, :], l_q[rows(h), h // 2, :],
                                               start=True, stop=True)
                                continue
                            for d in range(2):
                                x = l_xl[rows(h), d, h // 2, i - 1, :]
                                mm = pe.matmul(bank[:, bk + h % 2, (2 * d + h // 2) * P:(2 * d + h // 2 + 1) * P], x, x, start=True, stop=True)
                        mm.then_inc(sem["l_lv"], 1)
                    for h in (4, 5, 6, 7, 0, 1, 2, 3):
                        if h == 0:
                            pe.wait_ge(sem["l_lc"], by("l_lc", n))
                        a, v = (l_ah, J_V) if h < 4 else (l_ar, J_RV)
                        mm = pe.matmul(bank[:, 4, h * HD:(h + 1) * HD], a[:, h % 4, :], l_in[:, v + (h % 4) * HD:][:, :HD], start=True, stop=True)
                    mm.then_inc(sem["l_oR"], 1)
                    pe.wait_ge(sem["l_kb"], by("l_kb", n))
                    pe.wait_ge(sem["l_rkb"], by("l_rkb", n))
                    for bk, kb, v in ((0, l_kb, J_V), (1, l_rkb, J_RV)):
                        for i in range(4):
                            mm = pe.matmul(bank[:, bk, i * P:(i + 1) * P], kb[:, i * P:(i + 1) * P], l_in[:, v + (i % 2) * P:][:, :P], start=True, stop=True)
                        mm.then_inc(sem["l_dS"], 1)
                    pe.wait_ge(sem["l_ee"], by("l_ee", n))
                    pe.wait_ge(sem["l_at"], by("l_at", n))
                    pe.wait_ge(sem["l_v"], by("l_v", n))
                    for h in range(8):
                        for d in range(2):
                            mm = pe.matmul(bank[:, 5, h * HD:(h + 1) * HD], l_at[:, d, h, :], l_v1[:, d, h * HD:(h + 1) * HD], start=(d == 0), stop=(d == 1))
                    mm.then_inc(sem["l_oS"], 1)
                    for d in range(2):
                        pe.matmul(bank[:, 2 + d, :], l_tm[:, 4, :], l_v2[:, d, :], start=True, stop=True).then_inc(sem["l_dS"], 1)
                barrier(pe, l, 3)

                for i in range(4):
                    if i == 2:
                        inter(l * NT + 1)
                    pe.wait_ge(sem["a_diag"], by("a_diag", nl, i + 1))
                    if i >= 2:
                        pe.wait_ge(sem["a_rowcp"], by("a_rowcp", nl, i))
                    for half in range(2):
                        mm = pe.matmul(bank[:, 3 + 2 * (i % 2) + half, :], ones, s_diag[i % 2][:, 4 * half:4 * half + 4, :], start=True, stop=True)
                    mm.then_inc(sem["a_rowmm"], 1)
                pe.wait_ge(sem["r_w_in"], by("r_w_in", nl))
                pe.wait_ge(sem["a_rowcp"], by("a_rowcp", nl))
                inter(l * NT + 2)
                turn_y(l * NT + 1)
                project(l * NT + 1, 0)
                project(l * NT + 1, 1)
                with pe.Fori(1, NT - 1) as t:
                    n = l * NT + t + 1
                    pe.wait_ge(sem["r_lgc"], before("r_lgc", n - 1))
                    inter(n + 1)
                    turn_y(n)
                    project(n, 0)
                    turn_xn(n - 1)
                    project(n, 1)
                    router(n - 1)
                turn_y(l * NT + NT)
                project(l * NT + NT, 0)
                turn_xn(l * NT + NT - 1)
                project(l * NT + NT, 1)
                router(l * NT + NT - 1)
                turn_xn(l * NT + NT)
                router(l * NT + NT)
                barrier(pe, l, 4)

                pe.wait_ge(sem["k_soft"], by("k_soft", nl))
                for i in range(NT):
                    mm = turn(bank[0:NE, 1 + i // 4, (i % 4) * P:(i % 4 + 1) * P], lg_all[:, i, :])
                mm.then_inc(sem["k_aT"], 1)
                pe.wait_ge(sem["k_done"], by("k_done", nl))
                for i in range(4):
                    mm = turn(bank[:, 0, i * P:(i + 1) * P], k_t[:, i, :])
                mm.then_inc(sem["k_T"], 1)
                barrier(pe, l, 5)

                turn_rows(l * NE + 1)
                with pe.Fori(0, NE // 2 - 1) as j:
                    for p in range(2):
                        n, m = l * NE + 2 * j + p + 1, l * (NE // 2) + j + 1
                        gate_up(n, m, p)
                        turn_rows(n + 1)
                        down(n, m, p, n + 1)
                gate_up(l * NE + NE - 1, (l + 1) * (NE // 2), 0)
                turn_rows(l * NE + NE)
                down(l * NE + NE - 1, (l + 1) * (NE // 2), 0, l * NE + NE)
                gate_up(l * NE + NE, (l + 1) * (NE // 2), 1)
                down(l * NE + NE, (l + 1) * (NE // 2), 1, l * NE + NE)
                barrier(pe, l, 6)

        @block.scalar
        def _(act):
            def ev(out, in_, func=ACT.Copy, **kw):
                return act.activation(out, in_, func, **kw)

            act.dma_start(x_d[0:SEQ, :], x_prompt[0]).then_inc(x_init, 16)
            act.dma_start(x_d[SEQ:T, :], x_sample[0]).then_inc(x_init, 16)
            act.wait_ge(cond_in, 32)
            ev(cond[:, :, :], cond[:, :, :], ACT.Silu).then_inc(act_once, 1)
            act.wait_ge(const_in, 32)
            act.sem_inc(tick, 1)
            for col in (0, T + 1):
                act.dma_start(u_d.rearrange("u p t -> p u t")[:, :, col:col + 1], cst[:, C_SIN:C_SIN + UC].unsqueeze(2),
                              allow_slow_non_contiguous=True).then_inc(x_init, 16)
            act.wait_ge(dve_once, 3)
            for j in range(DEPTH):
                ev(a_lbt[:, 1 + j, :], a_lbt[:, 1 + j, :], ACT.Exp).then_inc(act_once, 1)
            act.wait_ge(primed, 1)

            def square_x(n):
                act.wait_ge(sem["p_x_in"], by("p_x_in", n))
                act.wait_ge(sem["p_rv"], before("p_rv", n))
                act.wait_ge(sem["p_xT"], before("p_xT", n))
                ev(p_xn, p_x, ACT.Square, accum_out=small[:, 0:1]).then_inc(sem["p_ss"], 1)

            def turn_p(t, n, more, p):
                act.wait_ge(sem["p_xT"], by("p_xT", n))
                act.sem_inc(tick, 1)
                for ch in range(4, DC):
                    last = ev(p_h[p][:, ch, :], bank[:, 1, (ch - 4) * P:(ch - 3) * P], ACT.Identity,
                              scale=scale1[:, t, ch:ch + 1], bias=shift1[:, t, ch:ch + 1])
                last.then_inc(sem["p_hTa"], 1)
                act.wait_ge(sem["p_mm"], by("p_mm", n, 1))
                act.wait_ge(sem["p_u_st"], before("p_u_st", n))
                ev(p_u[:, 0:4, :], bank[:, 0, :].rearrange("p (a b) -> p a b", a=4))
                ev(p_u[:, 4:6, :], bank[:, 1, 0:256].rearrange("p (a b) -> p a b", a=2)).then_inc(sem["p_eva"], 1)
                act.wait_ge(sem["p_mm"], by("p_mm", n, 2))
                act.wait_ge(sem["p_proj_st"], before("p_proj_st", n))
                ev(p_out[:, J_V:J_V + 256], bank[:, 2, 256:512])
                ev(p_out[:, J_Q:J_Q + 256], bank[:, 2, 0:256], ACT.Silu).then_inc(sem["p_eva"], 1)
                act.wait_ge(sem["p_mm"], by("p_mm", n, 3))
                ev(p_out[:, J_Z:J_Z + 512], bank[:, 4, :], ACT.Silu).then_inc(sem["p_eva"], 1)
                if more:
                    square_x(n + 1)
                act.wait_ge(sem["p_mm"], by("p_mm", n, 4))
                ev(p_out[:, J_G:J_G + 512], bank[:, 5, :], ACT.Silu).then_inc(sem["p_eva"], 1)
                act.wait_ge(sem["p_mm"], by("p_mm", n, 5))
                ev(p_out[:, J_F:J_F + 512], bank[:, 3, :], ACT.Sigmoid)
                ev(p_out[:, J_K:J_K + 512], bank[:, 3, :], ACT.Sigmoid, scale=-1.0).then_inc(sem["p_eva"], 1)

            def silu_conv(n):
                act.wait_ge(sem["l_cv"], by("l_cv", n))
                for b in range(UC):
                    last = ev(l_c[:, b, :], l_c[:, b, :], ACT.Silu, bias=vecs[:, 82 + b:83 + b])
                last.then_inc(sem["l_silu"], 1)

            def tile_l(t, n, more):
                act.wait_ge(sem["l_in"], by("l_in", n))
                act.wait_ge(sem["l_E"], before("l_E", n))
                ev(l_g, l_in[:, J_F:J_F + 512], ACT.Ln).then_inc(sem["l_g"], 1)
                act.wait_ge(sem["l_T"], by("l_T", n, 1))
                act.wait_ge(sem["l_xl"], before("l_xl", n))
                act.wait_ge(sem["l_qe"], before("l_qe", n))
                act.wait_ge(sem["l_lv"], before("l_lv", n))
                ev(l_q, bank[:, 0, 0:256].rearrange("p (a b) -> p a b", a=2), scale=HD ** -0.5)
                ev(l_k[:, 0], bank[:, 0, 256:512].rearrange("p (a b) -> p a b", a=2)).then_inc(sem["l_ev1"], 1)
                for i, (d, pair, b0) in enumerate(((0, 0, 6), (0, 1, 0), (1, 0, 2), (1, 1, 6))):
                    act.wait_ge(sem["l_D"], by("l_D", n, i + 1))
                    ev(l_ex[:, d, pair].rearrange("p a b -> p (a b)"), bank[:, b0:b0 + 2, :].rearrange("p a b -> p (a b)"), ACT.Exp)\
                        .then_inc(sem["l_ex"], 1)
                act.wait_ge(sem["l_T"], by("l_T", n, 4))
                act.wait_ge(sem["l_v"], before("l_v", n))
                act.wait_ge(sem["l_sk"], before("l_sk", n))
                act.wait_ge(sem["l_dS"], before("l_dS", n))
                ev(l_tm[:, 0:4, :], bank[:, 0, :].rearrange("p (a b) -> p a b", a=4)).then_inc(sem["l_ev3"], 1)
                for d in range(2):
                    act.wait_ge(sem["l_pm"], by("l_pm", n, d + 1))
                    act.wait_ge(sem["l_oS"], before("l_oS", n))
                    ev(l_at[:, d].rearrange("p a b -> p (a b)"), bank[:, 2 * d:2 * d + 2, :].rearrange("p a b -> p (a b)"), ACT.Exp)\
                        .then_inc(sem["l_pe"], 1)
                act.wait_ge(sem["l_E"], by("l_E", n))
                act.wait_ge(sem["l_kb"], before("l_kb", n))
                ev(l_ee, bank[:, 5, :], ACT.Exp).then_inc(sem["l_ee"], 1)
                if more:
                    silu_conv(n + 1)
                act.wait_ge(sem["l_oR"], by("l_oR", n))
                act.wait_ge(sem["l_ost"], before("l_ost", n))
                ev(l_o[:, 0:256], bank[:, 4, 0:256])
                ev(l_o[:, 768:1024], bank[:, 4, 256:512]).then_inc(sem["l_oeR"], 1)
                for i in range(2):
                    act.wait_ge(sem["l_dS"], by("l_dS", n, i + 1))
                    act.sem_inc(tick, 1)
                    for g in range(2):
                        src = bank[rows(g), i, :].rearrange("p (d q v) -> p d q v", d=2, q=2)[:, :, :, 64 * g:64 * g + 64]
                        ev(st_f[rows(g), t + 1, 2 * i:2 * i + 2, :], src[:, 0])
                        last = ev(st_b[rows(g), t, 2 * i:2 * i + 2, :], src[:, 1])
                    last.then_inc(sem["l_incA"], 1)

            def modulate_a(n):
                act.wait_ge(sem["e_xT"], by("e_xT", n, 2))
                act.wait_ge(sem["e_gu"], before("e_gu", n))
                for ch in range(4, DC):
                    last = ev(e_xt[:, ch, 0:CAP_S], bank[:, 1, (ch - 4) * P:(ch - 3) * P], ACT.Identity,
                              scale=scale2[:, 1, ch:ch + 1], bias=shift2[:, 1, ch:ch + 1])
                last.then_inc(sem["e_xta"], 1)

            def silu_gate(n):
                for f in range(FC):
                    act.wait_ge(sem["e_gu"], by("e_gu", n, f + 1))
                    act.wait_ge(sem["e_h"], before("e_h", n))
                    ev(e_sg[:, f, :], bank[:, 4 + f, 0:CAP_S + CAP_P], ACT.Silu).then_inc(sem["e_sg"], 1)

            def take_down(n):
                for i, bk in enumerate(DOWN_BANK):
                    m = min(3, DC - 3 * i)
                    act.wait_ge(sem["e_dn"], by("e_dn", n, i + 1))
                    act.wait_ge(sem["e_bk"], before("e_bk", n))
                    ev(e_yt[:, 3 * i:3 * i + m, :], bank[:, bk, 0:m * (CAP_S + CAP_P)].rearrange("p (a b) -> p a b", a=m)).then_inc(sem["e_yt"], 1)

            def squares_o(n):
                act.wait_ge(sem["r_o"], by("r_o", n))
                act.wait_ge(sem["r_red"], before("r_red", n))
                ev(r_sq, r_o, ACT.Square).then_inc(sem["r_sq"], 1)

            def take_yT(n):
                for half in range(2):
                    act.wait_ge(sem["r_yT"], by("r_yT", n, half + 1))
                    act.wait_ge(sem["r_out"], before("r_out", n))
                    ev(r_yt[:, 4 * half:4 * half + 4, :], bank[:, 3 + half, :].rearrange("p (a b) -> p a b", a=4)).then_inc(sem["r_yt"], 1)

            def squares_x(n):
                act.wait_ge(sem["r_x1"], by("r_x1", n))
                act.wait_ge(sem["r_rv2"], before("r_rv2", n))
                ev(r_junk, r_x1, ACT.Square, accum_out=small[:, 0:1]).then_inc(sem["r_ss"], 1)

            with act.Fori(0, DEPTH) as l:
                nl = l + 1
                act.wait_ge(sem["a_used"], by("a_used", nl, 1))
                ev(a_row, bank[0:2, 2:6, :].rearrange("p a b -> p (a b)")).then_inc(sem["a_rowcp"], 1)
                act.wait_ge(sem["a_rows_in"], by("a_rows_in", nl))
                ev(small[:, 40:56], head_row[:, 16:32], ACT.Exp).then_inc(act_once, 1)
                barrier(act, l, 1)
                square_x(l * NT + 1)
                with act.Fori(0, NT // 2) as j:
                    for p in range(2):
                        turn_p(2 * j + p, l * NT + 2 * j + p + 1, True, p)
                turn_p(NT - 1, l * NT + NT, False, 0)
                barrier(act, l, 2)
                act.wait_ge(sem["l_de"], by("l_de", nl))
                ev(l_s[:, 1], l_s[:, 1], ACT.Exp).then_inc(act_once, 1)
                act.wait_ge(sem["l_bmm"], by("l_bmm", nl))
                for d in range(2):
                    ev(eb_all[:, :, 8 * d:8 * d + 8], bank[:, 0, 72 * d:72 * d + 72].rearrange("p (a b) -> p a b", b=8), ACT.Exp)
                    ev(l_s[:, 2, :, 8 * d:8 * d + 8], bank[:, 1, 72 * d:72 * d + 72].rearrange("p (a b) -> p a b", b=8), ACT.Exp)
                ev(etot[:, :, :], bank[:, 2, 0:144].rearrange("p (a b) -> p a b", b=16), ACT.Exp).then_inc(sem["l_bex"], 1)
                silu_conv(l * NT + 1)
                with act.Fori(0, NT - 1) as t:
                    tile_l(t, l * NT + t + 1, True)
                tile_l(NT - 1, l * NT + NT, False)
                barrier(act, l, 3)
                for i in range(4):
                    if i == 2:
                        squares_o(l * NT + 1)
                    act.wait_ge(sem["a_rowmm"], by("a_rowmm", nl, i + 1))
                    b0 = 3 + 2 * (i % 2)
                    ev(gate_row[:, i // 2, i % 2, :], bank[:, b0:b0 + 2, :].rearrange("p a b -> p (a b)")).then_inc(sem["a_rowcp"], 1)
                take_yT(l * NT + 1)
                squares_o(l * NT + 2)
                squares_x(l * NT + 1)
                with act.Fori(1, NT - 1) as t:
                    n = l * NT + t + 1
                    take_yT(n)
                    squares_o(n + 1)
                    squares_x(n)
                take_yT(l * NT + NT)
                squares_x(l * NT + NT)
                barrier(act, l, 4)
                act.wait_ge(sem["k_mx"], by("k_mx", nl))
                ev(lg_all[:, :, :], lg_all[:, :, :], ACT.Exp).then_inc(sem["k_e"], 1)
                act.wait_ge(sem["k_aT"], by("k_aT", nl))
                ev(aff_t[:, 0:1024], bank[0:NE, 1:3, :].rearrange("p a b -> p (a b)"))
                ev(aff_t[:, 1024:T], bank[0:NE, 3, 0:P]).then_inc(sem["k_at"], 1)
                barrier(act, l, 5)
                modulate_a(l * NE + 1)
                with act.Fori(0, NE - 1) as e:
                    n = l * NE + e + 1
                    silu_gate(n)
                    modulate_a(n + 1)
                    take_down(n)
                silu_gate(l * NE + NE)
                take_down(l * NE + NE)
                barrier(act, l, 6)
            for t in range(NT):
                n = DEPTH * NT + t + 1
                act.wait_ge(sem["p_x_in"], by("p_x_in", n))
                act.wait_ge(sem["p_rv"], before("p_rv", n))
                ev(f_junk, f_x[:, t % 2], ACT.Square, accum_out=small[:, 0:1]).then_inc(sem["p_ss"], 1)

        @block.vector
        def _(dve):
            def tt(out, a, b, op=ALU.mult):
                return dve.tensor_tensor(out, a, b, op)

            def bc(v, n):
                return v.unsqueeze(len(v.shape)).broadcast_to(list(v.shape) + [n])

            once = [0]

            def step(ins):
                once[0] += 1
                ins.then_inc(dve_once, 1)
                dve.wait_ge(dve_once, once[0])

            dve.wait_ge(lb_in, 32)
            step(tt(a_lbt[:, 0, :], a_lb[:, 0, :], a_lb[:, 1, :], ALU.max))
            for j in range(DEPTH):
                step(tt(a_lbt[:, 1 + j, :], a_lb[:, j, :], a_lbt[:, 0, :], ALU.subtract))
            dve.wait_ge(act_once, 3)
            step(tt(a_lbt[:, 3, :], a_lbt[:, 1, :], a_lbt[:, 2, :], ALU.add))
            step(dve.reciprocal(a_lbt[:, 3, :], a_lbt[:, 3, :]))
            for j in range(DEPTH):
                step(tt(a_lbt[:, 1 + j, :], a_lbt[:, 1 + j, :], a_lbt[:, 3, :]))
            step(tt(a_lbt[:, 2, :], a_lbt[:, 1, :], a_lbt[:, 2, :], ALU.add))
            step(tt(lb[:, 0, 0, :], a_lbt[:, 1, :], a_lbt[:, 1, :], ALU.subtract))
            step(tt(lb[:, 1, 0, :], a_lbt[:, 2, :], a_lbt[:, 1, :], ALU.subtract))
            for j in range(DEPTH):
                step(dve.tensor_scalar(lb[:, j, 1, :], lb[:, j, 0, :], -1.0, 1.0, ALU.mult, ALU.add))
            dve.wait_ge(const_in, 32)
            step(dve.tensor_copy(lev_mask[:, :, :, :].rearrange("p d a b -> p (d a b)"), a_mask))
            dve.wait_ge(primed, 1)

            def norm_x(n):
                dve.wait_ge(sem["p_rstd"], by("p_rstd", n))
                dve.wait_ge(sem["p_xT"], before("p_xT", n))
                dve.tensor_scalar(p_xn, p_x, small[:, 2:3], None, ALU.mult).then_inc(sem["p_xn"], 1)

            def modulate_p(t, n, p):
                dve.wait_ge(sem["p_xT"], by("p_xT", n))
                for ch in range(4):
                    last = dve.tensor_scalar(p_h[p][:, ch, :], bank[:, 0, ch * P:(ch + 1) * P], scale1[:, t, ch:ch + 1],
                                             shift1[:, t, ch:ch + 1], ALU.mult, ALU.add)
                last.then_inc(sem["p_hTd"], 1)

            def turn_p(l, t, n, more, p):
                if more:
                    norm_x(n + 1)
                dve.wait_ge(sem["p_eva"], by("p_eva", n, 5))
                dve.wait_ge(sem["p_proj_st"], before("p_proj_st", n))
                tt(p_out[:, J_F:J_F + 512], p_out[:, J_F:J_F + 512], lb[:, l, 1, :]).then_inc(sem["p_f"], 1)
                tt(p_out[:, J_K:J_K + 512], p_out[:, J_K:J_K + 512], lb[:, l, 1, :]).then_inc(sem["p_f"], 1)
                dve.wait_ge(sem["p_f"], by("p_f", n, 1))
                dve.scalar_tensor_tensor(out=p_out[:, J_F:J_F + 512], in0=p_out[:, J_F:J_F + 512], scalar=2.0 ** -60, in1=lb[:, l, 0, :],
                                         op0=ALU.max, op1=ALU.add).then_inc(sem["p_f"], 1)
                dve.wait_ge(sem["p_mm"], by("p_mm", n, 6))
                dve.tensor_copy(p_out[:, J_RQ:J_RQ + 512], bank[:, 6, :]).then_inc(sem["p_evF"], 1)
                if more:
                    modulate_p(t + 1, n + 1, 1 - p)
                dve.wait_ge(sem["p_mm"], by("p_mm", n, 7))
                dve.tensor_copy(p_out[:, J_RV:J_RV + 256], bank[:, 7, 0:256])
                if more:
                    tt(mod[:, bass.ds(t * 4 + 16, 4), :], bank[:, 7, 272:280].rearrange("p (a b) -> p a b", b=2), bc(vecs[:, bass.ds(t * 4 + 32, 4)], 2), ALU.add)
                dve.tensor_copy(dt_all[:, t, :], bank[:, 7, 256:272]).then_inc(sem["p_evV"], 1)

            def modulate_d(n):
                dve.wait_ge(sem["e_xT"], by("e_xT", n, 1))
                dve.wait_ge(sem["e_gu"], before("e_gu", n))
                for ch in range(4):
                    dve.tensor_scalar(e_xt[:, ch, 0:CAP_S], bank[:, 0, ch * P:(ch + 1) * P], scale2[:, 1, ch:ch + 1],
                                      shift2[:, 1, ch:ch + 1], ALU.mult, ALU.add)
                dve.wait_ge(sem["e_xT"], by("e_xT", n, 3))
                tt(e_xt[:, :, CAP_S:], bank[:, 2, 0:DC * CAP_P].rearrange("p (a b) -> p a b", b=CAP_P), bc(scale2[:, 0, :], CAP_P))\
                    .then_inc(sem["e_xtd"], 1)
                dve.wait_ge(sem["e_xtd"], by("e_xtd", n, 1))
                tt(e_xt[:, :, CAP_S:], e_xt[:, :, CAP_S:], bc(shift2[:, 0, :], CAP_P), ALU.add).then_inc(sem["e_xtd"], 1)

            def times_up(n):
                for f in range(FC):
                    dve.wait_ge(sem["e_sg"], by("e_sg", n, f + 1))
                    dve.wait_ge(sem["e_dn"], before("e_dn", n))
                    tt(e_h[:, f, :], bank[:, 4 + f, 256:256 + CAP_S + CAP_P], e_sg[:, f, :]).then_inc(sem["e_h"], 1)

            def weighted(e, n):
                dve.wait_ge(sem["e_y"], before("e_y", n))
                dve.sem_inc(tick, 1)
                dve.tensor_copy(e_g[:, 0:1], k_val[:, 0, bass.ds(e, 1)])
                dve.tensor_copy(e_g[0:CAP_P, 1:2], k_val[0:CAP_P, 1, bass.ds(e, 1)]).then_inc(sem["e_gc"], 1)
                dve.wait_ge(sem["e_gc"], by("e_gc", n))
                dve.wait_ge(sem["e_jc"], by("e_jc", n))
                for half in range(2):
                    cols = slice(half * 512, (half + 1) * 512)
                    dve.wait_ge(sem["e_bk"], by("e_bk", n, 1 + half))
                    dve.scalar_tensor_tensor(out=e_y[:, cols], in0=bank[:, half, :], scalar=e_g[:, 0:1],
                                             in1=gate_row[:, 1, 1, cols], op0=ALU.mult, op1=ALU.mult).then_inc(sem["e_y"], 1)
                dve.wait_ge(sem["e_bk"], by("e_bk", n))
                dve.scalar_tensor_tensor(out=e_yp[0:CAP_P, :], in0=bank[0:CAP_P, 2:4, :].rearrange("p a b -> p (a b)"), scalar=e_g[0:CAP_P, 1:2],
                                         in1=gate_row[0:CAP_P, 1, 0, :], op0=ALU.mult, op1=ALU.mult).then_inc(sem["e_y"], 1)

            def spread(k0, g0, sc, sh):
                for tl, w, cd in ((0, 1, 0), (1, NT - 1, 1)):
                    def over(v):
                        return v.unsqueeze(1).broadcast_to([P, w, DC])
                    dve.scalar_tensor_tensor(out=sc[:, tl:tl + w, :], in0=over(mod[:, k0 + 8:k0 + 16, cd]), scalar=1.0,
                                             in1=over(vecs[:, g0:g0 + 8]), op0=ALU.add, op1=ALU.mult)
                    last = dve.tensor_copy(sh[:, tl:tl + w, :], over(mod[:, k0:k0 + 8, cd]))
                return last

            def diagonal(i, nl):
                k0 = 16 if i < 2 else 40
                tt(s_diag[i % 2], ident.unsqueeze(1).broadcast_to([P, DC, P]), bc(mod[:, k0:k0 + 8, i % 2], P)).then_inc(sem["a_diag"], 1)

            def mix(t, n):
                dve.wait_ge(sem["r_i1"], by("r_i1", n))
                ln = Link(dve, "r_o", n)
                kv = r_o.rearrange("p (m q h v) -> p m q h v", m=4, q=2, h=2)[:, 0:4:3]
                for h in range(2):
                    v = kv[:, :, :, h, :]
                    last = tt(v, v, bank[:, 7 * h, 0:256].rearrange("p (m q v) -> p m q v", m=2, q=2), ALU.add)
                ln(last)
                dve.wait_ge(sem["r_i2"], by("r_i2", n))
                for g in range(2):
                    last = tt(r_t.rearrange("p d (g a b) -> p d g a b", g=2, b=HD)[:, :, g], bank[:, 1 + g, :].rearrange("p (d a b) -> p d a b", d=2, b=HD),
                              bc(eb_all[:, t, :].rearrange("p (d g a) -> p d g a", d=2, g=2)[:, :, g, :], HD))
                ln(last)
                o_s, o_r = r_o[:, 256:768], r_o[:, 768:1024].rearrange("p (a b) -> p a b", b=HD)
                ln(tt(o_s, o_s, r_t1, ALU.add))
                ln(tt(o_s, o_s, r_t2, ALU.add))
                ln(tt(o_s, o_s, r_g[:, 0:512]))
                ln(dve.tensor_reduce(small[:, 4:8], o_r, AX, ALU.add))
                ln(dve.tensor_scalar(small[:, 4:8], small[:, 4:8], -1.0 / HD, None, ALU.mult))
                ln(tt(o_r, o_r, bc(small[:, 4:8], HD), ALU.add), last=True)

            def sums(n):
                dve.wait_ge(sem["r_sq"], by("r_sq", n))
                dve.wait_ge(sem["r_var"], before("r_var", n))
                dve.tensor_reduce(small[:, 32:48], r_sq.rearrange("p (a b) -> p a b", b=HD), AX, ALU.add).then_inc(sem["r_red"], 1)
                dve.wait_ge(sem["r_red"], by("r_red", n, 1))
                dve.tensor_reduce(small[:, 8:9], small[:, 36:44], AX, ALU.add).then_inc(sem["r_red"], 1)

            def normed(n):
                dve.wait_ge(sem["r_rs"], by("r_rs", n))
                dve.wait_ge(sem["r_yT"], before("r_yT", n))
                v = r_y.rearrange("p (a b) -> p a b", b=HD)
                tt(v, r_o.rearrange("p (a b) -> p a b", b=HD), bc(small[:, 48:64], HD)).then_inc(sem["r_y"], 1)
                dve.wait_ge(sem["r_y"], by("r_y", n, 1))
                dve.wait_ge(sem["r_gg"], by("r_gg", n))
                tt(r_y, r_y, r_gg).then_inc(sem["r_y"], 1)

            def gated(kind, n):
                dve.wait_ge(sem["r_x1"], before("r_x1", n))
                for half in range(2):
                    dve.wait_ge(sem["r_out"], by("r_out", n, half + 1))
                    tt(r_gy[:, half * 512:(half + 1) * 512], bank[:, 5 + half, :],
                       gate_row[:, 0, kind, half * 512:(half + 1) * 512]).then_inc(sem["r_gy"], 1)

            def second_norm(n):
                dve.wait_ge(sem["r_rs2"], by("r_rs2", n))
                dve.wait_ge(sem["r_xT"], before("r_xT", n))
                dve.wait_ge(sem["r_nst"], before("r_nst", n))
                dve.tensor_scalar(r_xn, r_x1, small[:, 2:3], None, ALU.mult).then_inc(sem["r_xn"], 1)

            def modulated(t, n):
                for ch in range(DC):
                    if ch % 4 == 0:
                        dve.wait_ge(sem["r_xT"], by("r_xT", n, ch // 4 + 1))
                        dve.wait_ge(sem["r_lg"], before("r_lg", n))
                    last = dve.tensor_scalar(r_ht[:, ch, :], bank[:, 7 * (ch // 4), (ch % 4) * P:(ch % 4 + 1) * P],
                                             scale2[:, t, ch:ch + 1], shift2[:, t, ch:ch + 1], ALU.mult, ALU.add)
                last.then_inc(sem["r_ht"], 1)

            def logits(t, n):
                dve.wait_ge(sem["r_lg"], by("r_lg", n))
                dve.tensor_copy(lg_all[:, t, :], bank[:, 1, 0:NE]).then_inc(sem["r_lgc"], 1)

            with dve.Fori(0, DEPTH) as l:
                nl = l + 1
                dve.wait_ge(sem["a_vecT"], by("a_vecT", nl))
                dve.tensor_copy(vecs[:, :], bank[:, 0, 0:88]).then_inc(sem["a_vecs"], 1)
                dve.wait_ge(sem["a_used"], by("a_used", nl))
                dve.wait_ge(sem["a_vecs"], by("a_vecs", nl))
                tt(mod[:, 0:16, :], bank[:, 1, 0:32].rearrange("p (a b) -> p a b", b=2), bc(vecs[:, 16:32], 2), ALU.add).then_inc(sem["a_mod"], 1)
                dve.wait_ge(sem["a_mod"], by("a_mod", nl))
                spread(0, 0, scale1, shift1).then_inc(sem["a_scales"], 1)
                barrier(dve, l, 1)
                norm_x(l * NT + 1)
                modulate_p(0, l * NT + 1, 0)
                with dve.Fori(0, NT // 2) as j:
                    for p in range(2):
                        turn_p(l, 2 * j + p, l * NT + 2 * j + p + 1, True, p)
                turn_p(l, NT - 1, l * NT + NT, False, 0)
                barrier(dve, l, 2)

                flat = [l_s[:, i].rearrange("p a b -> p (a b)") for i in range(4)]
                dts = dt_all[:, :, :].rearrange("p a b -> p (a b)")
                bias = head_row[:, 0:16].unsqueeze(1).broadcast_to([P, NT, 16])
                tt(dt_all[:, :, :], dt_all[:, :, :], bias, ALU.add).then_inc(sem["l_de"], 1)
                dve.wait_ge(sem["l_de"], by("l_de", nl, 1))
                dve.scalar_tensor_tensor(out=flat[1], in0=dts, scalar=-1.0, in1=dts, op0=ALU.mult, op1=ALU.min).then_inc(sem["l_de"], 1)
                dve.wait_ge(act_once, (l + 1) * 2 + 3)
                dve.sem_inc(tick, 1)
                ln = Link(dve, "l_dt", nl)
                ln(dve.tensor_scalar(flat[0], flat[1], 2.0, None, ALU.add))
                ln(dve.reciprocal(flat[0], flat[0]))
                ln(tt(flat[0], flat[0], flat[1]))
                ln(tt(flat[3], flat[0], flat[0]))
                ln(dve.tensor_scalar(flat[2], flat[3], 1.0 / 17, None, ALU.mult))
                for odd in (15, 13, 11, 9, 7, 5, 3):
                    ln(dve.scalar_tensor_tensor(out=flat[2], in0=flat[2], scalar=1.0 / odd, in1=flat[3], op0=ALU.add, op1=ALU.mult))
                ln(dve.scalar_tensor_tensor(out=flat[2], in0=flat[2], scalar=1.0, in1=flat[0], op0=ALU.add, op1=ALU.mult))
                ln(dve.tensor_scalar(dts, dts, 0.0, None, ALU.max))
                ln(dve.scalar_tensor_tensor(out=dts, in0=flat[2], scalar=2.0, in1=dts, op0=ALU.mult, op1=ALU.add))
                ln(dve.scalar_tensor_tensor(out=la_all[:, :, :], in0=dt_all[:, :, :], scalar=-1.0,
                                            in1=small[:, 40:56].unsqueeze(1).broadcast_to([P, NT, 16]), op0=ALU.mult, op1=ALU.mult), last=True)
                dve.wait_ge(sem["l_bex"], by("l_bex", nl))
                tt(dtee[:, :, :], dt_all[:, :, :], l_s[:, 2])
                for d in range(2):
                    for g in range(2):
                        dve.tensor_copy(dec[rows(g), :, d, 4:8], etot[rows(g), :, 8 * d + 4 * g:8 * d + 4 * g + 4])
                    last = dve.tensor_copy(dec[:, :, d, 2:4], cst[:, C_RT + 2 * d:C_RT + 2 * d + 2].unsqueeze(1).broadcast_to([P, NT, 2]))
                last.then_inc(sem["l_dec0"], 1)

                with dve.Fori(0, NT) as t:
                    n = l * NT + t + 1
                    dve.wait_ge(sem["l_T"], by("l_T", n, 2))
                    dve.wait_ge(sem["l_xl"], before("l_xl", n))
                    dve.wait_ge(sem["l_lv"], before("l_lv", n))
                    dve.tensor_copy(l_k[:, 1], bank[:, 1, 0:256].rearrange("p (a b) -> p a b", a=2)).then_inc(sem["l_ev2"], 1)
                    dve.wait_ge(sem["l_ev1"], by("l_ev1", n))
                    dve.wait_ge(sem["l_ev2"], by("l_ev2", n))
                    tt(l_kk, l_k[:, 0], l_k[:, 1], ALU.add).then_inc(sem["l_kk"], 1)
                    dve.wait_ge(sem["l_T"], by("l_T", n, 3))
                    dve.tensor_copy(l_rqk, bank[:, 4, :].rearrange("p (a b) -> p a b", a=4)).then_inc(sem["l_ev4"], 1)
                    for d in range(2):
                        dve.wait_ge(sem["l_ex"], by("l_ex", n, 2 * d + 2))
                        for level in range(NL):
                            for second in range(2):
                                src = l_q if (second == 1) == (d == 0) else l_k[:, d]
                                last = tt(halves(l_xl[:, d, :, level, :], level, second), halves(l_ex[:, d, :, level, :], level, second),
                                          halves(src, level, second))
                        last.then_inc(sem["l_xl"], 1)
                    dve.wait_ge(sem["l_T"], by("l_T", n, 4))
                    dve.wait_ge(sem["l_dS"], before("l_dS", n))
                    dve.tensor_copy(l_tm[:, 4, :], bank[:, 1, 0:P]).then_inc(sem["l_ev3b"], 1)
                    dve.wait_ge(sem["l_RA"], by("l_RA", n))
                    dve.wait_ge(sem["l_at"], before("l_at", n))
                    for g in range(2):
                        last = tt(l_bc[:, :, g, :], bank[:, 5 - g, 0:P].unsqueeze(1).broadcast_to([P, 2, P]), tri[:, LE:LE + 2, :])
                    last.then_inc(sem["l_bcm"], 1)
                    dve.wait_ge(sem["l_oR"], before("l_oR", n))
                    for h in range(2):
                        last = tt(l_ar[:, h:4:2, :], bank[:, 5 - h, 256:512].rearrange("p (a b) -> p a b", a=2),
                                  cst[:, C_RM:C_RM + 512].rearrange("p (a b) -> p a b", a=4)[:, h:4:2, :])
                    last.then_inc(sem["l_ar"], 1)
                    dve.wait_ge(sem["l_qst"], before("l_qst", n))
                    for d in range(2):
                        tt(l_qe[:, 4 * d:4 * d + 2, :], l_ex[:, d, :, 7, :], l_q)
                        tt(l_qe[:, 4 * d + 2:4 * d + 4, :], l_rqk[:, 0:2, :],
                           cst[:, C_RQ + d * 256:C_RQ + (d + 1) * 256].rearrange("p (a b) -> p a b", a=2))
                        dve.tensor_copy(dec[:, t, d, 0:2], l_ex[:, d, :, 7, P - 1 if d == 0 else 0]).then_inc(sem["l_qe"], 1)
                    dve.wait_ge(sem["l_bcm"], by("l_bcm", n))
                    for d in range(2):
                        dve.wait_ge(sem["l_pe"], by("l_pe", n, d + 1))
                        v = l_at[:, d].rearrange("p (g h) t -> p g h t", g=2)
                        tt(v, v, l_bc[:, d].unsqueeze(2).broadcast_to([P, 2, 4, P])).then_inc(sem["l_at"], 1)
                    dve.wait_ge(sem["l_ee"], by("l_ee", n))
                    tt(l_kb, l_in[:, J_K:J_K + 512], l_ee).then_inc(sem["l_kb"], 1)
                    for i in range(8):
                        dve.wait_ge(sem["l_lv"], by("l_lv", n, i + 1))
                        b0 = 6 if i % 2 == 0 else 0
                        dst = l_ah.rearrange("p (q h) t -> p h q t", h=2)
                        if i == 0:
                            dve.wait_ge(sem["l_oR"], before("l_oR", n))
                            for h in range(2):
                                src = bank[:, b0 + h, 0:256].rearrange("p (q t) -> p q t", q=2)
                                last = tt(dst[:, h], src, ident.unsqueeze(1).broadcast_to([P, 2, P]))
                            last.then_inc(sem["l_lc"], 1)
                        else:
                            for d in range(2):
                                dve.wait_ge(sem["l_lc"], by("l_lc", n, 2 * i - 1 + d))
                                dve.sem_inc(tick, 1)
                                src = bank[:, b0:b0 + 2, d * 256:(d + 1) * 256].rearrange("p h (q t) -> p h q t", q=2)
                                mask = lev_mask[:, d, i - 1, :].unsqueeze(1).unsqueeze(1).broadcast_to([P, 2, 2, P])
                                dve.copy_predicated(dst, mask, src).then_inc(sem["l_lc"], 1)
                    dve.wait_ge(sem["l_oS"], by("l_oS", n))
                    dve.wait_ge(sem["l_sk"], by("l_sk", n))
                    dve.wait_ge(sem["l_ost"], before("l_ost", n))
                    tt(l_o[:, 256:768], bank[:, 5, :], l_sk, ALU.add).then_inc(sem["l_oeS"], 1)
                    for d in range(2):
                        dve.wait_ge(sem["l_dS"], by("l_dS", n, 3 + d))
                        dve.sem_inc(tick, 1)
                        for g in range(2):
                            last = dve.tensor_copy((st_f[:, t + 1] if d == 0 else st_b[:, t])[rows(g), 4:8, :], bank[rows(g), 2 + d, 256 * g:256 * g + 256].rearrange("p (a b) -> p a b", a=4))
                        last.then_inc(sem["l_incD"], 1)
                barrier(dve, l, 3)

                dve.memset(st_f[:, 0], 0.0).then_inc(sem["s_init"], 1)
                spread(24, 8, scale2, shift2).then_inc(sem["a_scales"], 1)
                diagonal(0, nl)
                diagonal(1, nl)
                dve.wait_ge(sem["s_in"], by("s_in", nl))
                ln = Link(dve, "s_fs", nl)
                for tile in range(1, NT - 1):
                    step_f = r_y[:, 0:512].rearrange("p (a b) -> p a b", b=HD)
                    ln(tt(step_f, st_f[:, tile], bc(dec[:, tile, 0, :], HD)))
                    ln(tt(st_f[:, tile + 1], st_f[:, tile + 1], step_f, ALU.add), last=(tile == NT - 2))
                mix(0, l * NT + 1)
                sums(l * NT + 1)
                for i in range(2, 4):
                    dve.wait_ge(sem["a_rowmm"], by("a_rowmm", nl, i - 1))
                    diagonal(i, nl)
                normed(l * NT + 1)
                mix(1, l * NT + 2)
                sums(l * NT + 2)
                normed(l * NT + 2)
                dve.wait_ge(sem["a_rowmm"], by("a_rowmm", nl))
                gated(0, l * NT + 1)
                with dve.Fori(1, NT - 1) as t:
                    n = l * NT + t + 1
                    mix(t + 1, n + 1)
                    second_norm(n - 1)
                    sums(n + 1)
                    normed(n + 1)
                    modulated(t - 1, n - 1)
                    gated((t + 7) // 8, n)
                    logits(t - 1, n - 1)
                second_norm(l * NT + NT - 1)
                modulated(NT - 2, l * NT + NT - 1)
                gated(1, l * NT + NT)
                logits(NT - 2, l * NT + NT - 1)
                second_norm(l * NT + NT)
                modulated(NT - 1, l * NT + NT)
                logits(NT - 1, l * NT + NT)
                barrier(dve, l, 4)

                ln = Link(dve, "k_mx", nl)
                ln(dve.memset(k_t, 0.0))
                ln(dve.tensor_reduce(k_red, lg_all[:, :, :], AX, ALU.max))
                ln(tt(lg_all[:, :, :], lg_all[:, :, :], bc(k_red, NE), ALU.subtract), last=True)
                dve.wait_ge(sem["k_e"], by("k_e", nl))
                ln = Link(dve, "k_soft", nl)
                ln(dve.tensor_reduce(k_red, lg_all[:, :, :], AX, ALU.add))
                ln(dve.reciprocal(k_red, k_red))
                ln(tt(lg_all[:, :, :], lg_all[:, :, :], bc(k_red, NE)), last=True)
                dve.wait_ge(sem["k_at"], by("k_at", nl))
                dve.sem_inc(tick, 1)

                def round_(src, kind, r, n):
                    ln = Link(dve, "k_r", n)
                    ln.hold(dve.max(k_m8[0:NE, :], src))
                    ln.hold(dve.max_index(k_i8[0:NE, :].bitcast(U32), k_m8[0:NE, :], src))
                    dve.tensor_copy(k_t[0:NE, kind, bass.ds(r * 8, 8)], k_i8[0:NE, :].bitcast(U32))
                    dve.tensor_copy(k_t[0:NE, kind + 1, bass.ds(r * 8, 8)], k_m8[0:NE, :])
                    ln.hold(dve.match_replace(src, k_m8[0:NE, :], src, -1.0))

                ROUNDS_S, ROUNDS_P = CAP_S // 8, CAP_P // 8
                with dve.Fori(0, ROUNDS_S) as r:
                    round_(aff_t[:, SEQ:T], 0, r, l * (ROUNDS_S + ROUNDS_P) + r + 1)
                for r in range(ROUNDS_P):
                    round_(aff_t[:, 0:SEQ], 2, r, l * (ROUNDS_S + ROUNDS_P) + ROUNDS_S + r + 1)
                dve.tensor_copy(k_m8[0:NE, :], k_m8[0:NE, :]).then_inc(sem["k_done"], 1)
                dve.wait_ge(sem["k_T"], by("k_T", nl))
                dve.tensor_scalar(k_idx[:, 0, :].bitcast(U32), bank[:, 0, 0:NE], float(SEQ), None, ALU.add)
                dve.tensor_copy(k_idx[0:CAP_P, 1, :].bitcast(U32), bank[0:CAP_P, 0, 256:256 + NE])
                dve.tensor_copy(k_val[:, 0, :], bank[:, 0, P:P + NE])
                dve.tensor_copy(k_val[0:CAP_P, 1, :], bank[0:CAP_P, 0, 384:384 + NE]).then_inc(sem["k_ix"], 1)
                barrier(dve, l, 5)
                modulate_d(l * NE + 1)
                with dve.Fori(0, NE - 1) as e:
                    n = l * NE + e + 1
                    times_up(n)
                    modulate_d(n + 1)
                    weighted(e, n)
                times_up(l * NE + NE)
                weighted(NE - 1, l * NE + NE)
                barrier(dve, l, 6)
            dve.wait_ge(final_g_in, 16)
            for t in range(NT):
                n = DEPTH * NT + t + 1
                dve.wait_ge(sem["p_rstd"], by("p_rstd", n))
                if t:
                    dve.wait_ge(sem["p_u_st"], by("p_u_st", n - 1))
                dve.scalar_tensor_tensor(out=f_y[:, t % 2], in0=f_x[:, t % 2], scalar=small[:, 2:3], in1=f_g, op0=ALU.mult, op1=ALU.mult)\
                    .then_inc(sem["p_evF"], 1)

        @block.gpsimd
        def _(pool):
            def tt(out, a, b, op=ALU.mult):
                return pool.tensor_tensor(out, a, b, op)

            def bc(v, n):
                return v.unsqueeze(len(v.shape)).broadcast_to(list(v.shape) + [n])

            for name in COUNTS:
                if name not in SWDGE:
                    pool.sem_inc(sem[name], 1)
            pool.memset(minus_half[:, :], -0.5).then_inc(pool_once, 1)
            pool.wait_ge(pool_once, 1)
            pool.sem_inc(primed, 1)
            pool.wait_ge(const_in, 32)

            def rstd(src, mid, out, ss, rv, rs, used, n):
                pool.wait_ge(sem[ss], by(ss, n))
                pool.wait_ge(sem[rs], before(rs, n))
                pool.sem_inc(tick, 1)
                pool.tensor_scalar(small[:, mid:mid + 1], small[:, src:src + 1], 1.0 / D, EPS, ALU.mult, ALU.add).then_inc(sem[rv], 1)
                pool.wait_ge(sem[rv], by(rv, n))
                pool.wait_ge(sem[used], before(used, n))
                pool.sem_inc(tick, 1)
                tt(small[:, out:out + 1], small[:, mid:mid + 1], minus_half[:, 0:1], ALU.pow).then_inc(sem[rs], 1)

            def entering(t, n):
                pool.wait_ge(sem["r_i2"], before("r_i2", n))
                pool.sem_inc(tick, 1)
                pool.tensor_copy(r_st[:, 0], st_f[:, t])
                pool.tensor_copy(r_st[:, 1], st_b[:, t + 1]).then_inc(sem["r_st"], 1)

            def gates(n):
                pool.wait_ge(sem["r_in"], by("r_in", n))
                pool.wait_ge(sem["r_y"], before("r_y", n))
                pool.sem_inc(tick, 1)
                tt(r_gg[:, 0:256], r_g[:, 512:768], gain_row[:, 0:256])
                tt(r_gg[:, 768:1024], r_g[:, 768:1024], gain_row[:, 768:1024]).then_inc(sem["r_gg"], 1)

            def variances(n):
                pool.wait_ge(sem["r_red"], by("r_red", n))
                pool.sem_inc(tick, 1)
                for dst, src, m in ((small[:, 32:36], small[:, 32:36], HD), (small[:, 36:44], small[:, 8:9].broadcast_to([P, 8]), SSDW),
                                    (small[:, 44:48], small[:, 44:48], HD)):
                    last = pool.tensor_scalar(dst, src, 1.0 / m, EPS, ALU.mult, ALU.add)
                last.then_inc(sem["r_var"], 1)
                pool.wait_ge(sem["r_var"], by("r_var", n))
                pool.wait_ge(sem["r_y"], before("r_y", n))
                pool.sem_inc(tick, 1)
                tt(small[:, 48:64], small[:, 32:48], minus_half[:, :], ALU.pow).then_inc(sem["r_rs"], 1)

            def residual(n):
                pool.wait_ge(sem["r_gy"], by("r_gy", n))
                pool.wait_ge(sem["r_x_in"], by("r_x_in", n))
                pool.wait_ge(sem["r_xst"], before("r_xst", n))
                pool.wait_ge(sem["r_xn"], before("r_xn", n))
                pool.wait_ge(sem["r_ss"], before("r_ss", n))
                pool.sem_inc(tick, 1)
                tt(r_x1, r_x, r_gy, ALU.add).then_inc(sem["r_x1"], 1)
                rstd(0, 1, 2, "r_ss", "r_rv2", "r_rs2", "r_xn", n)

            with pool.Fori(0, DEPTH) as l:
                nl = l + 1
                barrier(pool, l, 1)
                with pool.Fori(0, NT) as t:
                    rstd(0, 1, 2, "p_ss", "p_rv", "p_rstd", "p_xn", l * NT + t + 1)
                barrier(pool, l, 2)
                with pool.Fori(0, NT) as t:
                    n = l * NT + t + 1
                    pool.wait_ge(sem["l_uin"], by("l_uin", n))
                    pool.sem_inc(tick, 1)
                    ln = Link(pool, "l_rope", n)
                    x = l_in[:, J_RQ:J_RQ + 512].rearrange("p (j m i) -> p j m i", j=2, i=32)
                    for dst, c0 in ((l_r1, C_COS), (l_r2, C_SIN)):
                        w = cst[:, bass.ds(c0 + t * 64, 64)].rearrange("p (j i) -> p j i", j=2).unsqueeze(2).broadcast_to([P, 2, 8, 32])
                        ln.hold(tt(dst.rearrange("p (j m i) -> p j m i", j=2, i=32), x, w))
                    v1, v2, vo = (v.rearrange("p (m two i) -> p m two i", two=2, i=32) for v in (l_r1, l_r2, l_rot))
                    pool.wait_ge(sem["l_T"], before("l_T", n))
                    pool.sem_inc(tick, 1)
                    ln.hold(tt(vo[:, :, 0, :], v1[:, :, 0, :], v2[:, :, 1, :], ALU.subtract))
                    ln(tt(vo[:, :, 1, :], v2[:, :, 0, :], v1[:, :, 1, :], ALU.add), last=True)
                    edge = l_u[:, :, 0:P + 2:P + 1]
                    tt(edge, edge, cst[:, bass.ds(C_HALO + t * 2, 2)].unsqueeze(1).broadcast_to([P, UC, 2])).then_inc(sem["l_halo"], 1)
                    pool.wait_ge(sem["l_halo"], by("l_halo", n))
                    pool.wait_ge(sem["l_T"], before("l_T", n))
                    pool.wait_ge(sem["l_BC"], before("l_BC", n))
                    pool.sem_inc(tick, 1)
                    pool.wait_ge(sem["l_qc"], before("l_qc", n))
                    pool.sem_inc(tick, 1)
                    ln = Link(pool, "l_cv", n)
                    ln(tt(l_c, l_u[:, :, 0:P], bc(vecs[:, 64:70], P)))
                    ln(tt(l_ct, l_u[:, :, 1:P + 1], bc(vecs[:, 70:76], P)))
                    ln(tt(l_c, l_c, l_ct, ALU.add))
                    ln(tt(l_ct, l_u[:, :, 2:P + 2], bc(vecs[:, 76:82], P)))
                    ln(tt(l_c, l_c, l_ct, ALU.add), last=True)
                    pool.wait_ge(sem["l_dec0"], by("l_dec0", nl))
                    pool.sem_inc(tick, 1)
                    pool.wait_ge(sem["l_pm"], before("l_pm", n))
                    pool.sem_inc(tick, 1)
                    for d in range(2):
                        last = tt(l_pr[:, d], tri[:, LE + d, :].unsqueeze(1).broadcast_to([P, 8, P]), bc(la_all[:, t, 8 * d:8 * d + 8], P))
                    last.then_inc(sem["l_prf"], 1)
                    pool.wait_ge(sem["l_rope"], by("l_rope", n))
                    pool.wait_ge(sem["l_dS"], before("l_dS", n))
                    pool.sem_inc(tick, 1)
                    for d in range(2):
                        last = tt(l_rkb[:, d * 256:(d + 1) * 256].rearrange("p (a b) -> p a b", b=HD),
                                  l_rot[:, 256:512].rearrange("p (a b) -> p a b", b=HD), bc(cst[:, C_RK + 4 * d:C_RK + 4 * d + 4], HD))
                    last.then_inc(sem["l_rkb"], 1)
                    pool.wait_ge(sem["l_ev3"], by("l_ev3", n))
                    pool.sem_inc(tick, 1)
                    pool.wait_ge(sem["l_oS"], before("l_oS", n))
                    pool.sem_inc(tick, 1)
                    xs = l_tm[:, 0:4, :].rearrange("p a (h b) -> p (a h) b", b=HD)
                    for d in range(2):
                        tt(l_v1[:, d].rearrange("p (a b) -> p a b", b=HD), xs, bc(dt_all[:, t, 8 * d:8 * d + 8], HD))
                        last = tt(l_v2[:, d].rearrange("p (a b) -> p a b", b=HD), xs, bc(dtee[:, t, 8 * d:8 * d + 8], HD))
                    last.then_inc(sem["l_v"], 1)
                    pool.wait_ge(sem["l_oeS"], before("l_oeS", n))
                    pool.sem_inc(tick, 1)
                    tt(l_sk.rearrange("p (a b) -> p a b", b=HD), xs, bc(head_row[:, 32:40], HD)).then_inc(sem["l_sk"], 1)
                    pool.wait_ge(sem["l_silu"], by("l_silu", n))
                    pool.wait_ge(sem["l_qst"], before("l_qst", n))
                    pool.sem_inc(tick, 1)
                    pool.tensor_copy(l_qe[:, 8, :], l_c[:, 5, :]).then_inc(sem["l_qc"], 1)
                barrier(pool, l, 3)
                pool.memset(st_b[:, 1], 0.0).then_inc(sem["s_zero"], 1)
                pool.wait_ge(sem["s_zero"], by("s_zero", nl))
                pool.wait_ge(sem["s_init"], by("s_init", nl))
                pool.sem_inc(tick, 1)
                entering(0, l * NT + 1)
                pool.wait_ge(sem["gain_in"], by("gain_in", nl))
                pool.sem_inc(tick, 1)
                pool.tensor_copy(r_gg[:, 256:768], gain_row[:, 256:768])
                gates(l * NT + 1)
                pool.wait_ge(sem["s_in"], by("s_in", nl))
                pool.sem_inc(tick, 1)
                ln = Link(pool, "s_bs", nl)
                for tile in range(NT - 1, 1, -1):
                    step_b = r_yt[:, 0:4, :].rearrange("p a (c b) -> p (a c) b", b=HD)
                    ln(tt(step_b, st_b[:, tile + 1], bc(dec[:, tile, 1, :], HD)))
                    ln(tt(st_b[:, tile], st_b[:, tile], step_b, ALU.add), last=(tile == 2))
                pool.wait_ge(sem["s_bs"], by("s_bs", nl))
                pool.wait_ge(sem["s_fs"], by("s_fs", nl))
                pool.sem_inc(tick, 1)
                variances(l * NT + 1)
                entering(1, l * NT + 2)
                with pool.Fori(0, NT - 2) as t:
                    n = l * NT + t + 1
                    gates(n + 1)
                    entering(t + 2, n + 2)
                    variances(n + 1)
                    residual(n)
                gates(l * NT + NT)
                variances(l * NT + NT)
                residual(l * NT + NT - 1)
                residual(l * NT + NT)
                barrier(pool, l, 4)
                barrier(pool, l, 5)

                def gather(e, n):
                    if not isinstance(e, int):
                        pool.wait_ge(sem["e_xg"], by("e_xg", n - 1))
                        pool.sem_inc(tick, 1)
                    pool.tensor_copy(e_i[:, 0:1].bitcast(U32), k_idx[:, 0, bass.ds(e, 1)].bitcast(U32))
                    pool.tensor_copy(e_i[0:CAP_P, 1:2].bitcast(U32), k_idx[0:CAP_P, 1, bass.ds(e, 1)].bitcast(U32)).then_inc(sem["e_ic"], 1)
                    pool.wait_ge(sem["e_ic"], by("e_ic", n))
                    pool.wait_ge(sem["e_xT"], before("e_xT", n))
                    pool.sem_inc(tick, 1)
                    pool.indirect_dma_start(e_x, None, xn_d, bass.IndirectOffsetOnAxis(ap=e_i[:, 0:1].bitcast(U32), axis=0)).then_inc(sem["e_xg"], 16)
                    pool.indirect_dma_start(e_xp[0:CAP_P, :], None, xn_d, bass.IndirectOffsetOnAxis(ap=e_i[0:CAP_P, 1:2].bitcast(U32), axis=0))\
                        .then_inc(sem["e_xg"], 16)

                def scatter(e, n):
                    if not isinstance(e, int) or e > 0:
                        pool.wait_ge(sem["e_sc"], by("e_sc", n - 1))
                        pool.wait_ge(sem["e_scp"], by("e_scp", n - 1))
                        pool.sem_inc(tick, 1)
                    pool.tensor_copy(k_j[:, 0:1].bitcast(U32), k_idx[:, 0, bass.ds(e, 1)].bitcast(U32))
                    pool.tensor_copy(k_j[0:CAP_P, 1:2].bitcast(U32), k_idx[0:CAP_P, 1, bass.ds(e, 1)].bitcast(U32)).then_inc(sem["e_jc"], 1)
                    pool.wait_ge(sem["e_jc"], by("e_jc", n))
                    pool.wait_ge(sem["e_y"], by("e_y", n))
                    pool.sem_inc(tick, 1)
                    pool.indirect_dma_start(x_d, bass.IndirectOffsetOnAxis(ap=k_j[:, 0:1].bitcast(U32), axis=0), e_y, None, compute_op=ALU.add)\
                        .then_inc(sem["e_sc"], 16)
                    pool.indirect_dma_start(x_d, bass.IndirectOffsetOnAxis(ap=k_j[0:CAP_P, 1:2].bitcast(U32), axis=0), e_yp[0:CAP_P, :], None, compute_op=ALU.add)\
                        .then_inc(sem["e_scp"], 16)

                gather(0, l * NE + 1)
                pool.wait_ge(sem["e_xg"], by("e_xg", l * NE + 1))
                pool.sem_inc(tick, 1)
                gather(1, l * NE + 2)
                scatter(0, l * NE + 1)
                with pool.Fori(1, NE - 1) as e:
                    n = l * NE + e + 1
                    gather(e + 1, n + 1)
                    scatter(e, n)
                scatter(NE - 1, l * NE + NE)
                pool.wait_ge(sem["e_sc"], by("e_sc", l * NE + NE))
                pool.wait_ge(sem["e_scp"], by("e_scp", l * NE + NE))
                pool.sem_inc(tick, 1)
                barrier(pool, l, 6)
            for t in range(NT):
                rstd(0, 1, 2, "p_ss", "p_rv", "p_rstd", "p_evF", DEPTH * NT + t + 1)


_INS = ["x_prompt", "x_sample", "state_hgrn", "state_ssd", "state_ret", "c", "c_ctx", "norm1_g", "norm2_g", "final_g",
        "w_ada", "b_ada", "w_in", "w_out", "hg_lb", "hg_norm_g", "ssd_conv_w", "ssd_conv_b", "ssd_dt_bias", "ssd_a_log",
        "ssd_d", "ssd_norm_g", "ret_norm_g", "w_router", "w_gate", "w_up", "w_down"]
_OUTS = [(1, SEQ, D), (1, DEC, D), (1, DEPTH, 2, 4, 64, 64), (1, DEPTH, 2, 8, 64, 64), (1, DEPTH, 2, 4, 64, 64)]


def kernel(**inputs):
    import numpy as _np
    import concourse.bacc as _bacc
    from concourse import mybir as _mybir
    from concourse.bass_utils import run_bass_kernel_spmd as _run

    nc = _bacc.Bacc("TRN2", target_bir_lowering=False, num_devices=1)
    arrays, args = {}, []
    const_f, const_m = shape_constants()
    given = [(name, _np.ascontiguousarray(inputs[name])) for name in _INS] + [("const_f", const_f), ("const_m", const_m)]
    for name, a in given:
        arrays[f"in_{name}_dram"] = a
        args.append(nc.dram_tensor(f"in_{name}_dram", a.shape, _mybir.dt.from_np(a.dtype), kind="ExternalInput").ap())
    for i, shape in enumerate(_OUTS):
        args.append(nc.dram_tensor(f"out_{i}_dram", shape, _mybir.dt.float32, kind="ExternalOutput").ap())
    trunk(nc, *args)
    r = _run(nc, [arrays], core_ids=[0])
    return tuple(r.results[0][f"out_{i}_dram"] for i in range(len(_OUTS)))
```
